# Optimizing a Trainium2 kernel written in Bass

```python
import math
import jax, jax.numpy as jnp
from jax import lax
import numpy as np

D_MODEL = 1024
BATCH = 1
SEQ = 512
DEPTH = 2
DEC_BATCH = 8
DEC_SEQ = 4
PAST_LEN = 2048
PAGE_SIZE = 128

N_A_LAYERS = DEPTH // 2
N_B_LAYERS = DEPTH - N_A_LAYERS
A_HEADS = 8
A_DK = D_MODEL // A_HEADS
A_DV = D_MODEL // A_HEADS
A_WIDTH = A_HEADS * A_DK
GLA_CHUNK = 32
B_HEADS = 8
B_DH = D_MODEL // B_HEADS // 2
B_VDIM = 2 * B_DH
B_WIDTH = B_HEADS * 2 * B_DH
Q_BLOCK = 128
MOE_GROUPS = 4
MOE_EPG = 4
MOE_EXPERTS = MOE_GROUPS * MOE_EPG
MOE_TOP_K = 2
MOE_D_EXPERT = 256
NORM_EPS = 1e-6
SUBLN_EPS = 1e-5
NEG_BIG = -1e30

kernel_name = 'yoco_hgrn2_diffattn_hmoe_step'

F32 = jnp.float32

def rmsnorm(x, w, eps=NORM_EPS):
    xf = x.astype(F32)
    y = xf * lax.rsqrt(jnp.mean(xf * xf, axis=-1, keepdims=True) + eps)
    return (y * w.astype(F32)).astype(x.dtype)

def lower_bounds(logits):
    p = jax.nn.softmax(logits.astype(F32), axis=0)
    return jnp.cumsum(p, axis=0) - p[0:1]

def alibi_slopes():
    return 2.0 ** (-8.0 * jnp.arange(1, B_HEADS + 1, dtype=F32) / B_HEADS)

def gla_chunked(q, k, v, logf, s0):
    B, T, H, DK = q.shape
    DV = v.shape[-1]
    c = math.gcd(T, GLA_CHUNK)
    n = T // c

    def to_chunks(a):
        return a.reshape(B, n, c, H, a.shape[-1]).transpose(1, 0, 3, 2, 4)

    causal = jnp.tril(jnp.ones((c, c), dtype=bool))

    def step(S, inp):
        qb, kb, vb, fb = inp
        b = jnp.cumsum(fb, axis=2)
        inter = jnp.einsum('bhtk,bhkv->bhtv', qb * jnp.exp(b), S)
        diff = b[:, :, :, None, :] - b[:, :, None, :, :]
        decay = jnp.exp(jnp.where(causal[:, :, None], diff, -jnp.inf))
        att = jnp.einsum('bhtk,bhsk,bhtsk->bhts', qb, kb, decay)
        intra = jnp.einsum('bhts,bhsv->bhtv', att, vb)
        bl = b[:, :, -1:, :]
        S_new = jnp.exp(bl[:, :, 0, :])[..., None] * S + jnp.einsum('bhsk,bhsv->bhkv', kb * jnp.exp(bl - b), vb)
        return S_new, inter + intra

    S, o = lax.scan(step, s0, (to_chunks(q), to_chunks(k), to_chunks(v), to_chunks(logf)))
    o = o.transpose(1, 0, 3, 2, 4).reshape(B, T, H, DV)
    return o, S

def hgrn2_mixer(hn, w_in, lb, gnorm_w, w_o, s0):
    B, T, _ = hn.shape
    proj = hn @ w_in
    q, f, i, g = jnp.split(proj, 4, axis=-1)
    fg = lb + (1.0 - lb) * jax.nn.sigmoid(f.astype(F32))
    logf = jnp.log(fg)
    k = 1.0 - fg

    def heads(a):
        return a.reshape(B, T, A_HEADS, -1)

    o, s_new = gla_chunked(heads(jax.nn.silu(q.astype(F32))), heads(k), heads(i.astype(F32)),
                           heads(logf), s0.astype(F32))
    o = rmsnorm(o, gnorm_w).reshape(B, T, A_WIDTH) * jax.nn.silu(g.astype(F32))
    return o.astype(hn.dtype) @ w_o, s_new

def diff_attn_prompt(q, k, v, lam):
    B, S = q.shape[:2]
    qb_len = math.gcd(S, Q_BLOCK)
    nb = S // qb_len
    slopes = alibi_slopes()
    kf = k.astype(F32)
    vf = v.astype(F32)
    qs = (q.astype(F32) * B_DH ** -0.5).reshape(B, nb, qb_len, B_HEADS, 2, B_DH).transpose(1, 0, 2, 3, 4, 5)
    kpos = jnp.arange(S)

    def block(args):
        qi, bi = args
        qpos = bi * qb_len + jnp.arange(qb_len)
        dist = qpos[:, None] - kpos[None, :]
        s = jnp.einsum('bqhcd,bkhcd->bhcqk', qi, kf) - slopes[:, None, None, None] * dist.astype(F32)
        s = jnp.where(dist >= 0, s, -jnp.inf)
        p = jax.nn.softmax(s, axis=-1)
        a = p[:, :, 0] - lam * p[:, :, 1]
        return jnp.einsum('bhqk,bkhv->bqhv', a, vf)

    o = lax.map(block, (qs, jnp.arange(nb)))
    return o.transpose(1, 0, 2, 3, 4).reshape(B, S, B_HEADS, B_VDIM)

def diff_attn_sample(q, k_new, v_new, cache_k, cache_v, page_table, lam):
    DB, T = q.shape[:2]
    n_pages = page_table.shape[1]
    past = n_pages * PAGE_SIZE
    slopes = alibi_slopes()
    qs = q.astype(F32) * B_DH ** -0.5
    qpos = past + jnp.arange(T)

    def alibi(kpos):
        return (-slopes[:, None, None] * (qpos[:, None] - kpos[None, :]).astype(F32))[None, :, None]

    def merge(carry, s, vv):
        m, l, acc = carry
        m_new = jnp.maximum(m, s.max(axis=-1))
        pe = jnp.exp(s - m_new[..., None])
        corr = jnp.exp(m - m_new)
        l = l * corr + pe.sum(axis=-1)
        acc = acc * corr[..., None] + jnp.einsum('bhctk,bkhv->bhctv', pe, vv)
        return (m_new, l, acc)

    def page_step(carry, p):
        phys = page_table[:, p]
        kp = cache_k[phys].astype(F32).reshape(DB, PAGE_SIZE, B_HEADS, 2, B_DH)
        vp = cache_v[phys].astype(F32)
        s = jnp.einsum('bthcd,bkhcd->bhctk', qs, kp) + alibi(p * PAGE_SIZE + jnp.arange(PAGE_SIZE))
        return merge(carry, s, vp), None

    init = (jnp.full((DB, B_HEADS, 2, T), NEG_BIG, F32), jnp.zeros((DB, B_HEADS, 2, T), F32),
            jnp.zeros((DB, B_HEADS, 2, T, B_VDIM), F32))
    carry, _ = lax.scan(page_step, init, jnp.arange(n_pages))
    s = jnp.einsum('bthcd,bkhcd->bhctk', qs, k_new.astype(F32)) + alibi(qpos)
    s = jnp.where(jnp.tril(jnp.ones((T, T), dtype=bool)), s, -jnp.inf)
    m, l, acc = merge(carry, s, v_new.astype(F32))
    o = acc / l[..., None]
    out = o[:, :, 0] - lam * o[:, :, 1]
    return out.transpose(0, 2, 1, 3)

def hier_moe(h, w_group, w_sub, w_gate, w_up, w_down):
    hf = h.astype(F32)
    pg = jax.nn.softmax(hf @ w_group.astype(F32), axis=-1)
    gidx = jnp.argmax(pg, axis=-1)
    gprob = jnp.max(pg, axis=-1)
    sub_all = jnp.einsum('btd,gde->btge', hf, w_sub.astype(F32))
    sub = jnp.einsum('btg,btge->bte', jax.nn.one_hot(gidx, MOE_GROUPS, dtype=F32), sub_all)
    vals, idx = lax.top_k(sub, MOE_TOP_K)
    w2 = jax.nn.softmax(vals, axis=-1) * gprob[..., None]
    eid = gidx[..., None] * MOE_EPG + idx
    gates = jnp.einsum('btke,btk->bte', jax.nn.one_hot(eid, MOE_EXPERTS, dtype=F32), w2)
    hid = jax.nn.silu(jnp.einsum('btd,edf->btef', h, w_gate)) * jnp.einsum('btd,edf->btef', h, w_up)
    hid = hid * gates.astype(h.dtype)[..., None]
    return jnp.einsum('btef,efd->btd', hid, w_down)

def _trunk(x, hgrn_s0, cache_k, cache_v, page_table, norm_mix_w, norm_ffn_w, a_w_in, a_lb_logits, a_gnorm_w,
           a_w_o, kv_norm_w, w_kv, b_w_q, b_lambda_q1, b_lambda_k1, b_lambda_q2, b_lambda_k2, b_subln_w, b_w_o,
           moe_w_group, moe_w_sub, moe_w_gate, moe_w_up, moe_w_down, final_norm_w):
    B, T, _ = x.shape
    sample = cache_k is not None
    lbs = lower_bounds(a_lb_logits)
    new_states = []
    k_sh = None
    v_sh = None
    h = x
    for l in range(DEPTH):
        hn = rmsnorm(h, norm_mix_w[l])
        if l < N_A_LAYERS:
            s0 = hgrn_s0[l] if sample else jnp.zeros((B, A_HEADS, A_DK, A_DV), F32)
            mix, s_new = hgrn2_mixer(hn, a_w_in[l], lbs[l], a_gnorm_w[l], a_w_o[l], s0)
            new_states.append(s_new.astype(x.dtype))
        else:
            j = l - N_A_LAYERS
            lam_init = 0.8 - 0.6 * math.exp(-0.3 * l)
            lam = (jnp.exp(jnp.sum(b_lambda_q1[j].astype(F32) * b_lambda_k1[j].astype(F32)))
                   - jnp.exp(jnp.sum(b_lambda_q2[j].astype(F32) * b_lambda_k2[j].astype(F32))) + lam_init)
            q = (hn @ b_w_q[j]).reshape(B, T, B_HEADS, 2, B_DH)
            kk = k_sh.reshape(B, T, B_HEADS, 2, B_DH)
            if sample:
                o = diff_attn_sample(q, kk, v_sh, cache_k, cache_v, page_table, lam)
            else:
                o = diff_attn_prompt(q, kk, v_sh, lam)
            o = rmsnorm(o, b_subln_w[j], SUBLN_EPS) * (1.0 - lam_init)
            mix = o.astype(x.dtype).reshape(B, T, B_WIDTH) @ b_w_o[j]
        h = h + mix
        h = h + hier_moe(rmsnorm(h, norm_ffn_w[l]), moe_w_group[l], moe_w_sub[l], moe_w_gate[l],
                         moe_w_up[l], moe_w_down[l])
        if l == N_A_LAYERS - 1:
            kv = rmsnorm(h, kv_norm_w) @ w_kv
            k_sh = kv[..., :B_WIDTH].reshape(B, T, B_HEADS, 2 * B_DH)
            v_sh = kv[..., B_WIDTH:].reshape(B, T, B_HEADS, B_VDIM)
    y = rmsnorm(h, final_norm_w)
    return y, jnp.stack(new_states), k_sh, v_sh

def setup_inputs(seed: int = 0) -> dict:
    key = jax.random.key(seed)
    ks = jax.random.split(key, 32)
    n_pages = PAST_LEN // PAGE_SIZE
    n_used = DEC_BATCH * n_pages
    n_pool = n_used + n_used // 4
    out_scale = (2 * DEPTH) ** -0.5

    def nrm(k, shape, scale):
        return jax.random.normal(k, shape, F32) * scale

    return {
        'x_prompt': nrm(ks[0], (BATCH, SEQ, D_MODEL), 1.0),
        'x_sample': nrm(ks[1], (DEC_BATCH, DEC_SEQ, D_MODEL), 1.0),
        'state_hgrn': nrm(ks[2], (N_A_LAYERS, DEC_BATCH, A_HEADS, A_DK, A_DV), 0.5),
        'cache_k': nrm(ks[3], (n_pool, PAGE_SIZE, B_HEADS, 2 * B_DH), 1.0),
        'cache_v': nrm(ks[4], (n_pool, PAGE_SIZE, B_HEADS, B_VDIM), 1.0),
        'page_table': jax.random.permutation(ks[5], n_pool)[:n_used].reshape(DEC_BATCH, n_pages).astype(jnp.int32),
        'norm_mix_w': 1.0 + nrm(ks[6], (DEPTH, D_MODEL), 0.02),
        'norm_ffn_w': 1.0 + nrm(ks[7], (DEPTH, D_MODEL), 0.02),
        'a_w_in': nrm(ks[8], (N_A_LAYERS, D_MODEL, 4 * A_WIDTH), D_MODEL ** -0.5),
        'a_lb_logits': nrm(ks[9], (N_A_LAYERS, A_WIDTH), 0.5),
        'a_gnorm_w': 1.0 + nrm(ks[10], (N_A_LAYERS, A_DV), 0.02),
        'a_w_o': nrm(ks[11], (N_A_LAYERS, A_WIDTH, D_MODEL), A_WIDTH ** -0.5 * out_scale),
        'kv_norm_w': 1.0 + nrm(ks[12], (D_MODEL,), 0.02),
        'w_kv': nrm(ks[13], (D_MODEL, 2 * B_WIDTH), D_MODEL ** -0.5),
        'b_w_q': nrm(ks[14], (N_B_LAYERS, D_MODEL, B_WIDTH), D_MODEL ** -0.5),
        'b_lambda_q1': nrm(ks[15], (N_B_LAYERS, B_DH), 0.1),
        'b_lambda_k1': nrm(ks[16], (N_B_LAYERS, B_DH), 0.1),
        'b_lambda_q2': nrm(ks[17], (N_B_LAYERS, B_DH), 0.1),
        'b_lambda_k2': nrm(ks[18], (N_B_LAYERS, B_DH), 0.1),
        'b_subln_w': 1.0 + nrm(ks[19], (N_B_LAYERS, B_VDIM), 0.02),
        'b_w_o': nrm(ks[20], (N_B_LAYERS, B_WIDTH, D_MODEL), B_WIDTH ** -0.5 * out_scale),
        'moe_w_group': nrm(ks[21], (DEPTH, D_MODEL, MOE_GROUPS), D_MODEL ** -0.5),
        'moe_w_sub': nrm(ks[22], (DEPTH, MOE_GROUPS, D_MODEL, MOE_EPG), D_MODEL ** -0.5),
        'moe_w_gate': nrm(ks[23], (DEPTH, MOE_EXPERTS, D_MODEL, MOE_D_EXPERT), D_MODEL ** -0.5),
        'moe_w_up': nrm(ks[24], (DEPTH, MOE_EXPERTS, D_MODEL, MOE_D_EXPERT), D_MODEL ** -0.5),
        'moe_w_down': nrm(ks[25], (DEPTH, MOE_EXPERTS, MOE_D_EXPERT, D_MODEL), MOE_D_EXPERT ** -0.5 * out_scale),
        'final_norm_w': 1.0 + nrm(ks[26], (D_MODEL,), 0.02),
    }

def reference(x_prompt, x_sample, state_hgrn, cache_k, cache_v, page_table, norm_mix_w, norm_ffn_w, a_w_in,
              a_lb_logits, a_gnorm_w, a_w_o, kv_norm_w, w_kv, b_w_q, b_lambda_q1, b_lambda_k1, b_lambda_q2,
              b_lambda_k2, b_subln_w, b_w_o, moe_w_group, moe_w_sub, moe_w_gate, moe_w_up, moe_w_down,
              final_norm_w):
    y_prompt, state_hgrn_prompt, k_prompt, v_prompt = _trunk(
        x_prompt, None, None, None, None, norm_mix_w, norm_ffn_w, a_w_in, a_lb_logits, a_gnorm_w, a_w_o,
        kv_norm_w, w_kv, b_w_q, b_lambda_q1, b_lambda_k1, b_lambda_q2, b_lambda_k2, b_subln_w, b_w_o,
        moe_w_group, moe_w_sub, moe_w_gate, moe_w_up, moe_w_down, final_norm_w)
    y_sample, state_hgrn_sample, k_sample, v_sample = _trunk(
        x_sample, state_hgrn, cache_k, cache_v, page_table, norm_mix_w, norm_ffn_w, a_w_in, a_lb_logits,
        a_gnorm_w, a_w_o, kv_norm_w, w_kv, b_w_q, b_lambda_q1, b_lambda_k1, b_lambda_q2, b_lambda_k2,
        b_subln_w, b_w_o, moe_w_group, moe_w_sub, moe_w_gate, moe_w_up, moe_w_down, final_norm_w)
    return (y_prompt, y_sample, state_hgrn_prompt, state_hgrn_sample, k_prompt, v_prompt, k_sample, v_sample)


_drawn_inputs = setup_inputs


def setup_inputs(seed=0):
    import zlib

    import numpy as np

    out = dict(_drawn_inputs(seed))
    spreads = {}
    factors = {'norm_ffn_w': 2.807,
     'a_gnorm_w': 4.339,
     'kv_norm_w': 2.883,
     'b_lambda_k1': 3.272,
     'b_lambda_q2': 2.686,
     'b_lambda_k2': 5.226,
     'b_subln_w': 8.0,
     'final_norm_w': 2.77}
    for name, (base, spread) in spreads.items():
        noise = np.random.default_rng([zlib.crc32(name.encode()), seed]).standard_normal(out[name].shape)
        drawn = base * np.exp(spread * noise) if base else spread * noise
        out[name] = __import__('jax').numpy.asarray(drawn.astype(out[name].dtype))
    for name, factor in factors.items():
        out[name] = (out[name] * factor).astype(out[name].dtype)
    return out
```

```python
import math
from contextlib import ExitStack, contextmanager

import concourse.bass as bass
from concourse import mybir

F32 = mybir.dt.float32
I32 = mybir.dt.int32
ALU = mybir.AluOpType
ACT = mybir.ActivationFunctionType
AX = mybir.AxisListType

P = 128
D = 1024
DC = D // P
SEQ = 512
DEC_B, DEC_T = 8, 4
SMP = DEC_B * DEC_T
TOK = SEQ + SMP
PT = SEQ // P
NT = PT + 1
HEADS = 8
HB = 512
EPG, GROUPS, EXPERTS, TOPK = 4, 4, 16, 2
FF = 256
BLOCKS = (TOK * TOPK - EXPERTS) // P + EXPERTS
SLOTS = BLOCKS * P
PAGE, PAGES = 128, 16
PAST = PAGE * PAGES
LEVELS = (8, 16, 32, 64, 128)
LAM_INIT = 0.8 - 0.6 * math.exp(-0.3)
FG_MIN = 2.0 ** -63
MASKED = 1e30
EPS, SUBLN_EPS = 1e-6, 1e-5
WEIGHT_SLOTS = 3


def rows(t):
    return P if t < PT else SMP


def cols(t):
    return slice(t * P, t * P + rows(t))


class Chain:

    def __init__(self, eng, sem, start=0):
        self.eng, self.sem, self.n = eng, sem, start

    def __call__(self, ins):
        self.n = self.n + 1
        ins.then_inc(self.sem, 1)
        self.eng.wait_ge(self.sem, self.n)


class Core:

    def __init__(self, nc, ctx):
        self.nc, self.ctx, self.stage_sems = nc, ctx, None
        self.ps = [self.psum(f"bank{i}", [P, HB]) for i in range(8)]
        self.ident = self.sb("ident", [P, P])
        self.ones = self.sb("ones", [1, P])
        self.h = self.sb("h", [P, NT, D])
        self.xT = self.sb("xT", [P, DC, TOK])
        self.stat = self.sb("stat", [P, 64])
        self.ss, self.ms, self.r0 = self.stat[:, 0:5], self.stat[:, 8:13], self.stat[:, 16:21]
        self.tmp, self.r = self.stat[:, 24:29], self.stat[:, 32:37]
        self.wring = [self.sb(f"wring{i}", [P, DC, HB]) for i in range(WEIGHT_SLOTS)]
        self.cw = self.sb("column_weights", [P, 5, DC])
        self.rowbuf = self.sb("row_weights", [1, 2 * P + 4 * 64])
        self.lamwork = self.sb("lambda_products", [1, 2, 64])
        self.levelmask = self.sb("level_masks", [P, 1 + len(LEVELS), P])
        self.restart = self.sb("scan_restart", [P, TOK])
        self.batchmask = self.sb("batch_mask", [SMP, DEC_B])
        self.lb = self.sb("lower_bound", [P, 4, HEADS])
        self.w_in = [self.sem(f"weights_landed{i}") for i in range(WEIGHT_SLOTS)]
        self.w_done = []
        self.w_issued = 0
        self.w_taken = 0
        self.order = {n: self.sem(f"{n}_order") for n in ("vector", "scalar", "gpsimd")}
        self.order_n = dict.fromkeys(self.order, 0)

    def sb(self, name, shape, dt=F32):
        return self.ctx.enter_context(self.nc.sbuf_tensor(name, shape, dt))

    def psum(self, name, shape, dt=F32):
        return self.ctx.enter_context(self.nc.psum_tensor(name, shape, dt))

    def sem(self, name):
        if self.stage_sems is None:
            return self.ctx.enter_context(self.nc.semaphore(name))
        self.stage_sems.append(self.nc.alloc_semaphore(name))
        return self.stage_sems[-1]

    @contextmanager
    def stage(self):
        self.stage_sems = []
        yield
        self.w_done = [None] * len(self.w_done)
        self.nc.clear_and_free_semaphores(self.stage_sems)
        self.nc.all_engine_barrier()
        self.stage_sems = None

    def load_weights(self, sp, halves):
        n = self.w_issued
        if n >= WEIGHT_SLOTS and self.w_done[n - WEIGHT_SLOTS]:
            sp.wait_ge(*self.w_done[n - WEIGHT_SLOTS])
        slot = n % WEIGHT_SLOTS
        for dst, src in halves(self.wring[slot]):
            sp.dma_start(dst, src).then_inc(self.w_in[slot], 16)
        self.w_issued += 1

    def take_weights(self, pe):
        n = self.w_taken
        pe.wait_ge(self.w_in[n % WEIGHT_SLOTS], 32 * (n // WEIGHT_SLOTS + 1))
        self.w_taken += 1
        return self.wring[n % WEIGHT_SLOTS]


def column_halves(w, n0):
    view = w.rearrange("(c p) n -> p c n", p=P)
    half = DC // 2
    return lambda tile: [(tile[:, 0:half, :], view[:, 0:half, n0:n0 + HB]),
                         (tile[:, half:DC, :], view[:, half:DC, n0:n0 + HB])]


def bcast(ap, axis, shape):
    return ap.unsqueeze(axis).to_broadcast(shape)



def setup(k, a, xs):
    nc = k.nc
    loaded, made = k.sem("inputs_loaded"), k.sem("constants_made")
    with nc.Block() as block:
        @block.sync
        def _(sp):
            for t in range(PT):
                sp.dma_start(k.h[:, t, :], a["x_prompt"][0, t * P:(t + 1) * P, :]).then_inc(loaded, 16)
            sp.dma_start(k.h[0:SMP, PT, :], a["x_sample"].rearrange("b t d -> (b t) d")).then_inc(loaded, 16)
            for i in range(2):
                k.load_weights(sp, column_halves(a["a_w_in"][0], 2 * D + i * HB))
            k.load_weights(sp, head_pair_halves(a, 0))
            sp.wait_ge(loaded, 15 * 16)

        @block.scalar
        def _(act):
            cols_of = lambda w: w.rearrange("(c p) -> p c", p=P)
            for i, w in enumerate((a["norm_mix_w"][0], a["norm_mix_w"][1], a["kv_norm_w"],
                                   a["norm_ffn_w"][0], a["norm_ffn_w"][1])):
                act.dma_start(k.cw[:, i, :], cols_of(w), allow_slow_non_contiguous=True).then_inc(loaded, 16)
            act.dma_start(k.lb[:, 0, :], cols_of(a["a_lb_logits"][0]), allow_slow_non_contiguous=True).then_inc(loaded, 16)
            r = k.rowbuf
            act.dma_start(r[:, 0:P], a["a_gnorm_w"]).then_inc(loaded, 16)
            act.dma_start(r[:, P:2 * P], a["b_subln_w"]).then_inc(loaded, 16)
            lam = r[:, 2 * P:].rearrange("a (i n) -> a i n", i=4)
            act.dma_start(lam[:, 0, :], a["b_lambda_q1"]).then_inc(loaded, 16)
            act.dma_start(lam[:, 1, :], a["b_lambda_k1"]).then_inc(loaded, 16)

        @block.gpsimd
        def _(pool):
            ch = Chain(pool, k.order["gpsimd"], k.order_n["gpsimd"])
            ch(pool.memset(k.ident[:, :], 0.0))
            ch(pool.affine_select(out=k.ident[:, :], in_=k.ident[:, :], compare_op=ALU.not_equal, fill=1.0,
                                  base=0, pattern=[[-1, P]], channel_multiplier=1))
            ch(pool.memset(k.ones[:, :], 1.0))
            ch(pool.memset(k.levelmask[:, :, :], 0.0))
            m = k.levelmask[:, 0, :].rearrange("p (n r) -> p n r", r=4)
            ch(pool.memset(m, 1.0))
            ch(pool.affine_select(out=m, in_=m, compare_op=ALU.is_ge, fill=0.0, base=0,
                                  pattern=[[-4, P // 4], [0, 4]], channel_multiplier=1))
            ch(pool.affine_select(out=m, in_=m, compare_op=ALU.is_ge, fill=0.0, base=0,
                                  pattern=[[4, P // 4], [1, 4]], channel_multiplier=-1))
            for i, size in enumerate(LEVELS):
                half = size // 2
                m = k.levelmask[:, i + 1, :].rearrange("p (n r) -> p n r", r=size)[:, :, half:size]
                ch(pool.memset(m, 1.0))
                ch(pool.affine_select(out=m, in_=m, compare_op=ALU.is_ge, fill=0.0, base=0,
                                      pattern=[[-size, P // size], [0, half]], channel_multiplier=1))
                ch(pool.affine_select(out=m, in_=m, compare_op=ALU.is_ge, fill=0.0, base=half - 1,
                                      pattern=[[size, P // size], [0, half]], channel_multiplier=-1))
            ch(pool.memset(k.restart[:, :], 1.0))
            ch(pool.memset(k.restart[:, 0:SEQ].rearrange("p (c n) -> p c n", n=P)[:, :, 0:1], 0.0))
            ch(pool.memset(k.restart[:, SEQ:TOK].rearrange("p (c n) -> p c n", n=DEC_T)[:, :, 0:1], 0.0))
            ch(pool.memset(k.batchmask[:, :], 1.0))
            ch(pool.affine_select(out=k.batchmask[:, :], in_=k.batchmask[:, :], compare_op=ALU.is_ge, fill=0.0,
                                  base=0, pattern=[[-DEC_T, DEC_B]], channel_multiplier=1))
            ch(pool.affine_select(out=k.batchmask[:, :], in_=k.batchmask[:, :], compare_op=ALU.is_ge, fill=0.0,
                                  base=DEC_T - 1, pattern=[[DEC_T, DEC_B]], channel_multiplier=-1))
            k.order_n["gpsimd"] = ch.n
            lam = k.rowbuf[:, 2 * P:].rearrange("a (i n) -> a i n", i=4)
            pool.dma_start(lam[:, 2, :], a["b_lambda_q2"]).then_inc(made, 16)
            pool.dma_start(lam[:, 3, :], a["b_lambda_k2"]).then_inc(made, 16)
            pool.wait_ge(made, 32)

        @block.vector
        def _(dve):
            for q in range(1, 4):
                nc.vector.memset(k.h[32 * q:32 * q + 32, PT, :], 0.0)


def head_pair_halves(a, pair):
    view = a["a_w_in"][0].rearrange("(c p) n -> p c n", p=P)
    n = 2 * P
    return lambda tile: [(tile[:, :, 0:n], view[:, :, pair * n:(pair + 1) * n]),
                         (tile[:, :, n:2 * n], view[:, :, D + pair * n:D + (pair + 1) * n])]



def inverse_root(dve, act_ready, root_ready, ch, nc, ms, r0, tmp, r):
    dve.wait_ge(*root_ready)
    ch(nc.vector.tensor_tensor(tmp, r0, r0, ALU.mult))
    ch(nc.vector.tensor_tensor(tmp, tmp, ms, ALU.mult))
    ch(nc.vector.tensor_scalar(tmp, tmp, -0.5, 1.5, ALU.mult, ALU.add))
    ch(nc.vector.tensor_tensor(r, r0, tmp, ALU.mult))


def norm_block(k, tag, weights, xs, store=None):
    nc = k.nc
    squares_a, squares_v = k.sem(f"{tag}_squares_act"), k.sem(f"{tag}_squares_dve")
    mean_ready, seed_ready = k.sem(f"{tag}_mean"), k.sem(f"{tag}_seed")
    xs_ready, turned = k.sem(f"{tag}_xs"), k.sem(f"{tag}_turned")
    out_v, out_a = k.sem(f"{tag}_out_dve"), k.sem(f"{tag}_out_act")
    ACT_TILES = (2, 3, 4)
    half = DC // 2
    nw = len(weights)
    junk = xs
    with nc.Block() as block:
        @block.scalar
        def _(act):
            for t in ACT_TILES:
                nc.scalar.activation(junk[:, t, :], k.h[:, t, :], ACT.Square,
                                     accum_out=k.ss[:, t:t + 1]).then_inc(squares_a, 1)
            act.wait_ge(mean_ready, 1)
            nc.scalar.activation(k.tmp, k.ms, ACT.Ln).then_inc(seed_ready, 1)
            act.wait_ge(seed_ready, 1)
            nc.scalar.activation(k.r0, k.tmp, ACT.Exp, scale=-0.5).then_inc(seed_ready, 1)
            for t in range(NT):
                act.wait_ge(turned, t + 1)
                for i, (w, out) in enumerate(weights):
                    for c in range(half, DC):
                        src = k.ps[2 * (t % 2) + 1][:, (c - half) * P:(c - half) * P + rows(t)]
                        nc.scalar.activation(out[:, c, cols(t)], src, ACT.Copy,
                                             scale=w[:, c:c + 1]).then_inc(out_a, 1)

        @block.vector
        def _(dve):
            ch = Chain(dve, k.order["vector"], k.order_n["vector"])
            for t in range(NT):
                if t not in ACT_TILES:
                    nc.vector.tensor_tensor_reduce(out=junk[:, t, :], in0=k.h[:, t, :], in1=k.h[:, t, :], scale=1.0,
                                                   scalar=0.0, op0=ALU.mult, op1=ALU.add,
                                                   accum_out=k.ss[:, t:t + 1]).then_inc(squares_v, 1)
            dve.wait_ge(squares_a, len(ACT_TILES))
            dve.wait_ge(squares_v, NT - len(ACT_TILES))
            nc.vector.tensor_scalar(k.ms, k.ss, 1.0 / D, EPS, ALU.mult, ALU.add).then_inc(mean_ready, 1)
            dve.wait_ge(mean_ready, 1)
            inverse_root(dve, None, (seed_ready, 2), ch, nc, k.ms, k.r0, k.tmp, k.r)
            for t in range(NT):
                nc.vector.tensor_scalar(xs[:, t, :], k.h[:, t, :], k.r[:, t:t + 1], None, ALU.mult)\
                    .then_inc(xs_ready, 1)
            for t in range(NT):
                dve.wait_ge(turned, t + 1)
                for w, out in weights:
                    src = k.ps[2 * (t % 2)][:, :].rearrange("p (c n) -> p c n", c=half)[:, :, 0:rows(t)]
                    nc.vector.tensor_tensor(out[:, 0:half, cols(t)], src,
                                            bcast(w[:, 0:half], 2, [P, half, rows(t)]), ALU.mult).then_inc(out_v, 1)
            k.order_n["vector"] = ch.n

        @block.tensor
        def _(pe):
            for t in range(NT):
                pe.wait_ge(xs_ready, t + 1)
                if t >= 2:
                    pe.wait_ge(out_v, nw * (t - 1))
                    pe.wait_ge(out_a, nw * half * (t - 1))
                for c in range(DC):
                    last = nc.tensor.transpose(k.ps[2 * (t % 2) + c // half][:, (c % half) * P:(c % half) * P + rows(t)],
                                               xs[0:rows(t), t, c * P:(c + 1) * P], k.ident[0:rows(t), 0:rows(t)])
                last.then_inc(turned, 1)

        if store is not None:
            @block.sync
            def _(sp):
                store(sp, xs_ready)


def broadcast_rows(k, rep):
    nc = k.nc
    summed, turned, out = k.sem("lambda_summed"), k.sem("rows_spread"), k.sem("rows_out")
    lam = k.rowbuf[:, 2 * P:].rearrange("a (i n) -> a i n", i=4)
    s = k.stat[0:1, 40:48]
    with nc.Block() as block:
        @block.vector
        def _(dve):
            for i in range(2):
                nc.vector.tensor_tensor_reduce(out=k.lamwork[:, i, :],
                                               in0=lam[:, 2 * i, :], in1=lam[:, 2 * i + 1, :], scale=1.0, scalar=0.0,
                                               op0=ALU.mult, op1=ALU.add, accum_out=s[:, i:i + 1]).then_inc(summed, 1)
            dve.wait_ge(summed, 3)
            nc.vector.scalar_tensor_tensor(out=s[:, 4:5], in0=s[:, 3:4], scalar=-LAM_INIT, in1=s[:, 2:3], op0=ALU.add,
                                           op1=ALU.subtract).then_inc(summed, 1)
            dve.wait_ge(turned, 1)
            nc.vector.tensor_copy(rep[:, 0:P], k.ps[7][:, 0:P]).then_inc(out, 1)
            nc.vector.tensor_scalar(rep[:, P:2 * P], k.ps[7][:, P:2 * P], 1.0 - LAM_INIT, None, ALU.mult).then_inc(out, 1)
            nc.vector.tensor_copy(rep[:, 2 * P:2 * P + 1], k.ps[7][:, 2 * P:2 * P + 1]).then_inc(out, 1)

        @block.scalar
        def _(act):
            act.wait_ge(summed, 2)
            nc.scalar.activation(s[:, 2:4], s[:, 0:2], ACT.Exp).then_inc(summed, 1)

        @block.tensor
        def _(pe):
            nc.tensor.matmul(k.ps[7][:, 0:2 * P], k.ones[0:1, :], k.rowbuf[:, 0:2 * P], start=True, stop=True)
            pe.wait_ge(summed, 4)
            nc.tensor.matmul(k.ps[7][:, 2 * P:2 * P + 1], k.ones[0:1, :], s[:, 4:5], start=True, stop=True).then_inc(turned, 1)



def hgrn_block(k, a, v, g, o, gnorm):
    nc = k.nc
    NLEV = 1 + len(LEVELS)
    with ExitStack() as tmp_ctx:
        def sb(name, shape):
            return tmp_ctx.enter_context(nc.sbuf_tensor(name, shape, F32))

        f_in, q = [sb(f"gla_fin{i}", [P, TOK]) for i in range(2)], [sb(f"gla_q{i}", [P, TOK]) for i in range(2)]
        kk, b = sb("gla_k", [P, TOK]), sb("gla_b", [P, TOK])
        mid4 = sb("gla_mid4", [P, TOK // 4])
        diff = [sb(f"gla_diff{i}", [P, TOK]) for i in range(2)]
        inv4 = sb("gla_inv4", [P, TOK])
        eb, kd = sb("gla_eb", [P, TOK]), inv4
        QE = [sb(f"gla_qe{i}", [P, TOK if i == 0 else SEQ]) for i in range(NLEV)]
        KE = [sb(f"gla_ke{i}", [P, TOK if i == 0 else SEQ]) for i in range(NLEV)]
        QS = sb("gla_qs", [P, TOK])
        QB = sb("gla_qb", [P, DEC_B * (SMP + DEC_T)])
        A = sb("gla_att", [P, PT, P])
        AS = sb("gla_att_s", [SMP, SMP])
        kdT, kdTs = sb("gla_kdT", [P, PT, P]), sb("gla_kdTs", [SMP, P])
        vm = sb("gla_vm", [SMP, DEC_B, P])
        S = [sb("gla_s", [P, PT, P])] * 2
        s0 = [sb(f"gla_s0_{i}", [P, DEC_B, P]) for i in range(2)]
        sn = [sb("gla_sn", [P, DEC_B, P])] * 2

        units = {}
        order = [("v", i, t) for i in range(2) for t in range(NT)]
        for h in range(HEADS):
            order += [("f", h), ("q", h), ("s", h)]
        order += [("g", i, t) for i in range(2) for t in range(NT)]
        n = 0
        for i, u in enumerate(order):
            if u[0] == "s":
                units[u] = (i + 1, 2)
            else:
                units[u] = (i + 1, n % 2)
                n += 1
        proj_done = k.sem("proj_done")
        v_out, qf_out, g_out = k.sem("v_evacuated"), k.sem("qf_evacuated"), k.sem("g_evacuated")
        evacuated = {}
        for u in order:
            if u[0] == "v":
                evacuated[u] = (v_out, NT * u[1] + u[2] + 1)
            elif u[0] == "g":
                evacuated[u] = (g_out, NT * u[1] + u[2] + 1)
            else:
                evacuated[u] = (qf_out, 4 * u[1] + {"f": 1, "q": 3, "s": 4}[u[0]])
        before = {}
        last_in = {}
        for u in order:
            before[u] = last_in.get(units[u][1])
            last_in[units[u][1]] = u

        fgc_ready, logf_ready, b_ready = k.sem("fg_ready"), k.sem("logf_ready"), k.sem("b_ready")
        diff_ready, exp_ready = k.sem("diff_ready"), k.sem("exp_ready")
        q_lev, k_lev = k.sem("q_level_ready"), k.sem("k_level_ready")
        kk_ready = k.sem("k_ready")
        turned, turned_out = k.sem("kd_turned"), k.sem("kd_turned_out")
        att_done, att_taken = k.sem("att_done"), k.sem("att_taken")
        ds_done, s_ready = k.sem("state_step_done"), k.sem("state_ready")
        sds_done, sn_ready, sn_scaled = k.sem("sample_step_done"), k.sem("sample_state_ready"), k.sem("sample_state_scaled")
        vm_ready, o_done, o_out = k.sem("vm_ready"), k.sem("o_done"), k.sem("o_evacuated")
        s0_in = [k.sem(f"s0_landed{i}") for i in range(2)]
        s_store, sn_store = [k.sem("s_stored")], [k.sem("sn_stored")]
        head = lambda h: slice(h * P, (h + 1) * P)
        blocks = lambda ap, n: ap.rearrange("p (c n) -> p c n", n=n)
        QBd = QB[:, :].rearrange("p (b x) -> p b x", x=SMP + DEC_T)[:, :, 0:DEC_T]

        with nc.Block() as block:
            @block.scalar
            def _(act):
                def evacuate_qf(h):
                    done, bank = units[("f", h)]
                    act.wait_ge(proj_done, done)
                    if h >= 2:
                        act.wait_ge(q_lev, (NLEV + 2) * (h - 1))
                    nc.scalar.activation(f_in[h % 2][:, 0:SEQ], k.ps[bank][:, :], ACT.Sigmoid).then_inc(qf_out, 1)
                    done, _ = units[("s", h)]
                    act.wait_ge(proj_done, done)
                    nc.scalar.activation(f_in[h % 2][:, SEQ:TOK], k.ps[2][:, 0:SMP], ACT.Sigmoid).then_inc(qf_out, 1)
                    _, bank = units[("q", h)]
                    nc.scalar.activation(q[h % 2][:, 0:SEQ], k.ps[bank][:, :], ACT.Silu).then_inc(qf_out, 1)
                    nc.scalar.activation(q[h % 2][:, SEQ:TOK], k.ps[2][:, SMP:2 * SMP], ACT.Silu).then_inc(qf_out, 1)

                def gla(h):
                    act.wait_ge(fgc_ready, 2 * h + 2)
                    nc.scalar.activation(f_in[h % 2][:, :], f_in[h % 2][:, :], ACT.Ln).then_inc(logf_ready, 1)
                    base = (NLEV + 1) * h
                    act.wait_ge(diff_ready, base + 1)
                    if h:
                        act.wait_ge(sn_scaled, h)
                    nc.scalar.activation(inv4[:, :], diff[0][:, :], ACT.Exp, scale=-1.0).then_inc(exp_ready, 1)
                    nc.scalar.activation(diff[0][:, :], diff[0][:, :], ACT.Exp).then_inc(exp_ready, 1)
                    nc.scalar.activation(eb[:, :], b[:, :], ACT.Exp).then_inc(exp_ready, 1)
                    for i in range(1, NLEV + 1):
                        act.wait_ge(diff_ready, base + i + 1)
                        w = TOK if i == NLEV else SEQ
                        nc.scalar.activation(diff[i % 2][:, 0:w], diff[i % 2][:, 0:w], ACT.Exp).then_inc(exp_ready, 1)
                    act.wait_ge(turned, h + 1)
                    nc.scalar.activation(kdT[:, :, :], k.ps[5][:, :], ACT.Copy).then_inc(turned_out, 1)
                    nc.scalar.activation(kdTs[:, :], k.ps[6][0:SMP, P:2 * P], ACT.Copy).then_inc(turned_out, 1)
                    act.wait_ge(o_done, h + 1)
                    nc.scalar.activation(o[:, 0:PT, head(h)], k.ps[7][:, :].rearrange("p (c n) -> p c n", c=PT), ACT.Copy)\
                        .then_inc(o_out, 1)
                    nc.scalar.activation(o[0:SMP, PT, head(h)], k.ps[6][0:SMP, 2 * P:3 * P], ACT.Copy).then_inc(o_out, 1)

                for h in range(HEADS):
                    evacuate_qf(h)
                    if h >= 1:
                        gla(h - 1)
                for i in range(2):
                    for t in range(NT):
                        done, bank = units[("g", i, t)]
                        act.wait_ge(proj_done, done)
                        nc.scalar.activation(g[0:rows(t), t, i * HB:(i + 1) * HB], k.ps[bank][0:rows(t), :], ACT.Silu)\
                            .then_inc(g_out, 1)
                gla(HEADS - 1)

            @block.vector
            def _(dve):
                ch = Chain(dve, k.order["vector"], k.order_n["vector"])
                lb = k.lb
                ch(nc.vector.tensor_tensor(lb[:, 1, :], lb[:, 0, :], lb[:, 0, :], ALU.subtract))
                ch(nc.vector.tensor_scalar(lb[:, 1, :], lb[:, 1, :], 1.0, None, ALU.add))
                ch(nc.vector.tensor_tensor(lb[:, 2, :], lb[:, 1, :], lb[:, 1, :], ALU.subtract))
                ch(nc.vector.tensor_scalar(lb[:, 3, :], lb[:, 2, :], -1.0, 1.0, ALU.mult, ALU.add))
                for i, lev in enumerate(LEVELS):
                    nc.vector.memset(QE[i + 1][:, :], 0.0)
                    ch(nc.vector.memset(KE[i + 1][:, :], 0.0))
                nc.vector.memset(QB[:, :], 0.0)
                nc.vector.memset(A[:, :, :], 0.0)
                ch(nc.vector.memset(AS[:, :], 0.0))
                for x in range(1, 4):
                    nc.vector.memset(g[32 * x:32 * x + 32, PT, :], 0.0)
                    nc.vector.memset(v[32 * x:32 * x + 32, PT, :], 0.0)
                for i in range(2):
                    for t in range(NT):
                        done, bank = units[("v", i, t)]
                        dve.wait_ge(proj_done, done)
                        nc.vector.tensor_copy(v[0:rows(t), t, i * HB:(i + 1) * HB], k.ps[bank][0:rows(t), :])\
                            .then_inc(v_out, 1)

                def elementwise(h):
                    dve.wait_ge(qf_out, 4 * h + 2)
                    if h:
                        dve.wait_ge(k_lev, (NLEV + 1) * h)
                    nc.vector.tensor_scalar(f_in[h % 2][:, :], f_in[h % 2][:, :], lb[:, 3, h:h + 1], lb[:, 2, h:h + 1],
                                            ALU.mult, ALU.add).then_inc(fgc_ready, 1)
                    dve.wait_ge(fgc_ready, 2 * h + 1)
                    nc.vector.tensor_scalar(kk[:, :], f_in[h % 2][:, :], -1.0, 1.0, ALU.mult, ALU.add).then_inc(kk_ready, 1)
                    dve.wait_ge(kk_ready, h + 1)
                    nc.vector.tensor_scalar(f_in[h % 2][:, :], f_in[h % 2][:, :], FG_MIN, None, ALU.max).then_inc(fgc_ready, 1)
                    dve.wait_ge(logf_ready, h + 1)
                    ch(nc.vector.tensor_tensor_scan(b[:, :], k.restart[:, :], f_in[h % 2][:, :], 0.0, ALU.mult, ALU.add))
                    b4 = blocks(b[:, :], 4)
                    ch(nc.vector.tensor_tensor(mid4[:, :], b4[:, :, 1], b4[:, :, 2], ALU.add))
                    nc.vector.scalar_tensor_tensor(out=blocks(diff[0][:, :], 4), in0=bcast(mid4[:, :], 2, [P, TOK // 4, 4]),
                                                   scalar=0.5, in1=b4, op0=ALU.mult, op1=ALU.subtract).then_inc(diff_ready, 1)
                    ebase = (NLEV + 3) * h
                    for i in range(1, NLEV + 1):
                        d = diff[i % 2]
                        if i >= 2:
                            dve.wait_ge(k_lev, (NLEV + 1) * h + i - 1)
                            dve.wait_ge(q_lev, (NLEV + 2) * h + i)
                        if i < NLEV:
                            size = LEVELS[i - 1]
                            half = size // 2
                            bv, dv = blocks(b[:, 0:SEQ], size), blocks(d[:, 0:SEQ], size)
                            mid = bcast(bv[:, :, half - 1], 2, [P, SEQ // size, half])
                            nc.vector.tensor_tensor(dv[:, :, 0:half], mid, bv[:, :, 0:half], ALU.subtract)
                            nc.vector.tensor_tensor(dv[:, :, half:size], bv[:, :, half:size], mid, ALU.subtract)\
                                .then_inc(diff_ready, 1)
                        else:
                            for lo, hi, n in ((0, SEQ, P), (SEQ, TOK, DEC_T)):
                                bv, dv = blocks(b[:, lo:hi], n), blocks(d[:, lo:hi], n)
                                last = nc.vector.tensor_tensor(dv, bcast(bv[:, :, n - 1], 2, [P, (hi - lo) // n, n]), bv,
                                                               ALU.subtract)
                            last.then_inc(diff_ready, 1)
                        j = i - 1
                        if h and j == 0:
                            dve.wait_ge(att_done, (NLEV + 1) * h)
                            dve.wait_ge(o_done, h)
                        if j == 0:
                            dve.wait_ge(qf_out, 4 * h + 4)
                            dve.wait_ge(exp_ready, ebase + 3)
                            nc.vector.tensor_tensor(QE[0][:, :], q[h % 2][:, :], inv4[:, :], ALU.mult).then_inc(q_lev, 1)
                            nc.vector.tensor_tensor(QS[:, :], q[h % 2][:, :], eb[:, :], ALU.mult).then_inc(q_lev, 1)
                        else:
                            size = LEVELS[j - 1]
                            dve.wait_ge(exp_ready, ebase + 3 + j)
                            up = slice(size // 2, size)
                            nc.vector.tensor_tensor(blocks(QE[j][:, :], size)[:, :, up], blocks(q[h % 2][:, 0:SEQ], size)[:, :, up],
                                                    blocks(diff[j % 2][:, 0:SEQ], size)[:, :, up], ALU.mult).then_inc(q_lev, 1)
                    dve.wait_ge(q_lev, (NLEV + 2) * h + 2)
                    nc.vector.tensor_copy(QBd, blocks(QS[:, SEQ:TOK], DEC_T)).then_inc(q_lev, 1)

                def matrices(h):
                    if h:
                        dve.wait_ge(o_done, h)
                    for i in range(NLEV):
                        dve.wait_ge(att_done, (NLEV + 1) * h + i + 1)
                        nc.vector.copy_predicated(A[:, :, :], bcast(k.levelmask[:, i, :].bitcast(I32), 1, [P, PT, P]),
                                                  k.ps[3 + i % 2][:, :].rearrange("p (c n) -> p c n", c=PT)).then_inc(att_taken, 1)
                        dve.wait_ge(att_taken, (NLEV + 1) * h + i + 1)
                    dve.wait_ge(att_done, (NLEV + 1) * (h + 1))
                    nc.vector.copy_predicated(AS[:, :], k.levelmask[0:SMP, 0, 0:SMP].bitcast(I32), k.ps[7][0:SMP, 0:SMP])\
                        .then_inc(att_taken, 1)
                    dve.wait_ge(ds_done, h + 1)
                    if h:
                        dve.wait_ge(s_store[0], 16 * h)
                    for c in range(PT):
                        new, step = S[h % 2][:, c, :], k.ps[5][:, c * P:(c + 1) * P]
                        if c == 0:
                            nc.vector.tensor_copy(new, step).then_inc(s_ready, 1)
                        else:
                            dve.wait_ge(s_ready, PT * h + c)
                            nc.vector.scalar_tensor_tensor(out=new, in0=S[h % 2][:, c - 1, :],
                                                           scalar=eb[:, c * P + P - 1:c * P + P], in1=step,
                                                           op0=ALU.mult, op1=ALU.add).then_inc(s_ready, 1)
                    dve.wait_ge(sds_done, h + 1)
                    dve.wait_ge(sn_scaled, h + 1)
                    for i in range(2):
                        part = sn[h % 2][:, 4 * i:4 * i + 4, :]
                        nc.vector.tensor_tensor(part, part, k.ps[3 + i][:, :].rearrange("p (c n) -> p c n", c=4), ALU.add)\
                            .then_inc(sn_ready, 1)

                elementwise(0)
                for h in range(1, HEADS):
                    matrices(h - 1)
                    elementwise(h)
                for i in range(2):
                    for t in range(NT):
                        dve.wait_ge(g_out, NT * i + t + 1)
                        gv = g[0:rows(t), t, i * HB:(i + 1) * HB].rearrange("p (h n) -> p h n", n=P)
                        nc.vector.tensor_tensor(gv, gv, bcast(gnorm[0:rows(t), :], 1, [rows(t), 4, P]), ALU.mult)
                matrices(HEADS - 1)
                k.order_n["vector"] = ch.n

            @block.gpsimd
            def _(pool):
                for h in range(HEADS):
                    ebase = (NLEV + 3) * h
                    if h:
                        pool.wait_ge(att_done, (NLEV + 1) * h)
                    for j in range(NLEV):
                        pool.wait_ge(exp_ready, ebase + (2 if j == 0 else 3 + j))
                        if j == 0:
                            pool.wait_ge(kk_ready, h + 1)
                            nc.gpsimd.tensor_tensor(KE[0][:, :], kk[:, :], diff[0][:, :], ALU.mult).then_inc(k_lev, 1)
                        else:
                            size = LEVELS[j - 1]
                            lo = slice(0, size // 2)
                            nc.gpsimd.tensor_tensor(blocks(KE[j][:, :], size)[:, :, lo], blocks(kk[:, 0:SEQ], size)[:, :, lo],
                                                    blocks(diff[j % 2][:, 0:SEQ], size)[:, :, lo], ALU.mult).then_inc(k_lev, 1)
                    pool.wait_ge(q_lev, (NLEV + 2) * h + 1)
                    pool.wait_ge(exp_ready, ebase + 3 + NLEV)
                    nc.gpsimd.tensor_tensor(kd[:, :], kk[:, :], diff[NLEV % 2][:, :], ALU.mult).then_inc(k_lev, 1)
                    pool.wait_ge(v_out, 2 * NT)
                    if h:
                        pool.wait_ge(sds_done, h)
                    nc.gpsimd.tensor_tensor(vm[:, :, :], bcast(v[0:SMP, PT, head(h)], 1, [SMP, DEC_B, P]),
                                            bcast(k.batchmask[:, :], 2, [SMP, DEC_B, P]), ALU.mult).then_inc(vm_ready, 1)
                    pool.wait_ge(s0_in[h % 2], 16 * (h // 2 + 1))
                    if h:
                        pool.wait_ge(sn_store[0], 16 * h)
                    ends = blocks(eb[:, SEQ:TOK], DEC_T)[:, :, DEC_T - 1]
                    nc.gpsimd.tensor_tensor(sn[h % 2][:, :, :], s0[h % 2][:, :, :], bcast(ends, 2, [P, DEC_B, P]), ALU.mult)\
                        .then_inc(sn_scaled, 1)

            @block.tensor
            def _(pe):
                def begin(u):
                    if before[u] is not None:
                        pe.wait_ge(*evacuated[before[u]])
                    return k.ps[units[u][1]]

                def by_token(kind, i, w):
                    for t in range(NT):
                        bank = begin((kind, i, t))
                        for c in range(DC):
                            last = nc.tensor.matmul(bank[0:rows(t), :], k.xT[:, c, cols(t)], w[:, c, :],
                                                    start=(c == 0), stop=(c == DC - 1))
                        last.then_inc(proj_done, 1)

                def by_feature(h, w):
                    for kind, off in (("f", 2 * P), ("q", 0)):
                        bank = begin((kind, h))
                        for c in range(DC):
                            lhsT = w[:, c, off + (h % 2) * P:off + (h % 2) * P + P]
                            last = nc.tensor.matmul(bank[:, :], lhsT, k.xT[:, c, 0:SEQ], start=(c == 0), stop=(c == DC - 1))
                        last.then_inc(proj_done, 1)
                    bank = begin(("s", h))
                    for j, off in enumerate((2 * P, 0)):
                        for c in range(DC):
                            lhsT = w[:, c, off + (h % 2) * P:off + (h % 2) * P + P]
                            last = nc.tensor.matmul(bank[:, j * SMP:(j + 1) * SMP], lhsT, k.xT[:, c, SEQ:TOK],
                                                    start=(c == 0), stop=(c == DC - 1))
                    last.then_inc(proj_done, 1)

                def gla(h):
                    pe.wait_ge(v_out, 2 * NT)
                    pe.wait_ge(k_lev, (NLEV + 1) * (h + 1))
                    pe.wait_ge(q_lev, (NLEV + 2) * (h + 1))
                    if h:
                        pe.wait_ge(s_ready, PT * h)
                        pe.wait_ge(o_out, 2 * h)
                        pe.wait_ge(sn_ready, 2 * h)
                    for c in range(PT):
                        nc.tensor.transpose(k.ps[5][:, c * P:(c + 1) * P], kd[:, c * P:(c + 1) * P], k.ident[:, :])
                    nc.tensor.transpose(k.ps[6][0:SMP, P:2 * P], kd[:, SEQ:TOK], k.ident[:, :]).then_inc(turned, 1)
                    for i in range(NLEV):
                        if i >= 2:
                            pe.wait_ge(att_taken, (NLEV + 1) * h + i - 1)
                        for c in range(PT):
                            part = slice(c * P, (c + 1) * P)
                            last = nc.tensor.matmul(k.ps[3 + i % 2][:, part], KE[i][:, part], QE[i][:, part], start=True, stop=True)
                        last.then_inc(att_done, 1)
                    nc.tensor.matmul(k.ps[7][0:SMP, 0:SMP], KE[0][:, SEQ:TOK], QE[0][:, SEQ:TOK], start=True, stop=True)\
                        .then_inc(att_done, 1)
                    pe.wait_ge(turned_out, 2 * (h + 1))
                    for c in range(PT):
                        last = nc.tensor.matmul(k.ps[5][:, c * P:(c + 1) * P], kdT[:, c, :], v[:, c, head(h)], start=True, stop=True)
                    last.then_inc(ds_done, 1)
                    pe.wait_ge(att_taken, (NLEV + 1) * (h + 1))
                    pe.wait_ge(vm_ready, h + 1)
                    for i in range(2):
                        last = nc.tensor.matmul(k.ps[3 + i][:, :], kdTs[:, :], vm[:, 4 * i:4 * i + 4, :], start=True, stop=True)
                    last.then_inc(sds_done, 1)
                    pe.wait_ge(s_ready, PT * (h + 1))
                    for c in range(PT):
                        out = k.ps[7][:, c * P:(c + 1) * P]
                        nc.tensor.matmul(out, A[:, c, :], v[:, c, head(h)], start=True, stop=(c == 0))
                        if c:
                            nc.tensor.matmul(out, QS[:, c * P:(c + 1) * P], S[h % 2][:, c - 1, :], start=False, stop=True)
                    out = k.ps[6][0:SMP, 2 * P:3 * P]
                    nc.tensor.matmul(out, AS[:, :], v[0:SMP, PT, head(h)], start=True, stop=False)
                    pe.wait_ge(s0_in[h % 2], 16 * (h // 2 + 1))
                    for bb in range(DEC_B):
                        last = nc.tensor.matmul(out, QB[:, bb * SMP:(bb + 1) * SMP], s0[h % 2][:, bb, :], start=False,
                                                stop=(bb == DEC_B - 1))
                    last.then_inc(o_done, 1)

                for i in range(2):
                    w = k.take_weights(pe)
                    by_token("v", i, w)
                    k.w_done.append((proj_done, units[("v", i, NT - 1)][0]))
                for h in range(HEADS):
                    if h % 2 == 0:
                        w = k.take_weights(pe)
                    by_feature(h, w)
                    if h % 2 == 1:
                        k.w_done.append((proj_done, units[("s", h)][0]))
                    if h:
                        gla(h - 1)
                for i in range(2):
                    w = k.take_weights(pe)
                    by_token("g", i, w)
                    k.w_done.append((proj_done, units[("g", i, NT - 1)][0]))
                gla(HEADS - 1)

            def store(sp, h):
                sp.wait_ge(s_ready, PT * (h + 1))
                sp.dma_start(a["state_prompt"][0, 0, h, :, :], S[h % 2][:, PT - 1, :]).then_inc(s_store[0], 16)
                sp.wait_ge(sn_ready, 2 * (h + 1))
                sp.dma_start(a["state_sample"][0, :, h, :, :].rearrange("b k v -> k b v"), sn[h % 2][:, :, :])\
                    .then_inc(sn_store[0], 16)

            @block.sync
            def _(sp):
                for h in range(HEADS):
                    if h % 2 == 0 and h // 2 + 1 < HEADS // 2:
                        k.load_weights(sp, head_pair_halves(a, h // 2 + 1))
                    if h >= HEADS - 2:
                        k.load_weights(sp, column_halves(a["a_w_in"][0], 3 * D + (h + 2 - HEADS) * HB))
                    if h >= 2:
                        sp.wait_ge(sn_scaled, h - 1)
                        sp.wait_ge(o_done, h - 1)
                    sp.dma_start(s0[h % 2][:, :, :], a["state_hgrn"][0, :, h, :, :].rearrange("b k v -> k b v"))\
                        .then_inc(s0_in[h % 2], 16)
                    if h >= 1:
                        store(sp, h - 1)
                for i in range(2):
                    k.load_weights(sp, column_halves(a["a_w_o"][0], i * HB))
                store(sp, HEADS - 1)
                sp.wait_ge(s_store[0], 16 * HEADS)
                sp.wait_ge(sn_store[0], 16 * HEADS)



def mix_out_block(k, tag, o, gate, eps, prefetch=()):
    nc = k.nc
    squared, summed, mean = k.sem(f"{tag}_squared"), k.sem(f"{tag}_summed"), k.sem(f"{tag}_mean")
    seed, scaled, gated = k.sem(f"{tag}_seed"), k.sem(f"{tag}_scaled"), k.sem(f"{tag}_gated")
    turned, out_a, out_v = k.sem(f"{tag}_turned"), k.sem(f"{tag}_out_act"), k.sem(f"{tag}_out_dve")
    projected, added = k.sem(f"{tag}_projected"), k.sem(f"{tag}_added")
    half = DC // 2
    by_head = lambda ap: ap.rearrange("p (h n) -> p h n", n=P)
    with ExitStack() as tmp_ctx:
        def sb(name, shape):
            return tmp_ctx.enter_context(nc.sbuf_tensor(f"{tag}_{name}", shape, F32))
        sq = [sb(f"sq{i}", [P, D]) for i in range(2)]
        stats = sb("stats", [P, 5, NT, HEADS])
        flat = [stats[:, i, :, :].rearrange("p t h -> p (t h)") for i in range(5)]
        with nc.Block() as block:
            @block.scalar
            def _(act):
                for t in range(NT):
                    if t >= 2:
                        act.wait_ge(summed, t - 1)
                    nc.scalar.activation(sq[t % 2][:, :], o[:, t, :], ACT.Square).then_inc(squared, 1)
                act.wait_ge(mean, 1)
                nc.scalar.activation(flat[2], flat[1], ACT.Ln).then_inc(seed, 1)
                act.wait_ge(seed, 1)
                nc.scalar.activation(flat[3], flat[2], ACT.Exp, scale=-0.5).then_inc(seed, 1)
                for t in range(NT):
                    act.wait_ge(turned, t + 1)
                    src = k.ps[2 * (t % 2) + 1][:, :].rearrange("p (c n) -> p c n", c=half)[:, :, 0:rows(t)]
                    nc.scalar.activation(k.xT[:, half:DC, cols(t)], src, ACT.Copy).then_inc(out_a, 1)

            @block.vector
            def _(dve):
                ch = Chain(dve, k.order["vector"], k.order_n["vector"])
                for t in range(NT):
                    dve.wait_ge(squared, t + 1)
                    nc.vector.tensor_reduce(out=stats[:, 0, t, :], in_=by_head(sq[t % 2][:, :]), op=ALU.add, axis=AX.X)\
                        .then_inc(summed, 1)
                dve.wait_ge(summed, NT)
                nc.vector.tensor_scalar(flat[1], flat[0], 1.0 / P, eps, ALU.mult, ALU.add).then_inc(mean, 1)
                dve.wait_ge(mean, 1)
                inverse_root(dve, None, (seed, 2), ch, nc, flat[1], flat[3], flat[2], flat[4])
                for t in range(NT):
                    nc.vector.tensor_tensor(by_head(o[:, t, :]), by_head(o[:, t, :]),
                                            bcast(stats[:, 4, t, :], 2, [P, HEADS, P]), ALU.mult).then_inc(scaled, 1)
                for t in range(NT):
                    dve.wait_ge(turned, t + 1)
                    src = k.ps[2 * (t % 2)][:, :].rearrange("p (c n) -> p c n", c=half)[:, :, 0:rows(t)]
                    nc.vector.tensor_copy(k.xT[:, 0:half, cols(t)], src).then_inc(out_v, 1)
                for i in range(2):
                    for t in range(NT):
                        n = NT * i + t
                        dve.wait_ge(projected, n + 1)
                        part = k.h[0:rows(t), t, i * HB:(i + 1) * HB]
                        nc.vector.tensor_tensor(part, part, k.ps[4 + n % 4][0:rows(t), :], ALU.add).then_inc(added, 1)
                k.order_n["vector"] = ch.n

            @block.gpsimd
            def _(pool):
                for t in range(NT):
                    pool.wait_ge(scaled, t + 1)
                    nc.gpsimd.tensor_tensor(by_head(o[:, t, :]), by_head(o[:, t, :]), gate(t), ALU.mult).then_inc(gated, 1)

            @block.tensor
            def _(pe):
                for t in range(NT):
                    pe.wait_ge(gated, t + 1)
                    if t >= 2:
                        pe.wait_ge(out_v, t - 1)
                        pe.wait_ge(out_a, t - 1)
                    for c in range(DC):
                        last = nc.tensor.transpose(k.ps[2 * (t % 2) + c // half][:, (c % half) * P:(c % half) * P + rows(t)],
                                                   o[0:rows(t), t, c * P:(c + 1) * P], k.ident[0:rows(t), 0:rows(t)])
                    last.then_inc(turned, 1)
                for i in range(2):
                    w = k.take_weights(pe)
                    for t in range(NT):
                        n = NT * i + t
                        pe.wait_ge(out_v, t + 1)
                        pe.wait_ge(out_a, t + 1)
                        if n >= 4:
                            pe.wait_ge(added, n - 3)
                        for c in range(DC):
                            last = nc.tensor.matmul(k.ps[4 + n % 4][0:rows(t), :], k.xT[:, c, cols(t)], w[:, c, :],
                                                    start=(c == 0), stop=(c == DC - 1))
                        last.then_inc(projected, 1)
                    k.w_done.append((projected, NT * (i + 1)))

            if prefetch:
                @block.sync
                def _(sp):
                    for halves in prefetch:
                        k.load_weights(sp, halves)



def moe_blocks(k, a, layer, slots_x, slots_y, zeroed, prefetch):
    nc = k.nc
    tag = f"moe{layer}"
    with ExitStack() as tmp_ctx:
        def sb(name, shape, dt=F32):
            return tmp_ctx.enter_context(nc.sbuf_tensor(f"{tag}_{name}", shape, dt))

        expert = sb("expert", [P, 2 * BLOCKS])
        expert_i = sb("expert_i", [1, BLOCKS], I32)
        slot_i = sb("slot_i", [P, TOPK, NT], I32)
        gates = sb("gates", [P, TOPK, NT])
        column = k.cw[:, 3 + layer, :]
        with ExitStack() as route_ctx:
            xs = route_ctx.enter_context(nc.sbuf_tensor(f"{tag}_xs", [P, NT, D], F32))
            norm_block(k, f"{tag}n", [(column, k.xT)], xs)
            route_block(k, a, tag, layer, route_ctx, xs, slots_x, expert, expert_i, slot_i, gates, zeroed)
        expert_block(k, a, tag, layer, tmp_ctx, slots_x, slots_y, expert_i, column)
        combine_block(k, tag, tmp_ctx, slots_y, slot_i, gates, prefetch)


def route_block(k, a, tag, layer, ctx, xs, slots_x, expert, expert_i, slot_i, gates, zeroed):
    nc = k.nc

    def sb(name, shape, dt=F32):
        return ctx.enter_context(nc.sbuf_tensor(f"{tag}_{name}", shape, dt))

    E, G = EXPERTS, GROUPS
    wr = sb("router", [P, DC, G + E])
    tri, onesq = sb("tri", [P, P]), sb("onesq", [P, P])
    L = sb("logits", [P, NT, G + E])
    one = sb("one", [P, 3, NT, 4])
    work = sb("work", [P, 6, NT, E])
    hot = sb("hot", [P, TOPK, NT, E])
    both = sb("both", [P, NT, E])
    sc = sb("scalars", [P, 12, NT])
    counts = sb("counts", [P, 6, E])
    step_i, step = sb("step_i", [P, BLOCKS], I32), sb("step", [P, BLOCKS])
    big = sb("big", [P, BLOCKS, E])
    slot = sb("slot", [P, TOPK, NT])
    w_in, made, logit, copied = k.sem(f"{tag}_router_landed"), k.sem(f"{tag}_made"), k.sem(f"{tag}_logit"), k.sem(f"{tag}_copied")
    to_exp, exped, picked = k.sem(f"{tag}_to_exp"), k.sem(f"{tag}_exped"), k.sem(f"{tag}_picked")
    placed, slots_ready, sent = k.sem(f"{tag}_placed"), k.sem(f"{tag}_slots_ready"), k.sem(f"{tag}_sent")
    zero_sem, zero_value = zeroed
    flat = lambda ap: ap.rearrange("p t e -> p (t e)")
    with nc.Block() as block:
        @block.sync
        def _(sp):
            wv = lambda x: x.rearrange("(c p) n -> p c n", p=P)
            sp.dma_start(wr[:, :, 0:G], wv(a["moe_w_group"][layer])).then_inc(w_in, 16)
            for gg in range(G):
                sp.dma_start(wr[:, :, G + EPG * gg:G + EPG * (gg + 1)], wv(a["moe_w_sub"][layer, gg])).then_inc(w_in, 16)

        @block.gpsimd
        def _(pool):
            ch = Chain(pool, k.order["gpsimd"], k.order_n["gpsimd"])
            nc.gpsimd.memset(onesq[:, :], 1.0)
            ch(nc.gpsimd.memset(tri[:, :], 1.0))
            ch(nc.gpsimd.affine_select(out=tri[:, :], in_=tri[:, :], compare_op=ALU.is_gt, fill=0.0, base=0,
                                       pattern=[[1, P]], channel_multiplier=-1))
            nc.gpsimd.iota(step_i[:, :], pattern=[[1, BLOCKS]], base=0, channel_multiplier=0).then_inc(made, 1)
            pool.wait_ge(made, 1)
            nc.gpsimd.tensor_copy(step[:, :], step_i[:, :]).then_inc(made, 1)
            k.order_n["gpsimd"] = ch.n
            pool.wait_ge(slots_ready, 1)
            if zero_value:
                pool.wait_ge(zero_sem, zero_value)
            for j in range(TOPK):
                for t in range(NT):
                    pool.indirect_dma_start(slots_x, bass.IndirectOffsetOnAxis(ap=slot_i[0:rows(t), j, t:t + 1], axis=0),
                                            xs[0:rows(t), t, :], None).then_inc(sent, 16)
            pool.wait_ge(sent, 16 * TOPK * NT)

        @block.tensor
        def _(pe):
            pe.wait_ge(w_in, 16 * (1 + G))
            for t in range(NT):
                if t:
                    pe.wait_ge(copied, t)
                for c in range(DC):
                    last = nc.tensor.matmul(k.ps[0][0:rows(t), 0:G + E], k.xT[:, c, cols(t)], wr[:, c, :],
                                            start=(c == 0), stop=(c == DC - 1))
                last.then_inc(logit, 1)
            pe.wait_ge(picked, 1)
            pe.wait_ge(made, 2)
            for t in range(NT):
                for u in range(t + 1):
                    nc.tensor.matmul(k.ps[1][:, t * E:(t + 1) * E], (tri if u == t else onesq)[:, :], both[:, u, :],
                                     start=(u == 0), stop=(u == t))
            for u in range(NT):
                last = nc.tensor.matmul(k.ps[1][:, NT * E:(NT + 1) * E], onesq[:, :], both[:, u, :], start=(u == 0),
                                        stop=(u == NT - 1))
            last.then_inc(placed, 1)

        @block.scalar
        def _(act):
            act.wait_ge(to_exp, 1)
            nc.scalar.activation(work[:, 0, :, 0:G], work[:, 0, :, 0:G], ACT.Exp).then_inc(exped, 1)
            act.wait_ge(to_exp, 2)
            nc.scalar.activation(sc[:, 4, :], sc[:, 4, :], ACT.Exp).then_inc(exped, 1)

        @block.vector
        def _(dve):
            ch = Chain(dve, k.order["vector"], k.order_n["vector"])
            TT, TS = nc.vector.tensor_tensor, nc.vector.tensor_scalar
            full = lambda ap: bcast(ap, 2, [P, NT, 4])
            ch(nc.vector.memset(L[:, :, :], 0.0))
            for t in range(NT):
                dve.wait_ge(logit, t + 1)
                nc.vector.tensor_copy(L[0:rows(t), t, :], k.ps[0][0:rows(t), 0:G + E]).then_inc(copied, 1)
            dve.wait_ge(copied, NT)

            def first_largest(values, top, out, room):
                ch(nc.vector.tensor_reduce(out=top, in_=values, op=ALU.max, axis=AX.X))
                ch(TT(out, values, full(top), ALU.is_equal))
                ch(nc.vector.tensor_copy(room, out[:, :, 0]))
                for e in range(1, 4):
                    ch(TT(sc[:, 11, :], out[:, :, e], room, ALU.mult))
                    ch(TT(out[:, :, e], out[:, :, e], sc[:, 11, :], ALU.subtract))
                    ch(TT(room, room, out[:, :, e], ALU.add))

            first_largest(L[:, :, 0:G], sc[:, 0, :], one[:, 0, :, :], sc[:, 10, :])
            TT(work[:, 0, :, 0:G], L[:, :, 0:G], full(sc[:, 0, :]), ALU.subtract).then_inc(to_exp, 1)
            ch(TT(work[:, 1, :, :].rearrange("p t (g e) -> p t g e", g=G), L[:, :, G:G + E].rearrange("p t (g e) -> p t g e", g=G),
                  bcast(one[:, 0, :, :], 3, [P, NT, G, EPG]), ALU.mult))
            ch(nc.vector.tensor_reduce(out=work[:, 2, :, 0:EPG], in_=work[:, 1, :, :].rearrange("p t (g e) -> p t e g", g=G),
                                       op=ALU.add, axis=AX.X))
            first_largest(work[:, 2, :, 0:EPG], sc[:, 1, :], one[:, 1, :, :], sc[:, 10, :])
            ch(nc.vector.scalar_tensor_tensor(out=work[:, 3, :, 0:EPG], in0=one[:, 1, :, :], scalar=-3e38,
                                              in1=work[:, 2, :, 0:EPG], op0=ALU.mult, op1=ALU.add))
            first_largest(work[:, 3, :, 0:EPG], sc[:, 2, :], one[:, 2, :, :], sc[:, 10, :])
            TT(sc[:, 4, :], sc[:, 2, :], sc[:, 1, :], ALU.subtract).then_inc(to_exp, 1)
            for j in range(TOPK):
                ch(TT(hot[:, j, :, :].rearrange("p t (g e) -> p t g e", g=G), bcast(one[:, 0, :, :], 3, [P, NT, G, EPG]),
                      bcast(one[:, 1 + j, :, :], 2, [P, NT, G, EPG]), ALU.mult))
            ch(TT(both[:, :, :], hot[:, 0, :, :], hot[:, 1, :, :], ALU.add))
            for q in range(1, 4):
                ch(nc.vector.memset(both[32 * q:32 * q + 32, PT, :], 0.0))
            dve.sem_inc(picked, 1)
            dve.wait_ge(exped, 2)
            ch(nc.vector.tensor_reduce(out=sc[:, 3, :], in_=work[:, 0, :, 0:G], op=ALU.add, axis=AX.X))
            ch(TS(sc[:, 5, :], sc[:, 4, :], 1.0, None, ALU.add))
            ch(TT(sc[:, 5, :], sc[:, 5, :], sc[:, 3, :], ALU.mult))
            ch(nc.vector.reciprocal(gates[:, 0, :], sc[:, 5, :]))
            ch(TT(gates[:, 1, :], gates[:, 0, :], sc[:, 4, :], ALU.mult))
            dve.wait_ge(placed, 1)
            cnt = k.ps[1][:, NT * E:(NT + 1) * E]
            nthr = (TOK + P - 1) // P
            ch(TS(counts[:, 0, :], cnt, 0.0, None, ALU.is_gt))
            for i in range(1, nthr):
                ch(nc.vector.scalar_tensor_tensor(out=counts[:, 0, :], in0=cnt, scalar=float(i * P), in1=counts[:, 0, :],
                                                  op0=ALU.is_gt, op1=ALU.add))
            ch(TS(counts[:, 1, :], counts[:, 0, :], 0.0, 1.0, ALU.mult, ALU.add))
            ch(nc.vector.tensor_tensor_scan(counts[:, 2, :], counts[:, 1, :], counts[:, 0, :], 0.0, ALU.mult, ALU.add))
            ch(TT(counts[:, 3, :], counts[:, 2, :], counts[:, 0, :], ALU.subtract))
            ch(nc.vector.scalar_tensor_tensor(out=work[:, 4, :, :], in0=bcast(counts[:, 3, :], 1, [P, NT, E]), scalar=float(P),
                                              in1=k.ps[1][:, 0:NT * E].rearrange("p (t e) -> p t e", e=E),
                                              op0=ALU.mult, op1=ALU.add))
            for j in range(TOPK):
                ch(TT(work[:, 5, :, :], work[:, 4, :, :], hot[:, j, :, :], ALU.mult))
                ch(nc.vector.tensor_reduce(out=slot[:, j, :], in_=work[:, 5, :, :], op=ALU.add, axis=AX.X))
            ch(nc.vector.tensor_copy(slot_i[:, :, :], slot[:, :, :]))
            dve.sem_inc(slots_ready, 1)
            ch(TT(big[:, :, :], bcast(counts[:, 2, :], 1, [P, BLOCKS, E]), bcast(step[:, :], 2, [P, BLOCKS, E]), ALU.is_le))
            ch(nc.vector.tensor_reduce(out=expert[:, 0:BLOCKS], in_=big[:, :, :], op=ALU.add, axis=AX.X))
            ch(TS(expert[:, 0:BLOCKS], expert[:, 0:BLOCKS], float(E - 1), None, ALU.min))
            ch(nc.vector.tensor_copy(expert_i[:, :], expert[0:1, 0:BLOCKS]))
            k.order_n["vector"] = ch.n


def expert_block(k, a, tag, layer, ctx, slots_x, slots_y, expert_i, column):
    nc = k.nc

    def sb(name, shape, dt=F32):
        return ctx.enter_context(nc.sbuf_tensor(f"{tag}_{name}", shape, dt))

    NB = 2
    FC = FF // P
    half = DC // 2
    X = [sb(f"x{i}", [P, D]) for i in range(NB)]
    WGU = [sb(f"wgu{i}", [P, 2, DC, FF]) for i in range(NB)]
    WD = [sb(f"wd{i}", [P, FC, D]) for i in range(NB)]
    XT = [sb(f"xt{i}", [P, DC, P]) for i in range(NB)]
    SG = [sb(f"sg{i}", [P, FF]) for i in range(NB)]
    HT = [sb(f"ht{i}", [P, FC, P]) for i in range(NB)]
    Y = [sb(f"y{i}", [P, D]) for i in range(NB)]
    x_in = [k.sem(f"{tag}_x_landed{i}") for i in range(NB)]
    gu_in = [k.sem(f"{tag}_gu_landed{i}") for i in range(NB)]
    d_in = [k.sem(f"{tag}_down_landed{i}") for i in range(NB)]
    y_out = [k.sem(f"{tag}_y_stored{i}") for i in range(NB)]
    x_turned, xt_a, xt_v = k.sem(f"{tag}_x_turned"), k.sem(f"{tag}_xt_act"), k.sem(f"{tag}_xt_dve")
    gu_done, silu_done, hid_done = k.sem(f"{tag}_gu_done"), k.sem(f"{tag}_silu_done"), k.sem(f"{tag}_hid_done")
    h_turned, ht_done = k.sem(f"{tag}_h_turned"), k.sem(f"{tag}_ht_done")
    down_done, y_a, y_v = k.sem(f"{tag}_down_done"), k.sem(f"{tag}_y_act"), k.sem(f"{tag}_y_dve")
    LOOP = (1, (BLOCKS - 2) // 2)
    assert BLOCKS % 2 == 0 and BLOCKS >= 6

    def wait(eng, sem, value):
        if not isinstance(value, int) or value > 0:
            eng.wait_ge(sem, value)

    with nc.Block() as block:
        @block.sync
        def _(sp):
            def load(i, c):
                j, u = 2 * i + c, c % 2
                e = sp.value_load(expert_i[0:1, bass.ds(j, 1)], min_val=0, max_val=EXPERTS - 1)
                wait(sp, x_turned, j - 1)
                sp.dma_start(X[u][:, :], slots_x[bass.ds(j * P, P), :]).then_inc(x_in[u], 16)
                wait(sp, gu_done, j - 1)
                for n, w in enumerate((a["moe_w_gate"], a["moe_w_up"])):
                    sp.dma_start(WGU[u][:, n, :, :], w[layer, bass.ds(e, 1), :, :].rearrange("a (c p) f -> p (a c) f", p=P))\
                        .then_inc(gu_in[u], 16)
                wait(sp, down_done, j - 1)
                sp.dma_start(WD[u][:, :, :], a["moe_w_down"][layer, bass.ds(e, 1), :, :].rearrange("a (c p) n -> p (a c) n", p=P))\
                    .then_inc(d_in[u], 16)

            load(0, 0)
            load(0, 1)
            with sp.Fori(1, BLOCKS // 2) as i:
                load(i, 0)
                load(i, 1)

        @block.scalar
        def _(act):
            def turn_out(i, c):
                j, u = 2 * i + c, c % 2
                act.wait_ge(x_turned, j + 1)
                for n in range(half, DC):
                    nc.scalar.activation(XT[u][:, n, :], k.ps[1][:, (n - half) * P:(n - half + 1) * P], ACT.Copy,
                                         scale=column[:, n:n + 1]).then_inc(xt_a, 1)

            def silu(i, c):
                j, u = 2 * i + c, c % 2
                act.wait_ge(gu_done, j + 1)
                wait(act, h_turned, j - 1)
                nc.scalar.activation(SG[u][:, :], k.ps[2 + u][:, 0:FF], ACT.Silu).then_inc(silu_done, 1)

            def y_store(i, c):
                j, u = 2 * i + c, c % 2
                act.wait_ge(down_done, j + 1)
                wait(act, y_out[u], 16 * (i + c // 2))
                nc.scalar.activation(Y[u][:, HB:D], k.ps[6][:, :], ACT.Copy).then_inc(y_a, 1)
                act.wait_ge(y_v, j + 1)
                act.wait_ge(y_a, j + 1)
                act.dma_start(slots_y[bass.ds(j * P, P), :], Y[u][:, :]).then_inc(y_out[u], 16)

            def step(i, c):
                silu(i, c)
                if not (isinstance(i, int) and 2 * i + c == BLOCKS - 1):
                    turn_out(i, c + 1)
                if not (isinstance(i, int) and 2 * i + c == 0):
                    y_store(i, c - 1)

            turn_out(0, 0)
            for c in range(3):
                step(0, c)
            with act.Fori(*LOOP) as i:
                step(i, 1)
                step(i, 2)
            step((BLOCKS - 1) // 2, 1)
            y_store((BLOCKS - 1) // 2, 1)
            for u in range(2):
                act.wait_ge(y_out[u], 16 * BLOCKS // 2)

        @block.vector
        def _(dve):
            def turn_out(i, c):
                j, u = 2 * i + c, c % 2
                dve.wait_ge(x_turned, j + 1)
                nc.vector.tensor_tensor(XT[u][:, 0:half, :], k.ps[0][:, :].rearrange("p (c n) -> p c n", c=half),
                                        bcast(column[:, 0:half], 2, [P, half, P]), ALU.mult).then_inc(xt_v, 1)

            def times_up(i, c):
                j, u = 2 * i + c, c % 2
                dve.wait_ge(silu_done, j + 1)
                nc.vector.tensor_tensor(SG[u][:, :], SG[u][:, :], k.ps[2 + u][:, FF:2 * FF], ALU.mult).then_inc(hid_done, 1)

            def y_half(i, c):
                j, u = 2 * i + c, c % 2
                dve.wait_ge(down_done, j + 1)
                wait(dve, y_out[u], 16 * (i + c // 2))
                nc.vector.tensor_copy(Y[u][:, 0:HB], k.ps[5][:, :]).then_inc(y_v, 1)

            def hidden_out(i, c):
                j, u = 2 * i + c, c % 2
                dve.wait_ge(h_turned, j + 1)
                nc.vector.tensor_copy(HT[u][:, :, :], k.ps[4][:, 0:FF].rearrange("p (c n) -> p c n", c=FC)).then_inc(ht_done, 1)

            def step(i, c):
                if not (isinstance(i, int) and 2 * i + c == BLOCKS - 1):
                    turn_out(i, c + 1)
                times_up(i, c)
                if not (isinstance(i, int) and 2 * i + c == 0):
                    y_half(i, c - 1)
                hidden_out(i, c)

            turn_out(0, 0)
            for c in range(3):
                step(0, c)
            with dve.Fori(*LOOP) as i:
                step(i, 1)
                step(i, 2)
            step((BLOCKS - 1) // 2, 1)
            y_half((BLOCKS - 1) // 2, 1)

        @block.tensor
        def _(pe):
            def turn_x(i, c):
                j, u = 2 * i + c, c % 2
                pe.wait_ge(x_in[u], 16 * (i + c // 2 + 1))
                wait(pe, xt_a, half * j)
                wait(pe, xt_v, j)
                for n in range(DC):
                    last = nc.tensor.transpose(k.ps[n // half][:, (n % half) * P:(n % half + 1) * P],
                                               X[u][:, n * P:(n + 1) * P], k.ident[:, :])
                last.then_inc(x_turned, 1)

            def gate_up(i, c):
                j, u = 2 * i + c, c % 2
                pe.wait_ge(gu_in[u], 32 * (i + c // 2 + 1))
                pe.wait_ge(xt_a, half * (j + 1))
                pe.wait_ge(xt_v, j + 1)
                wait(pe, hid_done, j - 1)
                for n in range(DC):
                    last = nc.tensor.matmul(k.ps[2 + u][:, :].rearrange("p (w f) -> p w f", w=2), XT[u][:, n, :],
                                            WGU[u][:, :, n, :], start=(n == 0), stop=(n == DC - 1))
                last.then_inc(gu_done, 1)

            def down(i, c):
                j, u = 2 * i + c, c % 2
                pe.wait_ge(d_in[u], 16 * (i + c // 2 + 1))
                pe.wait_ge(ht_done, j + 1)
                wait(pe, y_a, j)
                wait(pe, y_v, j)
                for b in range(2):
                    for n in range(FC):
                        last = nc.tensor.matmul(k.ps[5 + b][:, :], HT[u][:, n, :], WD[u][:, n, b * HB:(b + 1) * HB],
                                                start=(n == 0), stop=(n == FC - 1))
                last.then_inc(down_done, 1)

            def turn_hidden(i, c):
                j, u = 2 * i + c, c % 2
                pe.wait_ge(hid_done, j + 1)
                wait(pe, ht_done, j)
                for n in range(FC):
                    last = nc.tensor.transpose(k.ps[4][:, n * P:(n + 1) * P], SG[u][:, n * P:(n + 1) * P], k.ident[:, :])
                last.then_inc(h_turned, 1)

            def step(i, c):
                gate_up(i, c)
                if not (isinstance(i, int) and 2 * i + c == BLOCKS - 1):
                    turn_x(i, c + 1)
                if not (isinstance(i, int) and 2 * i + c == 0):
                    down(i, c - 1)
                turn_hidden(i, c)

            turn_x(0, 0)
            for c in range(3):
                step(0, c)
            with pe.Fori(*LOOP) as i:
                step(i, 1)
                step(i, 2)
            step((BLOCKS - 1) // 2, 1)
            down((BLOCKS - 1) // 2, 1)


def combine_block(k, tag, ctx, slots_y, slot_i, gates, prefetch):
    nc = k.nc
    rows_in = [ctx.enter_context(nc.sbuf_tensor(f"{tag}_gathered{i}", [P, D], F32)) for i in range(4)]
    landed = [k.sem(f"{tag}_gathered{i}") for i in range(4)]
    added = k.sem(f"{tag}_added")
    with nc.Block() as block:
        @block.sync
        def _(sp):
            for halves in prefetch:
                k.load_weights(sp, halves)

        @block.gpsimd
        def _(pool):
            for t in range(NT):
                for j in range(TOPK):
                    n = TOPK * t + j
                    if n >= 4:
                        pool.wait_ge(added, n - 3)
                    pool.indirect_dma_start(rows_in[n % 4][0:rows(t), :], None, slots_y,
                                            bass.IndirectOffsetOnAxis(ap=slot_i[0:rows(t), j, t:t + 1], axis=0))\
                        .then_inc(landed[n % 4], 16)

        @block.vector
        def _(dve):
            for t in range(NT):
                for j in range(TOPK):
                    n = TOPK * t + j
                    dve.wait_ge(landed[n % 4], 16 * (n // 4 + 1))
                    if n:
                        dve.wait_ge(added, n)
                    part = k.h[0:rows(t), t, :]
                    nc.vector.scalar_tensor_tensor(out=part, in0=rows_in[n % 4][0:rows(t), :], scalar=gates[0:rows(t), j, t:t + 1],
                                                   in1=part, op0=ALU.mult, op1=ALU.add).then_inc(added, 1)



def kvq_block(k, a, kv_xT, q_xT, ks, v, kT, qT, o):
    nc = k.nc
    done, out_v, out_a = k.sem("kvq_done"), k.sem("kvq_out_dve"), k.sem("kvq_out_act")
    turned, kt_out = k.sem("kT_turned"), k.sem("kT_out")
    stored = k.sem("kv_stored")
    order = [("k", i, t) for i in range(2) for t in range(NT)]
    for h in range(HEADS):
        order += [("q", h, 0), ("q", h, 1)]
    order += [("v", i, t) for i in range(2) for t in range(NT)]
    count = {u: n + 1 for n, u in enumerate(order)}
    nv, na, outs = 0, 0, {}
    for u in order:
        if u[0] == "q":
            na += 2
            outs[u] = (out_a, na)
        else:
            nv += 1
            outs[u] = (out_v, nv)
    bank_of, before, last_in, n = {}, {}, {}, 0
    for u in order:
        if u[0] == "q":
            bank_of[u] = 4 if u[2] else 2 + u[1] % 2
        else:
            bank_of[u] = n % 2
            n += 1
        before[u] = last_in.get(bank_of[u])
        last_in[bank_of[u]] = u
    with nc.Block() as block:
        @block.tensor
        def _(pe):
            def begin(u):
                if before[u] is not None:
                    pe.wait_ge(*outs[before[u]])
                return k.ps[bank_of[u]]

            def by_token(kind):
                for i in range(2):
                    w = k.take_weights(pe)
                    for t in range(NT):
                        bank = begin((kind, i, t))
                        for c in range(DC):
                            last = nc.tensor.matmul(bank[0:rows(t), :], kv_xT[:, c, cols(t)], w[:, c, :],
                                                    start=(c == 0), stop=(c == DC - 1))
                        last.then_inc(done, 1)
                    k.w_done.append((done, count[(kind, i, NT - 1)]))

            by_token("k")
            for h in range(HEADS):
                if h % 4 == 0:
                    w = k.take_weights(pe)
                for part, (lo, hi) in enumerate(((0, SEQ), (SEQ, TOK))):
                    bank = begin(("q", h, part))
                    for c in range(DC):
                        last = nc.tensor.matmul(bank[:, 0:hi - lo], w[:, c, (h % 4) * P:(h % 4 + 1) * P], q_xT[:, c, lo:hi],
                                                start=(c == 0), stop=(c == DC - 1))
                    last.then_inc(done, 1)
                if h % 4 == 3:
                    k.w_done.append((done, count[("q", h, 1)]))
            pe.wait_ge(out_v, 2 * NT)
            for h in range(HEADS):
                if h:
                    pe.wait_ge(kt_out, 2 * h)
                for t in range(PT):
                    nc.tensor.transpose(k.ps[5][:, t * P:(t + 1) * P], ks[:, t, h * P:(h + 1) * P], k.ident[:, :])
                nc.tensor.transpose(k.ps[6][:, 0:SMP], ks[0:SMP, PT, h * P:(h + 1) * P], k.ident[0:SMP, 0:SMP]).then_inc(turned, 1)
            by_token("v")

        @block.sync
        def _(sp):
            for i in range(1, 2):
                k.load_weights(sp, column_halves(a["b_w_q"][0], i * HB))
            k.load_weights(sp, column_halves(a["w_kv"], D))
            k.load_weights(sp, column_halves(a["w_kv"], D + HB))

            def store(src, prompt, sample):
                sp.dma_start(a[prompt][0].rearrange("(t p) h n -> p t (h n)", p=P), src[:, 0:PT, :]).then_inc(stored, 16)
                sp.dma_start(a[sample].rearrange("b t h n -> (b t) (h n)"), src[0:SMP, PT, :]).then_inc(stored, 16)

            sp.wait_ge(out_v, 2 * NT)
            store(ks, "k_prompt", "k_sample")
            for i in range(2):
                k.load_weights(sp, column_halves(a["b_w_o"][0], i * HB))
            sp.wait_ge(out_v, 4 * NT)
            store(v, "v_prompt", "v_sample")
            sp.wait_ge(stored, 64)

        @block.vector
        def _(dve):
            for q in range(1, 4):
                nc.vector.memset(o[32 * q:32 * q + 32, PT, :], 0.0)
            for c in range(2):
                nc.vector.memset(qT[1 - c][c * P // 2:(c + 1) * P // 2, :, :], 0.0)
            for kind, dst in (("k", ks), ("v", v)):
                for i in range(2):
                    for t in range(NT):
                        dve.wait_ge(done, count[(kind, i, t)])
                        nc.vector.tensor_copy(dst[0:rows(t), t, i * HB:(i + 1) * HB], k.ps[bank_of[(kind, i, t)]][0:rows(t), :])\
                            .then_inc(out_v, 1)

        @block.scalar
        def _(act):
            for h in range(HEADS):
                for part, (lo, hi) in enumerate(((0, SEQ), (SEQ, TOK))):
                    act.wait_ge(done, count[("q", h, part)])
                    for c in range(2):
                        rows_c = slice(c * P // 2, (c + 1) * P // 2)
                        nc.scalar.activation(qT[c][rows_c, h, lo:hi], k.ps[bank_of[("q", h, part)]][rows_c, 0:hi - lo], ACT.Copy,
                                             scale=0.125).then_inc(out_a, 1)
            for h in range(HEADS):
                act.wait_ge(turned, h + 1)
                nc.scalar.activation(kT[:, h, 0:SEQ], k.ps[5][:, :], ACT.Copy).then_inc(kt_out, 1)
                nc.scalar.activation(kT[:, h, SEQ:TOK], k.ps[6][:, 0:SMP], ACT.Copy).then_inc(kt_out, 1)



def prompt_attention(k, a, rep, v, kT, qT, qz, kTs, o):
    nc = k.nc
    units = [(h, i) for h in range(HEADS) for i in range(PT)]
    N = len(units)
    half = P // 2
    with ExitStack() as tmp_ctx:
        def sb(name, shape):
            return tmp_ctx.enter_context(nc.sbuf_tensor(name, shape, F32))
        dist = sb("pa_dist", [P, SEQ])
        bias = [sb(f"pa_bias{i}", [P, SEQ]) for i in range(2)]
        S = [sb(f"pa_s{i}", [P, 2, SEQ]) for i in range(2)]
        aT = [sb(f"pa_at{i}", [P, PT, P]) for i in range(2)]
        st = [sb(f"pa_stat{i}", [P, 10]) for i in range(2)]
        d_in, bias_ready = k.sem("pa_dist_landed"), k.sem("pa_bias")
        scored, biased, negated, exped = k.sem("pa_scored"), k.sem("pa_biased"), k.sem("pa_negated"), k.sem("pa_exp")
        combined, turned, at_out, o_done, o_out = (k.sem(f"pa_{n}") for n in ("combined", "turned", "at_out", "o_done", "o_out"))
        with nc.Block() as block:
            @block.sync
            def _(sp):
                sp.dma_start(dist[:, :], a["const_dist"]).then_inc(d_in, 16)

            @block.gpsimd
            def _(pool):
                pool.wait_ge(d_in, 16)
                for h in range(HEADS):
                    if h >= 2:
                        pool.wait_ge(biased, 2 * PT * (h - 1))
                    nc.gpsimd.tensor_scalar(bias[h % 2][:, :], dist[:, :], -(2.0 ** -(h + 1)), None, ALU.mult).then_inc(bias_ready, 1)

            @block.tensor
            def _(pe):
                def scores(n):
                    h, i = units[n]
                    w = (i + 1) * P
                    if n >= 2:
                        pe.wait_ge(biased, 2 * (n - 1))
                    for c in range(2):
                        last = nc.tensor.matmul(k.ps[2 * (n % 2) + c][:, 0:w], qT[c][:, h, i * P:(i + 1) * P], kT[:, h, 0:w],
                                                start=True, stop=True)
                        last.then_inc(scored, 1)

                def values(n):
                    h, i = units[n]
                    pe.wait_ge(combined, n + 1)
                    if n >= 2:
                        pe.wait_ge(at_out, n - 1)
                    for j in range(i + 1):
                        last = nc.tensor.transpose(k.ps[4 + n % 2][:, j * P:(j + 1) * P], S[n % 2][:, 0, j * P:(j + 1) * P], k.ident[:, :])
                    last.then_inc(turned, 1)
                    pe.wait_ge(at_out, n + 1)
                    if n >= 2:
                        pe.wait_ge(o_out, n - 1)
                    for j in range(i + 1):
                        last = nc.tensor.matmul(k.ps[6 + n % 2][:, 0:P], aT[n % 2][:, j, :], v[:, j, h * P:(h + 1) * P],
                                                start=(j == 0), stop=(j == i))
                    last.then_inc(o_done, 1)

                scores(0)
                for n in range(N):
                    if n + 1 < N:
                        scores(n + 1)
                    values(n)

            @block.vector
            def _(dve):
                ch = Chain(dve, k.order["vector"], k.order_n["vector"])
                ch(nc.vector.memset(qz[:, :, :, :], 0.0))
                for c in range(2):
                    part = slice(c * half, (c + 1) * half)
                    ch(nc.vector.tensor_copy(qz[part, :, :, c * DEC_T:(c + 1) * DEC_T],
                                             qT[c][part, :, SEQ:TOK].rearrange("p h (b t) -> p b h t", t=DEC_T)))
                ch(nc.vector.tensor_copy(kTs[:, :, :], kT[:, :, SEQ:TOK]))

                def bias_max(n):
                    h, i = units[n]
                    w = (i + 1) * P
                    dve.wait_ge(bias_ready, h + 1)
                    if n >= 2:
                        dve.wait_ge(turned, n - 1)
                    for c in range(2):
                        dve.wait_ge(scored, 2 * n + c + 1)
                        nc.vector.tensor_tensor_reduce(out=S[n % 2][:, c, 0:w], in0=k.ps[2 * (n % 2) + c][:, 0:w],
                                                       in1=bias[h % 2][:, (PT - 1 - i) * P:SEQ], scale=1.0, scalar=-3e38,
                                                       op0=ALU.add, op1=ALU.max,
                                                       accum_out=st[n % 2][:, c:c + 1]).then_inc(biased, 1)
                    dve.wait_ge(biased, 2 * (n + 1))
                    nc.vector.tensor_scalar(st[n % 2][:, 2:4], st[n % 2][:, 0:2], -1.0, None, ALU.mult).then_inc(negated, 1)

                def combine(n):
                    h, i = units[n]
                    w = (i + 1) * P
                    s = st[n % 2]
                    dve.wait_ge(exped, 2 * (n + 1))
                    ch(nc.vector.reciprocal(s[:, 6:8], s[:, 4:6]))
                    ch(nc.vector.tensor_tensor(s[:, 8:9], s[:, 7:8], rep[:, 2 * P:2 * P + 1], ALU.mult))
                    ch(nc.vector.tensor_scalar(S[n % 2][:, 1, 0:w], S[n % 2][:, 1, 0:w], s[:, 8:9], None, ALU.mult))
                    nc.vector.scalar_tensor_tensor(out=S[n % 2][:, 0, 0:w], in0=S[n % 2][:, 0, 0:w], scalar=s[:, 6:7],
                                                   in1=S[n % 2][:, 1, 0:w], op0=ALU.mult, op1=ALU.add).then_inc(combined, 1)

                bias_max(0)
                for n in range(N):
                    if n + 1 < N:
                        bias_max(n + 1)
                    combine(n)
                k.order_n["vector"] = ch.n

            @block.scalar
            def _(act):
                def exps(n):
                    h, i = units[n]
                    w = (i + 1) * P
                    act.wait_ge(negated, n + 1)
                    for c in range(2):
                        nc.scalar.activation(S[n % 2][:, c, 0:w], S[n % 2][:, c, 0:w], ACT.Exp, bias=st[n % 2][:, 2 + c:3 + c],
                                             accum_out=st[n % 2][:, 4 + c:5 + c]).then_inc(exped, 1)

                def outs(n):
                    h, i = units[n]
                    act.wait_ge(turned, n + 1)
                    nc.scalar.activation(aT[n % 2][:, 0:i + 1, :], k.ps[4 + n % 2][:, 0:(i + 1) * P].rearrange("p (j n) -> p j n", n=P),
                                         ACT.Copy).then_inc(at_out, 1)
                    act.wait_ge(o_done, n + 1)
                    nc.scalar.activation(o[:, i, h * P:(h + 1) * P], k.ps[6 + n % 2][:, 0:P], ACT.Copy).then_inc(o_out, 1)

                exps(0)
                for n in range(N):
                    if n + 1 < N:
                        exps(n + 1)
                    outs(n)



def sample_attention(k, a, rep, qz, kTs, o):
    nc = k.nc
    HT = HEADS * DEC_T
    QUAD = 32
    KRING, VRING, GROUP = 4, 8, 4
    GROUPS_ = PAGES // GROUP
    KEYS = PAST + DEC_T
    N5 = GROUPS_ + 1
    half = HEADS // 2
    with ExitStack() as tmp_ctx:
        def sb(name, shape, dt=F32):
            return tmp_ctx.enter_context(nc.sbuf_tensor(name, shape, dt))
        pt = sb("sa_pages", [1, DEC_B * PAGES], I32)
        K = k.wring[k.w_issued % WEIGHT_SLOTS][:, :, :].rearrange("p (r c) n -> p r (c n)", r=KRING)
        V = [sb(f"sa_v{i}", [P, D]) for i in range(VRING)]
        KT = sb("sa_kT", [P, HEADS, GROUP * P])
        S = sb("sa_scores", [P, KEYS])
        W = sb("sa_w", [P, KEYS])
        alibi = sb("sa_alibi", [P, KEYS])
        table = sb("sa_table", [P, 2 + HEADS + DEC_B * SMP])
        red = sb("sa_red", [P, 16])
        AT = sb("sa_at", [P, PAGES + 1, HT])
        Q = sb("sa_q", [P, HEADS, QUAD])
        knew, vnew = sb("sa_knew", [P, HEADS, DEC_T]), sb("sa_vnew", [P, D])
        place = sb("sa_place", [P, SMP])
        own = sb("sa_own", [P, D])
        own_head = table[:, 2:2 + HEADS]
        places = table[:, 2 + HEADS:].rearrange("p (b n) -> p b n", b=DEC_B)
        c_in = k.sem("sa_const_landed")
        k_in, v_in = [k.sem(f"sa_k_landed{i}") for i in range(KRING)], [k.sem(f"sa_v_landed{i}") for i in range(VRING)]
        vn_in = k.sem("sa_vnew_landed")
        names = ("cleared", "turned_a", "turned_b", "kt_out_a", "kt_out_b", "q_ready", "scored", "biased", "max_ready",
                 "exped", "normed", "w_turned", "at_out", "valued", "picked", "place_ready", "summed", "added")
        (cleared, turned_a, turned_b, kt_out_a, kt_out_b, q_ready, scored, biased, max_ready, exped, normed, w_turned,
         at_out, valued, picked, place_ready, summed, added) = (k.sem(f"sa_{n}") for n in names)

        def wait(eng, sem, value):
            if not isinstance(value, int) or value > 0:
                eng.wait_ge(sem, value)

        with nc.Block() as block:
            @block.sync
            def _(sp):
                sp.dma_start(pt[:, :], a["page_table"].rearrange("(x b) n -> x (b n)", x=1)).then_inc(c_in, 16)
                sp.dma_start(alibi[:, :], a["const_rows"][:, 0:KEYS]).then_inc(c_in, 16)
                sp.dma_start(table[:, :], a["const_rows"][:, KEYS:]).then_inc(c_in, 16)
                sp.wait_ge(c_in, 48)
                sp.wait_ge(cleared, 3)

                def load_k(b, p):
                    page = sp.value_load(pt[0:1, bass.ds(b * PAGES + p, 1)], min_val=0, max_val=a["cache_k"].shape[0] - 1)
                    wait(sp, turned_b, PAGES * b + p - KRING + 1)
                    sp.dma_start(K[:, p % KRING, :], a["cache_k"][bass.ds(page, 1), :, :, :].rearrange("a p h n -> (a p) (h n)"))\
                        .then_inc(k_in[p % KRING], 16)

                def load_v(b, g, valued_before):
                    for p in range(GROUP * g, GROUP * (g + 1)):
                        page = sp.value_load(pt[0:1, bass.ds(b * PAGES + p, 1)], min_val=0, max_val=a["cache_k"].shape[0] - 1)
                        wait(sp, valued, valued_before)
                        sp.dma_start(V[p % VRING][:, :], a["cache_v"][bass.ds(page, 1), :, :, :].rearrange("a p h n -> (a p) (h n)"))\
                            .then_inc(v_in[p % VRING], 16)

                def iteration(b, scores, values):
                    for g in range(GROUPS_):
                        if scores:
                            for p in range(GROUP * g, GROUP * (g + 1)):
                                load_k(b, p)
                        if values and g < GROUPS_ - 1:
                            load_v(b - 1, g + 1, N5 * (b - 1) + g)
                        if scores and g == GROUPS_ - 1:
                            load_v(b, 0, N5 * (b - 1) + g)
                        if values and g == 1:
                            wait(sp, valued, N5 * (b - 1))
                            sp.dma_start(vnew[0:DEC_T, :], a["v_sample"][bass.ds(b - 1, 1), :, :, :].rearrange("a t h n -> (a t) (h n)"))\
                                .then_inc(vn_in, 16)

                iteration(0, True, False)
                iteration(1, True, True)
                with sp.Fori(2, DEC_B) as b:
                    iteration(b, True, True)
                iteration(DEC_B, False, True)

            @block.scalar
            def _(act):
                def iteration(b, scores, values):
                    if values:
                        act.wait_ge(max_ready, 2 * b)
                        wait(act, w_turned, N5 * (b - 1))
                        nc.scalar.activation(W[:, :], S[:, :], ACT.Exp, bias=red[:, 6:7], accum_out=red[:, 7:8]).then_inc(exped, 1)
                    for p in range(PAGES if scores else 0):
                        act.wait_ge(turned_a, PAGES * b + p + 1)
                        nc.scalar.activation(KT[:, 0:half, (p % GROUP) * P:(p % GROUP + 1) * P],
                                             k.ps[2 * (p % 2)][:, :].rearrange("p (h n) -> p h n", h=half), ACT.Copy).then_inc(kt_out_a, 1)

                iteration(0, True, False)
                iteration(1, True, True)
                with act.Fori(2, DEC_B) as b:
                    iteration(b, True, True)
                iteration(DEC_B, False, True)

            @block.vector
            def _(dve):
                nc.vector.memset(Q[:, :, :], 0.0)
                nc.vector.memset(vnew[:, :], 0.0).then_inc(cleared, 1)
                nc.vector.memset(AT[:, PAGES, :], 0.0).then_inc(cleared, 1)
                nc.vector.memset(o[0:SMP, PT, :], 0.0).then_inc(cleared, 1)
                dve.wait_ge(cleared, 3)
                dve.wait_ge(c_in, 48)
                nc.vector.tensor_scalar(red[:, 9:10], table[:, 1:2], rep[:, 2 * P:2 * P + 1], table[:, 0:1],
                                        ALU.mult, ALU.add).then_inc(normed, 1)

                def bias_max(b, g):
                    w = GROUP * P if g < GROUPS_ else DEC_T
                    if g == 0:
                        wait(dve, exped, b)
                    dve.wait_ge(scored, N5 * b + g + 1)
                    nc.vector.memset(red[:, 11:12], 0.0)
                    part = slice(g * GROUP * P, g * GROUP * P + w)
                    nc.vector.tensor_tensor_reduce(out=S[:, part], in0=k.ps[4][:, 0:w], in1=alibi[:, part], scale=1.0,
                                                   scalar=-3e38, op0=ALU.add, op1=ALU.max,
                                                   accum_out=red[:, g:g + 1]).then_inc(biased, 1)

                def weights_out(b, g):
                    n = P if g < GROUPS_ else DEC_T
                    w = GROUP if g < GROUPS_ else 1
                    dve.wait_ge(w_turned, N5 * (b - 1) + g + 1)
                    src = k.ps[7][0:n, 0:w * P].rearrange("p (a x) -> p a x", x=QUAD)[:, :, 0:16]
                    src = src.rearrange("p a (h c t) -> p a h t c", h=2, c=2)
                    dst = AT[0:n, GROUP * g:GROUP * g + w, :].rearrange("p w (j h t) -> p (w j) h t", h=2, t=DEC_T)
                    nc.vector.tensor_reduce(out=dst, in_=src, op=ALU.add, axis=AX.X).then_inc(at_out, 1)

                def iteration(b, scores, values):
                    if scores:
                        wait(dve, scored, N5 * b)
                        for n in range(2):
                            nc.vector.tensor_copy(Q[:, n:HEADS:2, 8 * n:8 * n + 8],
                                                  qz[:, bass.ds(b, 1), n:HEADS:2, :].rearrange("p a h n -> p (a h) n"))
                        nc.vector.tensor_copy(knew[:, :, :], kTs[:, :, bass.ds(b * DEC_T, DEC_T)]).then_inc(q_ready, 1)
                    if values:
                        wait(dve, summed, 2 * (b - 1))
                        nc.vector.tensor_copy(place[:, :], places[:, bass.ds(b - 1, 1), :].rearrange("p a n -> p (a n)"))\
                            .then_inc(place_ready, 1)
                    for g in range(GROUPS_):
                        for p in range(GROUP * g, GROUP * (g + 1)):
                            if values and p % GROUP == GROUP - 1:
                                if g == 0:
                                    dve.wait_ge(exped, b)
                                    nc.vector.reciprocal(red[:, 8:9], red[:, 7:8]).then_inc(normed, 1)
                                    dve.wait_ge(normed, 3 * b - 1)
                                    nc.vector.tensor_tensor(red[:, 10:11], red[:, 8:9], red[:, 9:10], ALU.mult).then_inc(normed, 1)
                                    dve.wait_ge(normed, 3 * b)
                                    nc.vector.tensor_scalar(W[:, :], W[:, :], red[:, 10:11], None, ALU.mult).then_inc(normed, 1)
                                weights_out(b, g)
                            if scores:
                                dve.wait_ge(turned_b, PAGES * b + p + 1)
                                nc.vector.tensor_copy(KT[:, half:HEADS, (p % GROUP) * P:(p % GROUP + 1) * P],
                                                      k.ps[2 * (p % 2) + 1][:, :].rearrange("p (h n) -> p h n", h=half))\
                                    .then_inc(kt_out_b, 1)
                        if scores:
                            bias_max(b, g)
                    if values:
                        weights_out(b, GROUPS_)
                    if scores:
                        bias_max(b, GROUPS_)
                        dve.wait_ge(biased, N5 * (b + 1))
                        nc.vector.tensor_reduce(out=red[:, 5:6], in_=red[:, 0:5], op=ALU.max, axis=AX.X).then_inc(max_ready, 1)
                        dve.wait_ge(max_ready, 2 * b + 1)
                        nc.vector.tensor_scalar(red[:, 6:7], red[:, 5:6], -1.0, None, ALU.mult).then_inc(max_ready, 1)
                    if values:
                        dve.wait_ge(valued, N5 * b)
                        wait(dve, summed, 2 * (b - 1))
                        for n in range(2):
                            nc.vector.tensor_tensor(own[:, n * HB:(n + 1) * HB].rearrange("p (h n) -> p h n", n=P),
                                                    k.ps[5 + n][:, :].rearrange("p (h n) -> p h n", n=P),
                                                    bcast(own_head[:, half * n:half * (n + 1)], 2, [P, half, P]), ALU.mult)\
                                .then_inc(picked, 1)
                        for n, bank in enumerate((7, 4)):
                            dve.wait_ge(summed, 2 * (b - 1) + n + 1)
                            part = o[0:SMP, PT, n * HB:(n + 1) * HB]
                            nc.vector.tensor_tensor(part, part, k.ps[bank][0:SMP, :], ALU.add).then_inc(added, 1)

                iteration(0, True, False)
                iteration(1, True, True)
                with dve.Fori(2, DEC_B) as b:
                    iteration(b, True, True)
                iteration(DEC_B, False, True)

            @block.tensor
            def _(pe):
                def turn(b, p):
                    pe.wait_ge(k_in[p % KRING], 16 * (4 * b + p // KRING + 1))
                    for n, (free, signal) in enumerate(((kt_out_a, turned_a), (kt_out_b, turned_b))):
                        wait(pe, free, PAGES * b + p - 1)
                        for h in range(half):
                            hh = n * half + h
                            last = nc.tensor.transpose(k.ps[2 * (p % 2) + n][:, h * P:(h + 1) * P],
                                                       K[:, p % KRING, hh * P:(hh + 1) * P], k.ident[:, :])
                        last.then_inc(signal, 1)

                def score(b, g):
                    wait(pe, biased, N5 * b + g)
                    if g == 0:
                        pe.wait_ge(q_ready, b + 1)
                        wait(pe, added, 2 * (b - 1))
                    if g < GROUPS_:
                        pe.wait_ge(kt_out_a, PAGES * b + GROUP * (g + 1))
                        pe.wait_ge(kt_out_b, PAGES * b + GROUP * (g + 1))
                    for n in range(2):
                        for j in range(4):
                            h = 2 * j + n
                            rhs = KT[:, h, :] if g < GROUPS_ else knew[:, h, :]
                            w = GROUP * P if g < GROUPS_ else DEC_T
                            last = nc.tensor.matmul(k.ps[4][QUAD * j:QUAD * (j + 1), 0:w], Q[:, h, :], rhs, start=(n == 0), stop=(n == 1))
                    last.then_inc(scored, 1)

                def turn_weights(b, g):
                    if g == 0:
                        pe.wait_ge(normed, 3 * b + 1)
                        wait(pe, added, 2 * (b - 1))
                    wait(pe, at_out, N5 * (b - 1) + g)
                    if g < GROUPS_:
                        for n in range(GROUP):
                            p = GROUP * g + n
                            last = nc.tensor.transpose(k.ps[7][:, n * P:(n + 1) * P], W[:, p * P:(p + 1) * P], k.ident[:, :])
                    else:
                        last = nc.tensor.transpose(k.ps[7][0:DEC_T, 0:P], W[:, PAST:KEYS], k.ident[:, :])
                    last.then_inc(w_turned, 1)

                def value(b, g):
                    if g == 0:
                        wait(pe, picked, 2 * (b - 1))
                    pe.wait_ge(at_out, N5 * (b - 1) + g + 1)
                    if g < GROUPS_:
                        for p in range(GROUP * g, GROUP * (g + 1)):
                            pe.wait_ge(v_in[p % VRING], 16 * (2 * (b - 1) + p // VRING + 1))
                    else:
                        pe.wait_ge(vn_in, 16 * b)
                    pages = range(GROUP * g, GROUP * (g + 1)) if g < GROUPS_ else (PAGES,)
                    for n in range(2):
                        for p in pages:
                            q = p % 4
                            rhs = (V[p % VRING] if p < PAGES else vnew)[:, n * HB:(n + 1) * HB]
                            last = nc.tensor.matmul(k.ps[5 + n][QUAD * q:QUAD * (q + 1), :], AT[:, p, :], rhs, start=(p < 4),
                                                    stop=(p == PAGES or (p >= PAGES - 3)))
                    last.then_inc(valued, 1)

                def iteration(b, scores, values):
                    for g in range(GROUPS_):
                        for p in range(GROUP * g, GROUP * (g + 1)):
                            if values and p % GROUP == GROUP - 1:
                                turn_weights(b, g)
                            if scores:
                                turn(b, p)
                        if values:
                            value(b, g)
                        if scores:
                            score(b, g)
                    if values:
                        turn_weights(b, GROUPS_)
                    if scores:
                        score(b, GROUPS_)
                    if values:
                        value(b, GROUPS_)
                        pe.wait_ge(place_ready, b)
                        pe.wait_ge(at_out, N5 * b)
                        pe.wait_ge(biased, N5 * (b + 1) if scores else N5 * b)
                        for n, bank in enumerate((7, 4)):
                            pe.wait_ge(picked, 2 * (b - 1) + n + 1)
                            nc.tensor.matmul(k.ps[bank][0:SMP, :], place[:, :], own[:, n * HB:(n + 1) * HB], start=True, stop=True)\
                                .then_inc(summed, 1)

                iteration(0, True, False)
                iteration(1, True, True)
                with pe.Fori(2, DEC_B) as b:
                    iteration(b, True, True)
                iteration(DEC_B, False, True)



def final_block(k, a):
    nc = k.nc
    with ExitStack() as tmp_ctx:
        wrow = tmp_ctx.enter_context(nc.sbuf_tensor("final_row", [1, D], F32))
        y = tmp_ctx.enter_context(nc.sbuf_tensor("final_y", [P, NT, D], F32))
        w_in, squares, mean, seed = k.sem("final_w_landed"), k.sem("final_squares"), k.sem("final_mean"), k.sem("final_seed")
        spread, ready, stored = k.sem("final_spread"), k.sem("final_ready"), k.sem("final_stored")
        with nc.Block() as block:
            @block.sync
            def _(sp):
                sp.dma_start(wrow[:, :], a["final_norm_w"].rearrange("(a n) -> a n", a=1)).then_inc(w_in, 16)
                for t in range(NT):
                    sp.wait_ge(ready, 2 * (t + 1))
                    dst = a["y_prompt"][0, t * P:(t + 1) * P, :] if t < PT else a["y_sample"].rearrange("b t d -> (b t) d")
                    sp.dma_start(dst, y[0:rows(t), t, :]).then_inc(stored, 16)
                sp.wait_ge(stored, 16 * NT)

            @block.tensor
            def _(pe):
                pe.wait_ge(w_in, 16)
                for i in range(2):
                    last = nc.tensor.matmul(k.ps[i][:, :], k.ones[0:1, :], wrow[0:1, i * HB:(i + 1) * HB], start=True, stop=True)
                last.then_inc(spread, 1)

            @block.scalar
            def _(act):
                for t in range(NT):
                    nc.scalar.activation(y[:, t, :], k.h[:, t, :], ACT.Square, accum_out=k.ss[:, t:t + 1]).then_inc(squares, 1)
                act.wait_ge(mean, 1)
                nc.scalar.activation(k.tmp, k.ms, ACT.Ln).then_inc(seed, 1)
                act.wait_ge(seed, 1)
                nc.scalar.activation(k.r0, k.tmp, ACT.Exp, scale=-0.5).then_inc(seed, 1)

            @block.vector
            def _(dve):
                ch = Chain(dve, k.order["vector"], k.order_n["vector"])
                dve.wait_ge(squares, NT)
                nc.vector.tensor_scalar(k.ms, k.ss, 1.0 / D, EPS, ALU.mult, ALU.add).then_inc(mean, 1)
                dve.wait_ge(mean, 1)
                inverse_root(dve, None, (seed, 2), ch, nc, k.ms, k.r0, k.tmp, k.r)
                dve.wait_ge(spread, 1)
                for t in range(NT):
                    for i in range(2):
                        part = slice(i * HB, (i + 1) * HB)
                        nc.vector.scalar_tensor_tensor(out=y[:, t, part], in0=k.h[:, t, part], scalar=k.r[:, t:t + 1],
                                                       in1=k.ps[i][:, :], op0=ALU.mult, op1=ALU.mult).then_inc(ready, 1)
                k.order_n["vector"] = ch.n



def trunk(nc, a):
    with ExitStack() as ctx:
        k = Core(nc, ctx)
        rep = k.sb("row_gains", [P, 2 * P + 2])
        slots_x = nc.dram_tensor("slots_x", [SLOTS, D], F32, kind="Internal").ap()
        slots_y = nc.dram_tensor("slots_y", [SLOTS, D], F32, kind="Internal").ap()
        zeros_made, zeroed = k.sem("zeros_made"), k.sem("slots_zeroed")
        setup(k, a, None)
        broadcast_rows(k, rep)
        with k.stage(), ExitStack() as layer:
            sb = lambda name, shape: layer.enter_context(nc.sbuf_tensor(name, shape, F32))
            v, g = sb("hgrn_v", [P, NT, D]), sb("hgrn_g", [P, NT, D])
            norm_block(k, "mix0", [(k.cw[:, 0, :], k.xT)], v)
            with nc.Block() as block:
                @block.vector
                def _(dve):
                    nc.vector.memset(g[:, 0, :], 0.0).then_inc(zeros_made, 1)

                @block.sync
                def _(sp):
                    sp.wait_ge(zeros_made, 1)
                    for j in range(BLOCKS):
                        sp.dma_start(slots_x[j * P:(j + 1) * P, :], g[:, 0, :]).then_inc(zeroed, 16)
                    sp.wait_ge(zeroed, 16 * BLOCKS)
            hgrn_block(k, a, v, g, v, rep[:, 0:P])
            by_head = lambda ap: ap.rearrange("p (h n) -> p h n", n=P)
            mix_out_block(k, "out0", v, lambda t: by_head(g[:, t, :]), EPS)
        kv = a["w_kv"]
        with k.stage():
            moe_blocks(k, a, 0, slots_x, slots_y, (zeroed, 16 * BLOCKS),
                       [column_halves(kv, 0), column_halves(kv, HB), column_halves(a["b_w_q"][0], 0)])
        with k.stage(), ExitStack() as layer:
            sb = lambda name, shape: layer.enter_context(nc.sbuf_tensor(name, shape, F32))
            o = sb("attn_o", [P, NT, D])
            qz, kTs = sb("attn_qz", [P, DEC_B, HEADS, 2 * DEC_T]), sb("attn_kTs", [P, HEADS, SMP])
            with ExitStack() as prompt:
                sb = lambda name, shape: prompt.enter_context(nc.sbuf_tensor(name, shape, F32))
                kT, qT = sb("attn_kT", [P, HEADS, TOK]), [sb(f"attn_qT{c}", [P, HEADS, TOK]) for c in range(2)]
                v = sb("attn_v", [P, NT, D])
                with ExitStack() as proj:
                    sb = lambda name, shape: proj.enter_context(nc.sbuf_tensor(name, shape, F32))
                    q_xT = sb("attn_q_xT", [P, DC, TOK])
                    norm_block(k, "mix1", [(k.cw[:, 2, :], k.xT), (k.cw[:, 1, :], q_xT)], o)
                    kvq_block(k, a, k.xT, q_xT, o, v, kT, qT, o)
                prompt_attention(k, a, rep, v, kT, qT, qz, kTs, o)
            sample_attention(k, a, rep, qz, kTs, o)
            subln = bcast(rep[:, P:2 * P], 1, [P, HEADS, P])
            mix_out_block(k, "out1", o, lambda t: subln, SUBLN_EPS)
        moe_blocks(k, a, 1, slots_x, slots_y, (zeroed, 0), [])
        final_block(k, a)


INPUTS = ["x_prompt", "x_sample", "state_hgrn", "cache_k", "cache_v", "page_table", "norm_mix_w", "norm_ffn_w", "a_w_in",
          "a_lb_logits", "a_gnorm_w", "a_w_o", "kv_norm_w", "w_kv", "b_w_q", "b_lambda_q1", "b_lambda_k1", "b_lambda_q2",
          "b_lambda_k2", "b_subln_w", "b_w_o", "moe_w_group", "moe_w_sub", "moe_w_gate", "moe_w_up", "moe_w_down",
          "final_norm_w"]
OUTPUTS = [("y_prompt", (1, SEQ, D)), ("y_sample", (DEC_B, DEC_T, D)), ("state_prompt", (1, 1, HEADS, P, P)),
           ("state_sample", (1, DEC_B, HEADS, P, P)), ("k_prompt", (1, SEQ, HEADS, P)), ("v_prompt", (1, SEQ, HEADS, P)),
           ("k_sample", (DEC_B, DEC_T, HEADS, P)), ("v_sample", (DEC_B, DEC_T, HEADS, P))]


def constants():
    import numpy as np

    f32 = np.float32
    q, key = np.arange(P)[:, None], np.arange(SEQ)[None, :]
    dist = (SEQ - P + q - key).astype(f32)
    dist[dist < 0] = MASKED
    row = np.arange(P)
    j, x = row // 32, row % 32
    used, head, half, t = x < 16, 2 * j + x // 8, x // 4 % 2, x % 4
    pos = np.arange(PAST + DEC_T)[None, :]
    slope = (2.0 ** -(head + 1.0))[:, None].astype(f32)
    alibi = -slope * (PAST + t[:, None] - pos).astype(f32)
    alibi[pos > PAST + t[:, None]] = -MASKED
    alibi[~used] = 0
    halves = np.stack([used & (half == 0), used & (half == 1)], 1)
    own_head = (x // DEC_T)[:, None] == np.arange(HEADS)[None, :]
    place = np.arange(SMP)[None, None, :] == np.arange(DEC_B)[None, :, None] * DEC_T + (x % DEC_T)[:, None, None]
    return {"const_dist": dist, "const_rows": np.concatenate([alibi, halves, own_head, place.reshape(P, -1)], 1).astype(f32)}


def kernel(**inputs):
    import numpy as np
    import concourse.bacc as bacc
    from concourse.bass_utils import run_bass_kernel_spmd

    nc = bacc.Bacc("TRN2", target_bir_lowering=False, num_devices=1)
    arrays, a = {}, {}
    given = {n: np.ascontiguousarray(inputs[n]) for n in INPUTS}
    for name, x in {**given, **constants()}.items():
        arrays[name] = x
        a[name] = nc.dram_tensor(name, x.shape, mybir.dt.from_np(x.dtype), kind="ExternalInput").ap()
    for name, shape in OUTPUTS:
        a[name] = nc.dram_tensor(name, shape, F32, kind="ExternalOutput").ap()
    trunk(nc, a)
    r = run_bass_kernel_spmd(nc, [arrays], core_ids=[0])
    return tuple(r.results[0][name] for name, _ in OUTPUTS)
```

```python
import math
from contextlib import ExitStack, contextmanager

import concourse.bass as bass
from concourse import mybir

F32 = mybir.dt.float32
I32 = mybir.dt.int32
ALU = mybir.AluOpType
ACT = mybir.ActivationFunctionType
AX = mybir.AxisListType

P = 128
D = 1024
DC = D // P
SEQ = 512
DEC_B, DEC_T = 8, 4
SMP = DEC_B * DEC_T
TOK = SEQ + SMP
PT = SEQ // P
NT = PT + 1
HEADS = 8
HB = 512
EPG, GROUPS, EXPERTS, TOPK = 4, 4, 16, 2
FF = 256
BLOCKS = (TOK * TOPK - EXPERTS) // P + EXPERTS
SLOTS = BLOCKS * P
PAGE, PAGES = 128, 16
PAST = PAGE * PAGES
LEVELS = (8, 16, 32, 64, 128)
LAM_INIT = 0.8 - 0.6 * math.exp(-0.3)
FG_MIN = 2.0 ** -63
MASKED = 1e30
EPS, SUBLN_EPS = 1e-6, 1e-5
WEIGHT_SLOTS = 3


def rows(t):
    return P if t < PT else SMP


def cols(t):
    return slice(t * P, t * P + rows(t))


class Chain:

    def __init__(self, eng, sem, start=0):
        self.eng, self.sem, self.n = eng, sem, start

    def __call__(self, ins):
        self.n = self.n + 1
        ins.then_inc(self.sem, 1)
        self.eng.wait_ge(self.sem, self.n)


class Core:

    def __init__(self, nc, ctx):
        self.nc, self.ctx, self.stage_sems = nc, ctx, None
        self.ps = [self.psum(f"bank{i}", [P, HB]) for i in range(8)]
        self.ident = self.sb("ident", [P, P])
        self.ones = self.sb("ones", [1, P])
        self.h = self.sb("h", [P, NT, D])
        self.xT = self.sb("xT", [P, DC, TOK])
        self.stat = self.sb("stat", [P, 64])
        self.ss, self.ms, self.r0 = self.stat[:, 0:5], self.stat[:, 8:13], self.stat[:, 16:21]
        self.tmp, self.r = self.stat[:, 24:29], self.stat[:, 32:37]
        self.wring = [self.sb(f"wring{i}", [P, DC, HB]) for i in range(WEIGHT_SLOTS)]
        self.cw = self.sb("column_weights", [P, 5, DC])
        self.rowbuf = self.sb("row_weights", [1, 2 * P + 4 * 64])
        self.lamwork = self.sb("lambda_products", [1, 2, 64])
        self.levelmask = self.sb("level_masks", [P, 1 + len(LEVELS), P])
        self.restart = self.sb("scan_restart", [P, TOK])
        self.batchmask = self.sb("batch_mask", [SMP, DEC_B])
        self.lb = self.sb("lower_bound", [P, 4, HEADS])
        self.w_in = [self.sem(f"weights_landed{i}") for i in range(WEIGHT_SLOTS)]
        self.w_done = []
        self.w_issued = 0
        self.w_taken = 0
        self.order = {n: self.sem(f"{n}_order") for n in ("vector", "scalar", "gpsimd")}
        self.order_n = dict.fromkeys(self.order, 0)

    def sb(self, name, shape, dt=F32):
        return self.ctx.enter_context(self.nc.sbuf_tensor(name, shape, dt))

    def psum(self, name, shape, dt=F32):
        return self.ctx.enter_context(self.nc.psum_tensor(name, shape, dt))

    def sem(self, name):
        if self.stage_sems is None:
            return self.ctx.enter_context(self.nc.semaphore(name))
        self.stage_sems.append(self.nc.alloc_semaphore(name))
        return self.stage_sems[-1]

    @contextmanager
    def stage(self):
        self.stage_sems = []
        yield
        self.w_done = [None] * len(self.w_done)
        self.nc.clear_and_free_semaphores(self.stage_sems)
        self.nc.all_engine_barrier()
        self.stage_sems = None

    def load_weights(self, sp, halves):
        n = self.w_issued
        if n >= WEIGHT_SLOTS and self.w_done[n - WEIGHT_SLOTS]:
            sp.wait_ge(*self.w_done[n - WEIGHT_SLOTS])
        slot = n % WEIGHT_SLOTS
        for dst, src in halves(self.wring[slot]):
            sp.dma_start(dst, src).then_inc(self.w_in[slot], 16)
        self.w_issued += 1

    def take_weights(self, pe):
        n = self.w_taken
        pe.wait_ge(self.w_in[n % WEIGHT_SLOTS], 32 * (n // WEIGHT_SLOTS + 1))
        self.w_taken += 1
        return self.wring[n % WEIGHT_SLOTS]


def column_halves(w, n0):
    view = w.rearrange("(c p) n -> p c n", p=P)
    half = DC // 2
    return lambda tile: [(tile[:, 0:half, :], view[:, 0:half, n0:n0 + HB]),
                         (tile[:, half:DC, :], view[:, half:DC, n0:n0 + HB])]


def bcast(ap, axis, shape):
    return ap.unsqueeze(axis).to_broadcast(shape)



def setup(k, a, rep):
    nc = k.nc
    tokens_in, rows_in, columns_in = k.sem("tokens_landed"), k.sem("row_weights_landed"), k.sem("column_weights_landed")
    ident_made, turned, out = k.sem("ident_made"), k.sem("columns_turned"), k.sem("columns_out")
    summed, spread = k.sem("lambda_summed"), k.sem("rows_spread")
    lam = k.rowbuf[:, 2 * P:].rearrange("a (i n) -> a i n", i=4)
    s = k.stat[0:1, 40:48]
    by_feature = (a["norm_mix_w"][0], a["norm_mix_w"][1], a["kv_norm_w"], a["norm_ffn_w"][0], a["norm_ffn_w"][1],
                  a["a_lb_logits"][0])
    n_cols = len(by_feature) * DC
    with nc.sbuf_tensor("column_weights_by_row", [n_cols, P], F32) as weight_rows, nc.Block() as block:
        @block.sync
        def _(sp):
            for t in range(PT):
                sp.dma_start(k.h[:, t, :], a["x_prompt"][0, t * P:(t + 1) * P, :]).then_inc(tokens_in, 16)
            sp.dma_start(k.h[0:SMP, PT, :], a["x_sample"].rearrange("b t d -> (b t) d")).then_inc(tokens_in, 16)
            sp.wait_ge(columns_in, 16 * len(by_feature))
            sp.wait_ge(rows_in, 16 * 6)
            for i in range(2):
                k.load_weights(sp, column_halves(a["a_w_in"][0], 2 * D + i * HB))
            k.load_weights(sp, head_pair_halves(a, 0))
            sp.wait_ge(tokens_in, 16 * NT)

        @block.scalar
        def _(act):
            for i, w in enumerate((a["b_lambda_q1"], a["b_lambda_k1"], a["b_lambda_q2"], a["b_lambda_k2"])):
                act.dma_start(lam[:, i, :], w).then_inc(rows_in, 16)
            act.dma_start(k.rowbuf[:, 0:P], a["a_gnorm_w"]).then_inc(rows_in, 16)
            act.dma_start(k.rowbuf[:, P:2 * P], a["b_subln_w"]).then_inc(rows_in, 16)
            for i, w in enumerate(by_feature):
                act.dma_start(weight_rows[i * DC:(i + 1) * DC, :], w.rearrange("(c p) -> c p", p=P)).then_inc(columns_in, 16)
            act.wait_ge(summed, 2)
            nc.scalar.activation(s[:, 2:4], s[:, 0:2], ACT.Exp).then_inc(summed, 1)

        @block.gpsimd
        def _(pool):
            ch = Chain(pool, k.order["gpsimd"], k.order_n["gpsimd"])
            ch(pool.memset(k.ident[:, :], 0.0))
            ch(pool.affine_select(out=k.ident[:, :], in_=k.ident[:, :], compare_op=ALU.not_equal, fill=1.0,
                                  base=0, pattern=[[-1, P]], channel_multiplier=1))
            nc.gpsimd.memset(k.ones[:, :], 1.0).then_inc(ident_made, 1)
            ch(pool.memset(k.levelmask[:, :, :], 0.0))
            m = k.levelmask[:, 0, :].rearrange("p (n r) -> p n r", r=4)
            ch(pool.memset(m, 1.0))
            ch(pool.affine_select(out=m, in_=m, compare_op=ALU.is_ge, fill=0.0, base=0,
                                  pattern=[[-4, P // 4], [0, 4]], channel_multiplier=1))
            ch(pool.affine_select(out=m, in_=m, compare_op=ALU.is_ge, fill=0.0, base=0,
                                  pattern=[[4, P // 4], [1, 4]], channel_multiplier=-1))
            for i, size in enumerate(LEVELS):
                half = size // 2
                m = k.levelmask[:, i + 1, :].rearrange("p (n r) -> p n r", r=size)[:, :, half:size]
                ch(pool.memset(m, 1.0))
                ch(pool.affine_select(out=m, in_=m, compare_op=ALU.is_ge, fill=0.0, base=0,
                                      pattern=[[-size, P // size], [0, half]], channel_multiplier=1))
                ch(pool.affine_select(out=m, in_=m, compare_op=ALU.is_ge, fill=0.0, base=half - 1,
                                      pattern=[[size, P // size], [0, half]], channel_multiplier=-1))
            ch(pool.memset(k.restart[:, :], 1.0))
            ch(pool.memset(k.restart[:, 0:SEQ].rearrange("p (c n) -> p c n", n=P)[:, :, 0:1], 0.0))
            ch(pool.memset(k.restart[:, SEQ:TOK].rearrange("p (c n) -> p c n", n=DEC_T)[:, :, 0:1], 0.0))
            ch(pool.memset(k.batchmask[:, :], 1.0))
            ch(pool.affine_select(out=k.batchmask[:, :], in_=k.batchmask[:, :], compare_op=ALU.is_ge, fill=0.0,
                                  base=0, pattern=[[-DEC_T, DEC_B]], channel_multiplier=1))
            ch(pool.affine_select(out=k.batchmask[:, :], in_=k.batchmask[:, :], compare_op=ALU.is_ge, fill=0.0,
                                  base=DEC_T - 1, pattern=[[DEC_T, DEC_B]], channel_multiplier=-1))
            k.order_n["gpsimd"] = ch.n

        @block.vector
        def _(dve):
            for q in range(1, 4):
                nc.vector.memset(k.h[32 * q:32 * q + 32, PT, :], 0.0)
            dve.wait_ge(rows_in, 16 * 6)
            for i in range(2):
                nc.vector.tensor_tensor_reduce(out=k.lamwork[:, i, :],
                                               in0=lam[:, 2 * i, :], in1=lam[:, 2 * i + 1, :], scale=1.0, scalar=0.0,
                                               op0=ALU.mult, op1=ALU.add, accum_out=s[:, i:i + 1]).then_inc(summed, 1)
            dve.wait_ge(summed, 3)
            nc.vector.scalar_tensor_tensor(out=s[:, 4:5], in0=s[:, 3:4], scalar=-LAM_INIT, in1=s[:, 2:3], op0=ALU.add,
                                           op1=ALU.subtract).then_inc(summed, 1)
            dve.wait_ge(turned, 1)
            nc.vector.tensor_copy(k.cw[:, :, :].rearrange("p i c -> p (i c)"), k.ps[6][:, 0:n_cols - DC]).then_inc(out, 1)
            nc.vector.tensor_copy(k.lb[:, 0, :], k.ps[6][:, n_cols - DC:n_cols]).then_inc(out, 1)
            dve.wait_ge(spread, 1)
            nc.vector.tensor_copy(rep[:, 0:P], k.ps[7][:, 0:P]).then_inc(out, 1)
            nc.vector.tensor_scalar(rep[:, P:2 * P], k.ps[7][:, P:2 * P], 1.0 - LAM_INIT, None, ALU.mult).then_inc(out, 1)
            nc.vector.tensor_copy(rep[:, 2 * P:2 * P + 1], k.ps[7][:, 2 * P:2 * P + 1]).then_inc(out, 1)

        @block.tensor
        def _(pe):
            pe.wait_ge(ident_made, 1)
            pe.wait_ge(columns_in, 16 * len(by_feature))
            nc.tensor.transpose(k.ps[6][:, 0:n_cols], weight_rows[0:n_cols, :], k.ident[0:n_cols, 0:n_cols]).then_inc(turned, 1)
            pe.wait_ge(rows_in, 16 * 6)
            nc.tensor.matmul(k.ps[7][:, 0:2 * P], k.ones[0:1, :], k.rowbuf[:, 0:2 * P], start=True, stop=True)
            pe.wait_ge(summed, 4)
            nc.tensor.matmul(k.ps[7][:, 2 * P:2 * P + 1], k.ones[0:1, :], s[:, 4:5], start=True, stop=True).then_inc(spread, 1)


def head_pair_halves(a, pair):
    view = a["a_w_in"][0].rearrange("(c p) n -> p c n", p=P)
    n = 2 * P
    return lambda tile: [(tile[:, :, 0:n], view[:, :, pair * n:(pair + 1) * n]),
                         (tile[:, :, n:2 * n], view[:, :, D + pair * n:D + (pair + 1) * n])]



def inverse_root(dve, act_ready, root_ready, ch, nc, ms, r0, tmp, r):
    dve.wait_ge(*root_ready)
    ch(nc.vector.tensor_tensor(tmp, r0, r0, ALU.mult))
    ch(nc.vector.tensor_tensor(tmp, tmp, ms, ALU.mult))
    ch(nc.vector.tensor_scalar(tmp, tmp, -0.5, 1.5, ALU.mult, ALU.add))
    ch(nc.vector.tensor_tensor(r, r0, tmp, ALU.mult))


def norm_block(k, tag, weights, xs, store=None):
    nc = k.nc
    squares_a, squares_v = k.sem(f"{tag}_squares_act"), k.sem(f"{tag}_squares_dve")
    mean_ready, seed_ready = k.sem(f"{tag}_mean"), k.sem(f"{tag}_seed")
    xs_ready, turned = k.sem(f"{tag}_xs"), k.sem(f"{tag}_turned")
    out_v, out_a = k.sem(f"{tag}_out_dve"), k.sem(f"{tag}_out_act")
    ACT_TILES = (2, 3, 4)
    half = DC // 2
    nw = len(weights)
    junk = xs
    with nc.Block() as block:
        @block.scalar
        def _(act):
            for t in ACT_TILES:
                nc.scalar.activation(junk[:, t, :], k.h[:, t, :], ACT.Square,
                                     accum_out=k.ss[:, t:t + 1]).then_inc(squares_a, 1)
            act.wait_ge(mean_ready, 1)
            nc.scalar.activation(k.tmp, k.ms, ACT.Ln).then_inc(seed_ready, 1)
            act.wait_ge(seed_ready, 1)
            nc.scalar.activation(k.r0, k.tmp, ACT.Exp, scale=-0.5).then_inc(seed_ready, 1)
            for t in range(NT):
                act.wait_ge(turned, t + 1)
                for i, (w, out) in enumerate(weights):
                    for c in range(half, DC):
                        src = k.ps[2 * (t % 2) + 1][:, (c - half) * P:(c - half) * P + rows(t)]
                        nc.scalar.activation(out[:, c, cols(t)], src, ACT.Copy,
                                             scale=w[:, c:c + 1]).then_inc(out_a, 1)

        @block.vector
        def _(dve):
            ch = Chain(dve, k.order["vector"], k.order_n["vector"])
            for t in range(NT):
                if t not in ACT_TILES:
                    nc.vector.tensor_tensor_reduce(out=junk[:, t, :], in0=k.h[:, t, :], in1=k.h[:, t, :], scale=1.0,
                                                   scalar=0.0, op0=ALU.mult, op1=ALU.add,
                                                   accum_out=k.ss[:, t:t + 1]).then_inc(squares_v, 1)
            dve.wait_ge(squares_a, len(ACT_TILES))
            dve.wait_ge(squares_v, NT - len(ACT_TILES))
            nc.vector.tensor_scalar(k.ms, k.ss, 1.0 / D, EPS, ALU.mult, ALU.add).then_inc(mean_ready, 1)
            dve.wait_ge(mean_ready, 1)
            inverse_root(dve, None, (seed_ready, 2), ch, nc, k.ms, k.r0, k.tmp, k.r)
            for t in range(NT):
                nc.vector.tensor_scalar(xs[:, t, :], k.h[:, t, :], k.r[:, t:t + 1], None, ALU.mult)\
                    .then_inc(xs_ready, 1)
            for t in range(NT):
                dve.wait_ge(turned, t + 1)
                for w, out in weights:
                    src = k.ps[2 * (t % 2)][:, :].rearrange("p (c n) -> p c n", c=half)[:, :, 0:rows(t)]
                    nc.vector.tensor_tensor(out[:, 0:half, cols(t)], src,
                                            bcast(w[:, 0:half], 2, [P, half, rows(t)]), ALU.mult).then_inc(out_v, 1)
            k.order_n["vector"] = ch.n

        @block.tensor
        def _(pe):
            for t in range(NT):
                pe.wait_ge(xs_ready, t + 1)
                if t >= 2:
                    pe.wait_ge(out_v, nw * (t - 1))
                    pe.wait_ge(out_a, nw * half * (t - 1))
                for c in range(DC):
                    last = nc.tensor.transpose(k.ps[2 * (t % 2) + c // half][:, (c % half) * P:(c % half) * P + rows(t)],
                                               xs[0:rows(t), t, c * P:(c + 1) * P], k.ident[0:rows(t), 0:rows(t)])
                last.then_inc(turned, 1)

        if store is not None:
            @block.sync
            def _(sp):
                store(sp, xs_ready)



def project_tokens(nc, bank, xT, w, t):
    for c in range(DC):
        if t < PT:
            last = nc.tensor.matmul(bank[:, :], xT[:, c, cols(t)], w[:, c, :], start=(c == 0), stop=(c == DC - 1))
        else:
            for j in range(HB // P):
                last = nc.tensor.matmul(bank[SMP * j:SMP * (j + 1), 0:P], xT[:, c, cols(t)], w[:, c, j * P:(j + 1) * P],
                                        start=(c == 0), stop=(c == DC - 1))
    return last


def token_parts(bank, out, i, t):
    if t < PT:
        return [(bank[:, :], out[:, t, i * HB:(i + 1) * HB])]
    return [(bank[SMP * j:SMP * (j + 1), 0:P], out[0:SMP, t, i * HB + j * P:i * HB + (j + 1) * P]) for j in range(HB // P)]



GATE_UNITS = [[("g", n // NT, n % NT) for n in range(*span)] for span in ((0, 2), (2, 3), (3, 4), (4, 5), (5, 6), (6, 7),
                                                                          (7, 8), (8, 8), (8, 10))]
GATE_TILE_AT = [0, 4]



def hgrn_block(k, a, v, g, o, gnorm, slots, zeroed):
    nc = k.nc
    NLEV = 1 + len(LEVELS)
    with ExitStack() as tmp_ctx:
        def sb(name, shape):
            return tmp_ctx.enter_context(nc.sbuf_tensor(name, shape, F32))

        f_in, q = [sb(f"gla_fin{i}", [P, TOK]) for i in range(2)], [sb(f"gla_q{i}", [P, TOK]) for i in range(2)]
        kk, b = sb("gla_k", [P, TOK]), sb("gla_b", [P, TOK])
        mid4 = sb("gla_mid4", [P, TOK // 4])
        diff = [sb(f"gla_diff{i}", [P, TOK]) for i in range(2)]
        inv4 = sb("gla_inv4", [P, TOK])
        eb, kd = sb("gla_eb", [P, TOK]), inv4
        QE = [sb(f"gla_qe{i}", [P, TOK if i == 0 else SEQ]) for i in range(NLEV)]
        KE = [sb(f"gla_ke{i}", [P, TOK if i == 0 else SEQ]) for i in range(NLEV)]
        smp_qf = sb("gla_sample_qf", [P, P])
        QS = sb("gla_qs", [P, TOK])
        QB = sb("gla_qb", [P, DEC_B * (SMP + DEC_T)])
        A = sb("gla_att", [P, PT, P])
        AS = sb("gla_att_s", [SMP, SMP])
        kdT, kdTs = sb("gla_kdT", [P, PT, P]), sb("gla_kdTs", [SMP, P])
        below = sb("gla_vm", [P, DEC_B, P])
        vm = below[0:SMP, :, :]
        zero = below[SMP:P, :, :].rearrange("p b n -> p (b n)")
        ZERO = P - SMP
        assert SLOTS % ZERO == 0
        S = [sb("gla_s", [P, PT, P])] * 2
        s0 = [sb(f"gla_s0_{i}", [P, DEC_B, P]) for i in range(2)]
        sn = [sb("gla_sn", [P, DEC_B, P])] * 2

        units = {}
        order = [("v", i, t) for i in range(2) for t in range(NT)]
        for h in range(HEADS):
            if h % 2 == 0:
                order += [("s", h // 2)]
            order += [("f", h), ("q", h)] + GATE_UNITS[h]
        order += GATE_UNITS[HEADS]
        n = 0
        for i, u in enumerate(order):
            if u[0] == "s":
                units[u] = (i + 1, 2)
            else:
                units[u] = (i + 1, n % 2)
                n += 1
        proj_done, s_copied, s_turned = k.sem("proj_done"), k.sem("sample_qf_copied"), k.sem("sample_qf_turned")
        v_out, qf_out, g_out = k.sem("v_evacuated"), k.sem("qf_evacuated"), k.sem("g_evacuated")
        evacuated = {}
        for u in order:
            if u[0] == "v":
                evacuated[u] = (v_out, NT * u[1] + u[2] + 1)
            elif u[0] == "g":
                evacuated[u] = (g_out, NT * u[1] + u[2] + 1)
            else:
                evacuated[u] = (qf_out, 4 * u[1] + {"f": 1, "q": 3}[u[0]] if u[0] != "s" else 8 * u[1] + 8)
        before = {}
        last_in = {}
        for u in order:
            before[u] = last_in.get(units[u][1])
            last_in[units[u][1]] = u

        fgc_ready, logf_ready, b_ready = k.sem("fg_ready"), k.sem("logf_ready"), k.sem("b_ready")
        diff_ready, exp_ready = k.sem("diff_ready"), k.sem("exp_ready")
        q_lev, k_lev = k.sem("q_level_ready"), k.sem("k_level_ready")
        kk_ready = k.sem("k_ready")
        turned, turned_out = k.sem("kd_turned"), k.sem("kd_turned_out")
        att_done, att_taken = k.sem("att_done"), k.sem("att_taken")
        ds_done, s_ready = k.sem("state_step_done"), k.sem("state_ready")
        sds_done, sn_ready, sn_scaled = k.sem("sample_step_done"), k.sem("sample_state_ready"), k.sem("sample_state_scaled")
        vm_ready, o_done, o_out = k.sem("vm_ready"), k.sem("o_done"), k.sem("o_evacuated")
        zero_made = k.sem("zero_made")
        s0_in = [k.sem(f"s0_landed{i}") for i in range(2)]
        s_store, sn_store = [k.sem("s_stored")], [k.sem("sn_stored")]
        head = lambda h: slice(h * P, (h + 1) * P)
        blocks = lambda ap, n: ap.rearrange("p (c n) -> p c n", n=n)
        QBd = QB[:, :].rearrange("p (b x) -> p b x", x=SMP + DEC_T)[:, :, 0:DEC_T]

        with nc.Block() as block:
            @block.scalar
            def _(act):
                def evacuate_qf(h):
                    x = SMP * (h % 2)
                    if h % 2 == 0:
                        act.wait_ge(proj_done, units[("s", h // 2)][0])
                        nc.scalar.activation(smp_qf[:, :], k.ps[2][:, 0:P], ACT.Copy).then_inc(s_copied, 1)
                    done, bank = units[("f", h)]
                    act.wait_ge(proj_done, done)
                    if h >= 2:
                        act.wait_ge(q_lev, (NLEV + 2) * (h - 1))
                    nc.scalar.activation(f_in[h % 2][:, 0:SEQ], k.ps[bank][:, :], ACT.Sigmoid).then_inc(qf_out, 1)
                    act.wait_ge(s_turned, h // 2 + 1)
                    nc.scalar.activation(f_in[h % 2][:, SEQ:TOK], k.ps[2][:, P + 2 * SMP + x:P + 3 * SMP + x], ACT.Sigmoid)\
                        .then_inc(qf_out, 1)
                    done, bank = units[("q", h)]
                    act.wait_ge(proj_done, done)
                    nc.scalar.activation(q[h % 2][:, 0:SEQ], k.ps[bank][:, :], ACT.Silu).then_inc(qf_out, 1)
                    nc.scalar.activation(q[h % 2][:, SEQ:TOK], k.ps[2][:, P + x:P + SMP + x], ACT.Silu).then_inc(qf_out, 1)

                def gate(u):
                    done, bank = units[u]
                    _, i, t = u
                    act.wait_ge(proj_done, done)
                    for n, (src, dst) in enumerate(token_parts(k.ps[bank], g, i, t)):
                        last = nc.scalar.activation(dst, src, ACT.Silu)
                    last.then_inc(g_out, 1)

                def exponentials(h):
                    act.wait_ge(fgc_ready, 2 * h + 2)
                    nc.scalar.activation(f_in[h % 2][:, :], f_in[h % 2][:, :], ACT.Ln).then_inc(logf_ready, 1)
                    base = (NLEV + 1) * h
                    act.wait_ge(diff_ready, base + 1)
                    if h:
                        act.wait_ge(sn_scaled, h)
                    nc.scalar.activation(inv4[:, :], diff[0][:, :], ACT.Exp, scale=-1.0).then_inc(exp_ready, 1)
                    nc.scalar.activation(diff[0][:, :], diff[0][:, :], ACT.Exp).then_inc(exp_ready, 1)
                    nc.scalar.activation(eb[:, :], b[:, :], ACT.Exp).then_inc(exp_ready, 1)
                    for i in range(1, NLEV + 1):
                        act.wait_ge(diff_ready, base + i + 1)
                        w = TOK if i == NLEV else SEQ
                        nc.scalar.activation(diff[i % 2][:, 0:w], diff[i % 2][:, 0:w], ACT.Exp).then_inc(exp_ready, 1)

                def results(h):
                    act.wait_ge(turned, h + 1)
                    nc.scalar.activation(kdT[:, :, :], k.ps[5][:, :], ACT.Copy).then_inc(turned_out, 1)
                    nc.scalar.activation(kdTs[:, :], k.ps[6][0:SMP, P:2 * P], ACT.Copy).then_inc(turned_out, 1)
                    act.wait_ge(o_done, h + 1)
                    nc.scalar.activation(o[:, 0:PT, head(h)], k.ps[7][:, :].rearrange("p (c n) -> p c n", c=PT), ACT.Copy)\
                        .then_inc(o_out, 1)
                    nc.scalar.activation(o[0:SMP, PT, head(h)], k.ps[6][0:SMP, 2 * P:3 * P], ACT.Copy).then_inc(o_out, 1)

                for h in range(HEADS):
                    evacuate_qf(h)
                    for u in GATE_UNITS[h]:
                        gate(u)
                    if h:
                        results(h - 1)
                    exponentials(h)
                for u in GATE_UNITS[HEADS]:
                    gate(u)
                results(HEADS - 1)

            @block.vector
            def _(dve):
                ch = Chain(dve, k.order["vector"], k.order_n["vector"])
                lb = k.lb
                nc.vector.memset(below[:, :, :], 0.0).then_inc(zero_made, 1)
                ch(nc.vector.tensor_tensor(lb[:, 1, :], lb[:, 0, :], lb[:, 0, :], ALU.subtract))
                ch(nc.vector.tensor_scalar(lb[:, 1, :], lb[:, 1, :], 1.0, None, ALU.add))
                ch(nc.vector.tensor_tensor(lb[:, 2, :], lb[:, 1, :], lb[:, 1, :], ALU.subtract))
                ch(nc.vector.tensor_scalar(lb[:, 3, :], lb[:, 2, :], -1.0, 1.0, ALU.mult, ALU.add))
                for i, lev in enumerate(LEVELS):
                    nc.vector.memset(QE[i + 1][:, :], 0.0)
                    ch(nc.vector.memset(KE[i + 1][:, :], 0.0))
                nc.vector.memset(QB[:, :], 0.0)
                nc.vector.memset(A[:, :, :], 0.0)
                ch(nc.vector.memset(AS[:, :], 0.0))
                for x in range(1, 4):
                    nc.vector.memset(g[32 * x:32 * x + 32, PT, :], 0.0)
                    nc.vector.memset(v[32 * x:32 * x + 32, PT, :], 0.0)
                for i in range(2):
                    for t in range(NT):
                        done, bank = units[("v", i, t)]
                        dve.wait_ge(proj_done, done)
                        for src, dst in token_parts(k.ps[bank], v, i, t):
                            last = nc.vector.tensor_copy(dst, src)
                        last.then_inc(v_out, 1)

                def elementwise(h):
                    dve.wait_ge(qf_out, 4 * h + 2)
                    if h:
                        dve.wait_ge(k_lev, (NLEV + 1) * h)
                    nc.vector.tensor_scalar(f_in[h % 2][:, :], f_in[h % 2][:, :], lb[:, 3, h:h + 1], lb[:, 2, h:h + 1],
                                            ALU.mult, ALU.add).then_inc(fgc_ready, 1)
                    dve.wait_ge(fgc_ready, 2 * h + 1)
                    nc.vector.tensor_scalar(kk[:, :], f_in[h % 2][:, :], -1.0, 1.0, ALU.mult, ALU.add).then_inc(kk_ready, 1)
                    dve.wait_ge(kk_ready, h + 1)
                    nc.vector.tensor_scalar(f_in[h % 2][:, :], f_in[h % 2][:, :], FG_MIN, None, ALU.max).then_inc(fgc_ready, 1)
                    dve.wait_ge(logf_ready, h + 1)
                    ch(nc.vector.tensor_tensor_scan(b[:, :], k.restart[:, :], f_in[h % 2][:, :], 0.0, ALU.mult, ALU.add))
                    b4 = blocks(b[:, :], 4)
                    ch(nc.vector.tensor_tensor(mid4[:, :], b4[:, :, 1], b4[:, :, 2], ALU.add))
                    nc.vector.scalar_tensor_tensor(out=blocks(diff[0][:, :], 4), in0=bcast(mid4[:, :], 2, [P, TOK // 4, 4]),
                                                   scalar=0.5, in1=b4, op0=ALU.mult, op1=ALU.subtract).then_inc(diff_ready, 1)
                    ebase = (NLEV + 3) * h
                    for i in range(1, NLEV + 1):
                        d = diff[i % 2]
                        if i >= 2:
                            dve.wait_ge(k_lev, (NLEV + 1) * h + i - 1)
                            dve.wait_ge(q_lev, (NLEV + 2) * h + i)
                        if i < NLEV:
                            size = LEVELS[i - 1]
                            half = size // 2
                            bv, dv = blocks(b[:, 0:SEQ], size), blocks(d[:, 0:SEQ], size)
                            mid = bcast(bv[:, :, half - 1], 2, [P, SEQ // size, half])
                            nc.vector.tensor_tensor(dv[:, :, 0:half], mid, bv[:, :, 0:half], ALU.subtract)
                            nc.vector.tensor_tensor(dv[:, :, half:size], bv[:, :, half:size], mid, ALU.subtract)\
                                .then_inc(diff_ready, 1)
                        else:
                            for lo, hi, n in ((0, SEQ, P), (SEQ, TOK, DEC_T)):
                                bv, dv = blocks(b[:, lo:hi], n), blocks(d[:, lo:hi], n)
                                last = nc.vector.tensor_tensor(dv, bcast(bv[:, :, n - 1], 2, [P, (hi - lo) // n, n]), bv,
                                                               ALU.subtract)
                            last.then_inc(diff_ready, 1)
                        j = i - 1
                        if h and j == 0:
                            dve.wait_ge(att_done, (NLEV + 1) * h)
                            dve.wait_ge(o_done, h)
                        if j == 0:
                            dve.wait_ge(qf_out, 4 * h + 4)
                            dve.wait_ge(exp_ready, ebase + 3)
                            nc.vector.tensor_tensor(QE[0][:, :], q[h % 2][:, :], inv4[:, :], ALU.mult).then_inc(q_lev, 1)
                            nc.vector.tensor_tensor(QS[:, :], q[h % 2][:, :], eb[:, :], ALU.mult).then_inc(q_lev, 1)
                        else:
                            size = LEVELS[j - 1]
                            dve.wait_ge(exp_ready, ebase + 3 + j)
                            up = slice(size // 2, size)
                            nc.vector.tensor_tensor(blocks(QE[j][:, :], size)[:, :, up], blocks(q[h % 2][:, 0:SEQ], size)[:, :, up],
                                                    blocks(diff[j % 2][:, 0:SEQ], size)[:, :, up], ALU.mult).then_inc(q_lev, 1)
                    dve.wait_ge(q_lev, (NLEV + 2) * h + 2)
                    nc.vector.tensor_copy(QBd, blocks(QS[:, SEQ:TOK], DEC_T)).then_inc(q_lev, 1)

                def matrices(h):
                    if h:
                        dve.wait_ge(o_done, h)
                    for i in range(NLEV):
                        dve.wait_ge(att_done, (NLEV + 1) * h + i + 1)
                        nc.vector.copy_predicated(A[:, :, :], bcast(k.levelmask[:, i, :].bitcast(I32), 1, [P, PT, P]),
                                                  k.ps[3 + i % 2][:, :].rearrange("p (c n) -> p c n", c=PT)).then_inc(att_taken, 1)
                        dve.wait_ge(att_taken, (NLEV + 1) * h + i + 1)
                    dve.wait_ge(att_done, (NLEV + 1) * (h + 1))
                    nc.vector.copy_predicated(AS[:, :], k.levelmask[0:SMP, 0, 0:SMP].bitcast(I32), k.ps[7][0:SMP, 0:SMP])\
                        .then_inc(att_taken, 1)
                    dve.wait_ge(ds_done, h + 1)
                    if h:
                        dve.wait_ge(s_store[0], 16 * h)
                    for c in range(PT):
                        new, step = S[h % 2][:, c, :], k.ps[5][:, c * P:(c + 1) * P]
                        if c == 0:
                            nc.vector.tensor_copy(new, step).then_inc(s_ready, 1)
                        else:
                            dve.wait_ge(s_ready, PT * h + c)
                            nc.vector.scalar_tensor_tensor(out=new, in0=S[h % 2][:, c - 1, :],
                                                           scalar=eb[:, c * P + P - 1:c * P + P], in1=step,
                                                           op0=ALU.mult, op1=ALU.add).then_inc(s_ready, 1)
                    dve.wait_ge(sds_done, h + 1)
                    dve.wait_ge(sn_scaled, h + 1)
                    for i in range(2):
                        part = sn[h % 2][:, 4 * i:4 * i + 4, :]
                        nc.vector.tensor_tensor(part, part, k.ps[3 + i][:, :].rearrange("p (c n) -> p c n", c=4), ALU.add)\
                            .then_inc(sn_ready, 1)

                elementwise(0)
                for h in range(1, HEADS):
                    matrices(h - 1)
                    elementwise(h)
                for i in range(2):
                    for t in range(NT):
                        dve.wait_ge(g_out, NT * i + t + 1)
                        gv = g[0:rows(t), t, i * HB:(i + 1) * HB].rearrange("p (h n) -> p h n", n=P)
                        nc.vector.tensor_tensor(gv, gv, bcast(gnorm[0:rows(t), :], 1, [rows(t), 4, P]), ALU.mult)
                matrices(HEADS - 1)
                k.order_n["vector"] = ch.n

            @block.gpsimd
            def _(pool):
                for h in range(HEADS):
                    ebase = (NLEV + 3) * h
                    if h:
                        pool.wait_ge(att_done, (NLEV + 1) * h)
                    for j in range(NLEV):
                        pool.wait_ge(exp_ready, ebase + (2 if j == 0 else 3 + j))
                        if j == 0:
                            pool.wait_ge(kk_ready, h + 1)
                            nc.gpsimd.tensor_tensor(KE[0][:, :], kk[:, :], diff[0][:, :], ALU.mult).then_inc(k_lev, 1)
                        else:
                            size = LEVELS[j - 1]
                            lo = slice(0, size // 2)
                            nc.gpsimd.tensor_tensor(blocks(KE[j][:, :], size)[:, :, lo], blocks(kk[:, 0:SEQ], size)[:, :, lo],
                                                    blocks(diff[j % 2][:, 0:SEQ], size)[:, :, lo], ALU.mult).then_inc(k_lev, 1)
                    pool.wait_ge(q_lev, (NLEV + 2) * h + 1)
                    pool.wait_ge(exp_ready, ebase + 3 + NLEV)
                    nc.gpsimd.tensor_tensor(kd[:, :], kk[:, :], diff[NLEV % 2][:, :], ALU.mult).then_inc(k_lev, 1)
                    pool.wait_ge(v_out, 2 * NT)
                    if h == 0:
                        pool.wait_ge(zero_made, 1)
                    if h:
                        pool.wait_ge(sds_done, h)
                    nc.gpsimd.tensor_tensor(vm[:, :, :], bcast(v[0:SMP, PT, head(h)], 1, [SMP, DEC_B, P]),
                                            bcast(k.batchmask[:, :], 2, [SMP, DEC_B, P]), ALU.mult).then_inc(vm_ready, 1)
                    pool.wait_ge(s0_in[h % 2], 16 * (h // 2 + 1))
                    if h:
                        pool.wait_ge(sn_store[0], 16 * h)
                    ends = blocks(eb[:, SEQ:TOK], DEC_T)[:, :, DEC_T - 1]
                    nc.gpsimd.tensor_tensor(sn[h % 2][:, :, :], s0[h % 2][:, :, :], bcast(ends, 2, [P, DEC_B, P]), ALU.mult)\
                        .then_inc(sn_scaled, 1)

            @block.tensor
            def _(pe):
                def begin(u):
                    if before[u] is not None:
                        pe.wait_ge(*evacuated[before[u]])
                    return k.ps[units[u][1]]

                def by_token(u, w):
                    project_tokens(nc, begin(u), k.xT, w, u[2]).then_inc(proj_done, 1)

                def by_feature(h, w):
                    if h % 2 == 0:
                        project_tokens(nc, begin(("s", h // 2)), k.xT, w, PT).then_inc(proj_done, 1)
                    for kind, off in (("f", 2 * P), ("q", 0)):
                        bank = begin((kind, h))
                        for c in range(DC):
                            lhsT = w[:, c, off + (h % 2) * P:off + (h % 2) * P + P]
                            last = nc.tensor.matmul(bank[:, :], lhsT, k.xT[:, c, 0:SEQ], start=(c == 0), stop=(c == DC - 1))
                        last.then_inc(proj_done, 1)

                def gla(h):
                    pe.wait_ge(v_out, 2 * NT)
                    pe.wait_ge(k_lev, (NLEV + 1) * (h + 1))
                    pe.wait_ge(q_lev, (NLEV + 2) * (h + 1))
                    if h:
                        pe.wait_ge(s_ready, PT * h)
                        pe.wait_ge(o_out, 2 * h)
                        pe.wait_ge(sn_ready, 2 * h)
                    for c in range(PT):
                        nc.tensor.transpose(k.ps[5][:, c * P:(c + 1) * P], kd[:, c * P:(c + 1) * P], k.ident[:, :])
                    nc.tensor.transpose(k.ps[6][0:SMP, P:2 * P], kd[:, SEQ:TOK], k.ident[:, :]).then_inc(turned, 1)
                    for i in range(NLEV):
                        if i >= 2:
                            pe.wait_ge(att_taken, (NLEV + 1) * h + i - 1)
                        for c in range(PT):
                            part = slice(c * P, (c + 1) * P)
                            last = nc.tensor.matmul(k.ps[3 + i % 2][:, part], KE[i][:, part], QE[i][:, part], start=True, stop=True)
                        last.then_inc(att_done, 1)
                    nc.tensor.matmul(k.ps[7][0:SMP, 0:SMP], KE[0][:, SEQ:TOK], QE[0][:, SEQ:TOK], start=True, stop=True)\
                        .then_inc(att_done, 1)
                    pe.wait_ge(turned_out, 2 * (h + 1))
                    for c in range(PT):
                        last = nc.tensor.matmul(k.ps[5][:, c * P:(c + 1) * P], kdT[:, c, :], v[:, c, head(h)], start=True, stop=True)
                    last.then_inc(ds_done, 1)
                    pe.wait_ge(att_taken, (NLEV + 1) * (h + 1))
                    pe.wait_ge(vm_ready, h + 1)
                    for i in range(2):
                        last = nc.tensor.matmul(k.ps[3 + i][:, :], kdTs[:, :], vm[:, 4 * i:4 * i + 4, :], start=True, stop=True)
                    last.then_inc(sds_done, 1)
                    pe.wait_ge(s_ready, PT * (h + 1))
                    for c in range(PT):
                        out = k.ps[7][:, c * P:(c + 1) * P]
                        nc.tensor.matmul(out, A[:, c, :], v[:, c, head(h)], start=True, stop=(c == 0))
                        if c:
                            nc.tensor.matmul(out, QS[:, c * P:(c + 1) * P], S[h % 2][:, c - 1, :], start=False, stop=True)
                    out = k.ps[6][0:SMP, 2 * P:3 * P]
                    nc.tensor.matmul(out, AS[:, :], v[0:SMP, PT, head(h)], start=True, stop=False)
                    pe.wait_ge(s0_in[h % 2], 16 * (h // 2 + 1))
                    for bb in range(DEC_B):
                        last = nc.tensor.matmul(out, QB[:, bb * SMP:(bb + 1) * SMP], s0[h % 2][:, bb, :], start=False,
                                                stop=(bb == DEC_B - 1))
                    last.then_inc(o_done, 1)

                for i in range(2):
                    w = k.take_weights(pe)
                    for t in range(NT):
                        by_token(("v", i, t), w)
                    k.w_done.append((proj_done, units[("v", i, NT - 1)][0]))
                for h in range(HEADS):
                    if h % 2 == 0:
                        w = k.take_weights(pe)
                        k.w_done.append((proj_done, units[("q", h + 1)][0]))
                    by_feature(h, w)
                    if h % 2 == 0:
                        pe.wait_ge(s_copied, h // 2 + 1)
                        nc.tensor.transpose(k.ps[2][:, P:2 * P], smp_qf[:, :], k.ident[:, :]).then_inc(s_turned, 1)
                    if h in GATE_TILE_AT:
                        w_gate = k.take_weights(pe)
                        i = GATE_TILE_AT.index(h)
                        k.w_done.append((proj_done, units[("g", i, NT - 1)][0]))
                    for u in GATE_UNITS[h]:
                        by_token(u, w_gate)
                    if h:
                        gla(h - 1)
                for u in GATE_UNITS[HEADS]:
                    by_token(u, w_gate)
                gla(HEADS - 1)

            def store(sp, h):
                sp.wait_ge(s_ready, PT * (h + 1))
                sp.dma_start(a["state_prompt"][0, 0, h, :, :], S[h % 2][:, PT - 1, :]).then_inc(s_store[0], 16)
                sp.wait_ge(sn_ready, 2 * (h + 1))
                sp.dma_start(a["state_sample"][0, :, h, :, :].rearrange("b k v -> k b v"), sn[h % 2][:, :, :])\
                    .then_inc(sn_store[0], 16)

            @block.sync
            def _(sp):
                gate_tile = lambda i: column_halves(a["a_w_in"][0], 3 * D + i * HB)
                tiles = {0: [gate_tile(0), head_pair_halves(a, 1)], 2: [head_pair_halves(a, 2)],
                         4: [gate_tile(1), head_pair_halves(a, 3)]}
                for h in range(HEADS):
                    for tile in tiles.get(h, ()):
                        k.load_weights(sp, tile)
                    if h >= 2:
                        sp.wait_ge(sn_scaled, h - 1)
                        sp.wait_ge(o_done, h - 1)
                    sp.dma_start(s0[h % 2][:, :, :], a["state_hgrn"][0, :, h, :, :].rearrange("b k v -> k b v"))\
                        .then_inc(s0_in[h % 2], 16)
                    if h == 0:
                        sp.wait_ge(zero_made, 1)
                    for j in range(h * SLOTS // ZERO // HEADS, (h + 1) * SLOTS // ZERO // HEADS):
                        for x in slots:
                            sp.dma_start(x[j * ZERO:(j + 1) * ZERO, :], zero).then_inc(zeroed, 16)
                    if h >= 1:
                        store(sp, h - 1)
                for i in range(2):
                    k.load_weights(sp, column_halves(a["a_w_o"][0], i * HB))
                store(sp, HEADS - 1)
                sp.wait_ge(s_store[0], 16 * HEADS)
                sp.wait_ge(sn_store[0], 16 * HEADS)
                sp.wait_ge(zeroed, 16 * len(slots) * SLOTS // ZERO)



def mix_out_block(k, tag, o, gate, eps, prefetch=()):
    nc = k.nc
    squared, summed, mean = k.sem(f"{tag}_squared"), k.sem(f"{tag}_summed"), k.sem(f"{tag}_mean")
    seed, scaled, gated = k.sem(f"{tag}_seed"), k.sem(f"{tag}_scaled"), k.sem(f"{tag}_gated")
    turned, out_a, out_v = k.sem(f"{tag}_turned"), k.sem(f"{tag}_out_act"), k.sem(f"{tag}_out_dve")
    projected, added = k.sem(f"{tag}_projected"), k.sem(f"{tag}_added")
    half = DC // 2
    by_head = lambda ap: ap.rearrange("p (h n) -> p h n", n=P)
    with ExitStack() as tmp_ctx:
        def sb(name, shape):
            return tmp_ctx.enter_context(nc.sbuf_tensor(f"{tag}_{name}", shape, F32))
        sq = [sb(f"sq{i}", [P, D]) for i in range(2)]
        stats = sb("stats", [P, 5, NT, HEADS])
        flat = [stats[:, i, :, :].rearrange("p t h -> p (t h)") for i in range(5)]
        with nc.Block() as block:
            @block.scalar
            def _(act):
                for t in range(NT):
                    if t >= 2:
                        act.wait_ge(summed, t - 1)
                    nc.scalar.activation(sq[t % 2][:, :], o[:, t, :], ACT.Square).then_inc(squared, 1)
                act.wait_ge(mean, 1)
                nc.scalar.activation(flat[2], flat[1], ACT.Ln).then_inc(seed, 1)
                act.wait_ge(seed, 1)
                nc.scalar.activation(flat[3], flat[2], ACT.Exp, scale=-0.5).then_inc(seed, 1)
                for t in range(NT):
                    act.wait_ge(turned, t + 1)
                    src = k.ps[2 * (t % 2) + 1][:, :].rearrange("p (c n) -> p c n", c=half)[:, :, 0:rows(t)]
                    nc.scalar.activation(k.xT[:, half:DC, cols(t)], src, ACT.Copy).then_inc(out_a, 1)

            @block.vector
            def _(dve):
                ch = Chain(dve, k.order["vector"], k.order_n["vector"])
                for t in range(NT):
                    dve.wait_ge(squared, t + 1)
                    nc.vector.tensor_reduce(out=stats[:, 0, t, :], in_=by_head(sq[t % 2][:, :]), op=ALU.add, axis=AX.X)\
                        .then_inc(summed, 1)
                dve.wait_ge(summed, NT)
                nc.vector.tensor_scalar(flat[1], flat[0], 1.0 / P, eps, ALU.mult, ALU.add).then_inc(mean, 1)
                dve.wait_ge(mean, 1)
                inverse_root(dve, None, (seed, 2), ch, nc, flat[1], flat[3], flat[2], flat[4])
                for t in range(NT):
                    nc.vector.tensor_tensor(by_head(o[:, t, :]), by_head(o[:, t, :]),
                                            bcast(stats[:, 4, t, :], 2, [P, HEADS, P]), ALU.mult).then_inc(scaled, 1)
                for t in range(NT):
                    dve.wait_ge(turned, t + 1)
                    src = k.ps[2 * (t % 2)][:, :].rearrange("p (c n) -> p c n", c=half)[:, :, 0:rows(t)]
                    nc.vector.tensor_copy(k.xT[:, 0:half, cols(t)], src).then_inc(out_v, 1)
                for i in range(2):
                    for t in range(NT):
                        n = NT * i + t
                        dve.wait_ge(projected, n + 1)
                        for src, part in token_parts(k.ps[4 + n % 4], k.h, i, t):
                            last = nc.vector.tensor_tensor(part, part, src, ALU.add)
                        last.then_inc(added, 1)
                k.order_n["vector"] = ch.n

            @block.gpsimd
            def _(pool):
                for t in range(NT):
                    pool.wait_ge(scaled, t + 1)
                    nc.gpsimd.tensor_tensor(by_head(o[:, t, :]), by_head(o[:, t, :]), gate(t), ALU.mult).then_inc(gated, 1)

            @block.tensor
            def _(pe):
                for t in range(NT):
                    pe.wait_ge(gated, t + 1)
                    if t >= 2:
                        pe.wait_ge(out_v, t - 1)
                        pe.wait_ge(out_a, t - 1)
                    for c in range(DC):
                        last = nc.tensor.transpose(k.ps[2 * (t % 2) + c // half][:, (c % half) * P:(c % half) * P + rows(t)],
                                                   o[0:rows(t), t, c * P:(c + 1) * P], k.ident[0:rows(t), 0:rows(t)])
                    last.then_inc(turned, 1)
                for i in range(2):
                    w = k.take_weights(pe)
                    for t in range(NT):
                        n = NT * i + t
                        pe.wait_ge(out_v, t + 1)
                        pe.wait_ge(out_a, t + 1)
                        if n >= 4:
                            pe.wait_ge(added, n - 3)
                        project_tokens(nc, k.ps[4 + n % 4], k.xT, w, t).then_inc(projected, 1)
                    k.w_done.append((projected, NT * (i + 1)))

            if prefetch:
                @block.sync
                def _(sp):
                    for halves in prefetch:
                        k.load_weights(sp, halves)



def moe_blocks(k, a, layer, slots_x, slots_y, prefetch):
    nc = k.nc
    tag = f"moe{layer}"
    with ExitStack() as tmp_ctx:
        def sb(name, shape, dt=F32):
            return tmp_ctx.enter_context(nc.sbuf_tensor(f"{tag}_{name}", shape, dt))

        expert = sb("expert", [P, 2 * BLOCKS])
        expert_i = sb("expert_i", [1, BLOCKS + 1], I32)
        slot_i = sb("slot_i", [P, TOPK, NT], I32)
        gates = sb("gates", [P, TOPK, NT])
        column = k.cw[:, 3 + layer, :]
        buffers = ExpertBuffers(k, a, tag, layer, tmp_ctx, expert_i)
        with ExitStack() as route_ctx:
            xs = route_ctx.enter_context(nc.sbuf_tensor(f"{tag}_xs", [P, NT, D], F32))
            norm_block(k, f"{tag}n", [(column, k.xT)], xs)
            route_block(k, a, tag, layer, route_ctx, xs, slots_x, expert, expert_i, slot_i, gates, buffers)
        expert_block(k, a, tag, layer, buffers, slots_x, slots_y, expert_i, column, prefetch)
        combine_block(k, tag, tmp_ctx, slots_y, slot_i, gates)


def route_block(k, a, tag, layer, ctx, xs, slots_x, expert, expert_i, slot_i, gates, buffers):
    nc = k.nc

    def sb(name, shape, dt=F32):
        return ctx.enter_context(nc.sbuf_tensor(f"{tag}_{name}", shape, dt))

    E, G = EXPERTS, GROUPS
    COL = 32
    wr = sb("router", [P, DC, COL])
    logT = sb("logits_T", [P, TOK])
    sum4 = sb("sum4", [P, COL])
    tri, onesq = sb("tri", [P, P]), sb("onesq", [P, P])
    L = sb("logits", [P, NT, G + E])
    one = sb("one", [P, 3, NT, 4])
    work = sb("work", [P, 6, NT, E])
    hot = sb("hot", [P, TOPK, NT, E])
    both = sb("both", [P, NT, E])
    sc = sb("scalars", [P, 12, NT])
    counts = sb("counts", [P, 6, E])
    step_i, step = sb("step_i", [P, BLOCKS], I32), sb("step", [P, BLOCKS])
    big = sb("big", [P, BLOCKS, E])
    slot = sb("slot", [P, TOPK, NT])
    w_in, made, logit, copied = k.sem(f"{tag}_router_landed"), k.sem(f"{tag}_made"), k.sem(f"{tag}_logit"), k.sem(f"{tag}_copied")
    to_exp, exped, picked = k.sem(f"{tag}_to_exp"), k.sem(f"{tag}_exped"), k.sem(f"{tag}_picked")
    cleared, blocks_ready = k.sem(f"{tag}_router_cleared"), k.sem(f"{tag}_blocks_ready")
    rows_started = k.sem(f"{tag}_rows_started")
    placed, slots_ready, sent = k.sem(f"{tag}_placed"), k.sem(f"{tag}_slots_ready"), k.sem(f"{tag}_sent")
    flat = lambda ap: ap.rearrange("p t e -> p (t e)")
    with nc.Block() as block:
        @block.sync
        def _(sp):
            wv = lambda x: x.rearrange("(c p) n -> p c n", p=P)
            sp.wait_ge(cleared, 1)
            sp.dma_start(wr[:, :, 0:G], wv(a["moe_w_group"][layer])).then_inc(w_in, 16)
            for gg in range(G):
                sp.dma_start(wr[:, :, G + EPG * gg:G + EPG * (gg + 1)], wv(a["moe_w_sub"][layer, gg])).then_inc(w_in, 16)
            sp.wait_ge(blocks_ready, 1)
            sp.wait_ge(rows_started, 1)
            e = buffers.expert(sp, 0)
            buffers.load_gate_up(sp, 0, e)
            buffers.load_down(sp, 0, e)

        @block.gpsimd
        def _(pool):
            ch = Chain(pool, k.order["gpsimd"], k.order_n["gpsimd"])
            nc.gpsimd.memset(onesq[:, :], 1.0)
            ch(nc.gpsimd.memset(tri[:, :], 1.0))
            ch(nc.gpsimd.affine_select(out=tri[:, :], in_=tri[:, :], compare_op=ALU.is_gt, fill=0.0, base=0,
                                       pattern=[[1, P]], channel_multiplier=-1))
            nc.gpsimd.iota(step_i[:, :], pattern=[[1, BLOCKS]], base=0, channel_multiplier=0).then_inc(made, 1)
            pool.wait_ge(made, 1)
            nc.gpsimd.tensor_copy(step[:, :], step_i[:, :]).then_inc(made, 1)
            ch(nc.gpsimd.memset(sum4[:, :], 0.0))
            for j in range(P // COL):
                ins = nc.gpsimd.affine_select(out=sum4[:, :], in_=sum4[:, :], compare_op=ALU.not_equal, fill=1.0,
                                              base=-COL * j, pattern=[[-1, COL]], channel_multiplier=1)
                ch(ins) if j < P // COL - 1 else ins.then_inc(made, 1)
            k.order_n["gpsimd"] = ch.n
            pool.wait_ge(slots_ready, 1)
            for j in range(TOPK):
                for t in range(NT):
                    pool.indirect_dma_start(slots_x, bass.IndirectOffsetOnAxis(ap=slot_i[0:rows(t), j, t:t + 1], axis=0),
                                            xs[0:rows(t), t, :], None).then_inc(sent, 16)
            pool.sem_inc(rows_started, 1)
            pool.wait_ge(sent, 16 * TOPK * NT)

        @block.tensor
        def _(pe):
            pe.wait_ge(w_in, 16 * (1 + G))
            for lo, hi, bank in ((0, SEQ, k.ps[0]), (SEQ, TOK, k.ps[2])):
                for c in range(DC):
                    j = c % 4
                    last = nc.tensor.matmul(bank[COL * j:COL * (j + 1), 0:hi - lo], wr[:, c, :], k.xT[:, c, lo:hi],
                                            start=(c < 4), stop=(c >= 4))
                last.then_inc(logit, 1)
            pe.wait_ge(copied, 2)
            pe.wait_ge(made, 3)
            for t in range(NT):
                last = nc.tensor.matmul(k.ps[3][0:rows(t), t * COL:(t + 1) * COL], logT[:, cols(t)], sum4[:, :],
                                        start=True, stop=True)
            last.then_inc(logit, 1)
            pe.wait_ge(picked, 1)
            every = both[:, :, :].rearrange("p t e -> p (t e)")
            nc.tensor.matmul(k.ps[1][:, 0:NT * E], tri[:, :], every, start=True, stop=True)
            nc.tensor.matmul(k.ps[1][:, NT * E:2 * NT * E], onesq[:, :], every, start=True, stop=True).then_inc(placed, 1)

        @block.scalar
        def _(act):
            act.wait_ge(to_exp, 1)
            nc.scalar.activation(work[:, 0, :, 0:G], work[:, 0, :, 0:G], ACT.Exp).then_inc(exped, 1)
            act.wait_ge(to_exp, 2)
            nc.scalar.activation(sc[:, 4, :], sc[:, 4, :], ACT.Exp).then_inc(exped, 1)

        @block.vector
        def _(dve):
            ch = Chain(dve, k.order["vector"], k.order_n["vector"])
            TT, TS = nc.vector.tensor_tensor, nc.vector.tensor_scalar
            full = lambda ap: bcast(ap, 2, [P, NT, 4])
            nc.vector.memset(wr[:, :, :], 0.0).then_inc(cleared, 1)
            ch(nc.vector.memset(L[:, :, :], 0.0))
            dve.wait_ge(logit, 1)
            nc.vector.tensor_copy(logT[:, 0:SEQ], k.ps[0][:, :]).then_inc(copied, 1)
            dve.wait_ge(logit, 2)
            nc.vector.tensor_copy(logT[:, SEQ:TOK], k.ps[2][:, 0:SMP]).then_inc(copied, 1)
            dve.wait_ge(logit, 3)
            by_tile = k.ps[3][:, 0:NT * COL].rearrange("p (t e) -> p t e", e=COL)
            ch(nc.vector.tensor_copy(L[:, 0:PT, :], by_tile[:, 0:PT, 0:G + E]))
            ch(nc.vector.tensor_copy(L[0:SMP, PT, :], by_tile[0:SMP, PT, 0:G + E]))

            def first_largest(values, top, out, room):
                ch(nc.vector.tensor_reduce(out=top, in_=values, op=ALU.max, axis=AX.X))
                ch(TT(out, values, full(top), ALU.is_equal))
                ch(nc.vector.tensor_copy(room, out[:, :, 0]))
                for e in range(1, 4):
                    ch(TT(sc[:, 11, :], out[:, :, e], room, ALU.mult))
                    ch(TT(out[:, :, e], out[:, :, e], sc[:, 11, :], ALU.subtract))
                    ch(TT(room, room, out[:, :, e], ALU.add))

            first_largest(L[:, :, 0:G], sc[:, 0, :], one[:, 0, :, :], sc[:, 10, :])
            TT(work[:, 0, :, 0:G], L[:, :, 0:G], full(sc[:, 0, :]), ALU.subtract).then_inc(to_exp, 1)
            ch(TT(work[:, 1, :, :].rearrange("p t (g e) -> p t g e", g=G), L[:, :, G:G + E].rearrange("p t (g e) -> p t g e", g=G),
                  bcast(one[:, 0, :, :], 3, [P, NT, G, EPG]), ALU.mult))
            ch(nc.vector.tensor_reduce(out=work[:, 2, :, 0:EPG], in_=work[:, 1, :, :].rearrange("p t (g e) -> p t e g", g=G),
                                       op=ALU.add, axis=AX.X))
            first_largest(work[:, 2, :, 0:EPG], sc[:, 1, :], one[:, 1, :, :], sc[:, 10, :])
            ch(nc.vector.scalar_tensor_tensor(out=work[:, 3, :, 0:EPG], in0=one[:, 1, :, :], scalar=-3e38,
                                              in1=work[:, 2, :, 0:EPG], op0=ALU.mult, op1=ALU.add))
            first_largest(work[:, 3, :, 0:EPG], sc[:, 2, :], one[:, 2, :, :], sc[:, 10, :])
            TT(sc[:, 4, :], sc[:, 2, :], sc[:, 1, :], ALU.subtract).then_inc(to_exp, 1)
            for j in range(TOPK):
                ch(TT(hot[:, j, :, :].rearrange("p t (g e) -> p t g e", g=G), bcast(one[:, 0, :, :], 3, [P, NT, G, EPG]),
                      bcast(one[:, 1 + j, :, :], 2, [P, NT, G, EPG]), ALU.mult))
            ch(TT(both[:, :, :], hot[:, 0, :, :], hot[:, 1, :, :], ALU.add))
            for q in range(1, 4):
                ch(nc.vector.memset(both[32 * q:32 * q + 32, PT, :], 0.0))
            dve.sem_inc(picked, 1)
            dve.wait_ge(exped, 2)
            ch(nc.vector.tensor_reduce(out=sc[:, 3, :], in_=work[:, 0, :, 0:G], op=ALU.add, axis=AX.X))
            ch(TS(sc[:, 5, :], sc[:, 4, :], 1.0, None, ALU.add))
            ch(TT(sc[:, 5, :], sc[:, 5, :], sc[:, 3, :], ALU.mult))
            ch(nc.vector.reciprocal(gates[:, 0, :], sc[:, 5, :]))
            ch(TT(gates[:, 1, :], gates[:, 0, :], sc[:, 4, :], ALU.mult))
            dve.wait_ge(placed, 1)
            totals = k.ps[1][:, NT * E:2 * NT * E].rearrange("p (t e) -> p t e", e=E)
            before = work[:, 0, :, :]
            ch(nc.vector.memset(before[:, 0, :], 0.0))
            for t in range(1, NT):
                ch(TT(before[:, t, :], before[:, t - 1, :], totals[:, t - 1, :], ALU.add))
            cnt = counts[:, 5, :]
            ch(TT(cnt, before[:, PT, :], totals[:, PT, :], ALU.add))
            ch(TT(before, before, k.ps[1][:, 0:NT * E].rearrange("p (t e) -> p t e", e=E), ALU.add))
            ch(TS(counts[:, 0, :], cnt, 0.0, None, ALU.is_gt))
            for i in range(1, NT):
                ch(nc.vector.scalar_tensor_tensor(out=counts[:, 0, :], in0=cnt, scalar=float(i * P), in1=counts[:, 0, :],
                                                  op0=ALU.is_gt, op1=ALU.add))
            ch(TS(counts[:, 1, :], counts[:, 0, :], 0.0, 1.0, ALU.mult, ALU.add))
            ch(nc.vector.tensor_tensor_scan(counts[:, 2, :], counts[:, 1, :], counts[:, 0, :], 0.0, ALU.mult, ALU.add))
            ch(TT(counts[:, 3, :], counts[:, 2, :], counts[:, 0, :], ALU.subtract))
            ch(nc.vector.scalar_tensor_tensor(out=work[:, 4, :, :], in0=bcast(counts[:, 3, :], 1, [P, NT, E]), scalar=float(P),
                                              in1=before,
                                              op0=ALU.mult, op1=ALU.add))
            for j in range(TOPK):
                ch(TT(work[:, 5, :, :], work[:, 4, :, :], hot[:, j, :, :], ALU.mult))
                ch(nc.vector.tensor_reduce(out=slot[:, j, :], in_=work[:, 5, :, :], op=ALU.add, axis=AX.X))
            ch(nc.vector.tensor_copy(slot_i[:, :, :], slot[:, :, :]))
            dve.sem_inc(slots_ready, 1)
            ch(TT(big[:, :, :], bcast(counts[:, 2, :], 1, [P, BLOCKS, E]), bcast(step[:, :], 2, [P, BLOCKS, E]), ALU.is_le))
            ch(nc.vector.tensor_reduce(out=expert[:, 0:BLOCKS], in_=big[:, :, :], op=ALU.add, axis=AX.X))
            ch(TS(expert[:, 0:BLOCKS], expert[:, 0:BLOCKS], float(E - 1), None, ALU.min))
            ch(TS(counts[:, 4, 0:BLOCKS // 2 - 2], step[:, 4:BLOCKS:2], counts[:, 2, E - 1:E], None, ALU.is_lt))
            ch(nc.vector.tensor_reduce(out=counts[:, 4, E - 1:E], in_=counts[:, 4, 0:BLOCKS // 2 - 2], op=ALU.add, axis=AX.X))
            ch(TS(expert[:, BLOCKS:BLOCKS + 1], counts[:, 4, E - 1:E], 1.0, None, ALU.add))
            nc.vector.tensor_copy(expert_i[:, :], expert[0:1, 0:BLOCKS + 1]).then_inc(blocks_ready, 1)
            k.order_n["vector"] = ch.n


class ExpertBuffers:

    def __init__(self, k, a, tag, layer, ctx, expert_i):
        sb = lambda name, shape: ctx.enter_context(k.nc.sbuf_tensor(f"{tag}_{name}", shape, F32))
        self.a, self.layer, self.expert_i, self.sb = a, layer, expert_i, sb
        self.WGU = [sb(f"wgu{i}", [P, 2, DC, FF]) for i in range(2)]
        self.WD = [sb(f"wd{i}", [P, FF // P, D]) for i in range(2)]
        self.gu_in = [k.sem(f"{tag}_gu_landed{i}") for i in range(2)]
        self.d_in = [k.sem(f"{tag}_down_landed{i}") for i in range(2)]

    def expert(self, sp, j):
        return sp.value_load(self.expert_i[0:1, bass.ds(j, 1)], min_val=0, max_val=EXPERTS - 1)

    def load_gate_up(self, sp, u, e):
        for n, w in enumerate((self.a["moe_w_gate"], self.a["moe_w_up"])):
            sp.dma_start(self.WGU[u][:, n, :, :], w[self.layer, bass.ds(e, 1), :, :].rearrange("a (c p) f -> p (a c) f", p=P))\
                .then_inc(self.gu_in[u], 16)

    def load_down(self, sp, u, e):
        sp.dma_start(self.WD[u][:, :, :], self.a["moe_w_down"][self.layer, bass.ds(e, 1), :, :].rearrange("a (c p) n -> p (a c) n", p=P))\
            .then_inc(self.d_in[u], 16)


def expert_block(k, a, tag, layer, buffers, slots_x, slots_y, expert_i, column, prefetch):
    nc, sb = k.nc, buffers.sb
    NB = 2
    FC = FF // P
    half = DC // 2
    X = [sb(f"x{i}", [P, D]) for i in range(NB)]
    WGU, WD, gu_in, d_in = buffers.WGU, buffers.WD, buffers.gu_in, buffers.d_in
    XT = [sb(f"xt{i}", [P, DC, P]) for i in range(NB)]
    SG = [sb(f"sg{i}", [P, FF]) for i in range(NB)]
    HT = [sb(f"ht{i}", [P, FC, P]) for i in range(NB)]
    Y = [sb(f"y{i}", [P, D]) for i in range(NB)]
    x_in = [k.sem(f"{tag}_x_landed{i}") for i in range(NB)]
    y_out = [k.sem(f"{tag}_y_stored{i}") for i in range(NB)]
    x_turned, xt_a, xt_v = k.sem(f"{tag}_x_turned"), k.sem(f"{tag}_xt_act"), k.sem(f"{tag}_xt_dve")
    gu_done, silu_done, hid_done = k.sem(f"{tag}_gu_done"), k.sem(f"{tag}_silu_done"), k.sem(f"{tag}_hid_done")
    h_turned, ht_done = k.sem(f"{tag}_h_turned"), k.sem(f"{tag}_ht_done")
    down_done, y_a, y_v = k.sem(f"{tag}_down_done"), k.sem(f"{tag}_y_act"), k.sem(f"{tag}_y_dve")
    STEPS = (BLOCKS - 2) // 2
    assert BLOCKS % 2 == 0 and BLOCKS >= 6

    def steps_in_use(eng):
        return eng.value_load(expert_i[0:1, BLOCKS:BLOCKS + 1], min_val=1, max_val=STEPS)

    def wait(eng, sem, value):
        if not isinstance(value, int) or value > 0:
            eng.wait_ge(sem, value)

    with nc.Block() as block:
        @block.sync
        def _(sp):
            def load(i, c):
                j, u = 2 * i + c, c % 2
                e = buffers.expert(sp, j)
                wait(sp, x_turned, j - 1)
                sp.dma_start(X[u][:, :], slots_x[bass.ds(j * P, P), :]).then_inc(x_in[u], 16)
                wait(sp, gu_done, j - 1)
                buffers.load_gate_up(sp, u, e)
                wait(sp, down_done, j - 1)
                buffers.load_down(sp, u, e)

            for u in range(NB):
                sp.dma_start(X[u][:, :], slots_x[u * P:(u + 1) * P, :]).then_inc(x_in[u], 16)
            e = buffers.expert(sp, 1)
            buffers.load_gate_up(sp, 1, e)
            buffers.load_down(sp, 1, e)
            steps = steps_in_use(sp)
            with sp.Fori(1, STEPS + 1) as i:
                with sp.If(i <= steps):
                    load(i, 0)
                    load(i, 1)
            for halves in prefetch:
                k.load_weights(sp, halves)

        @block.scalar
        def _(act):
            def turn_out(i, c):
                j, u = 2 * i + c, c % 2
                act.wait_ge(x_turned, j + 1)
                for n in range(half, DC):
                    nc.scalar.activation(XT[u][:, n, :], k.ps[1][:, (n - half) * P:(n - half + 1) * P], ACT.Copy,
                                         scale=column[:, n:n + 1]).then_inc(xt_a, 1)

            def silu(i, c):
                j, u = 2 * i + c, c % 2
                act.wait_ge(gu_done, j + 1)
                wait(act, h_turned, j - 1)
                nc.scalar.activation(SG[u][:, :], k.ps[2 + u][:, 0:FF], ACT.Silu).then_inc(silu_done, 1)

            def y_store(i, c):
                j, u = 2 * i + c, c % 2
                act.wait_ge(down_done, j + 1)
                wait(act, y_out[u], 16 * (i + c // 2))
                nc.scalar.activation(Y[u][:, HB:D], k.ps[6][:, :], ACT.Copy).then_inc(y_a, 1)
                act.wait_ge(y_v, j + 1)
                act.wait_ge(y_a, j + 1)
                act.dma_start(slots_y[bass.ds(j * P, P), :], Y[u][:, :]).then_inc(y_out[u], 16)

            def step(i, c, last=False):
                silu(i, c)
                if not last:
                    turn_out(i, c + 1)
                if not (isinstance(i, int) and 2 * i + c == 0):
                    y_store(i, c - 1)

            turn_out(0, 0)
            steps = steps_in_use(act)
            for c in range(3):
                step(0, c)
            with act.Fori(1, STEPS) as i:
                with act.If(i < steps):
                    step(i, 1)
                    step(i, 2)
            step(steps, 1, last=True)
            y_store(steps, 1)

        @block.vector
        def _(dve):
            def turn_out(i, c):
                j, u = 2 * i + c, c % 2
                dve.wait_ge(x_turned, j + 1)
                nc.vector.tensor_tensor(XT[u][:, 0:half, :], k.ps[0][:, :].rearrange("p (c n) -> p c n", c=half),
                                        bcast(column[:, 0:half], 2, [P, half, P]), ALU.mult).then_inc(xt_v, 1)

            def times_up(i, c):
                j, u = 2 * i + c, c % 2
                dve.wait_ge(silu_done, j + 1)
                nc.vector.tensor_tensor(SG[u][:, :], SG[u][:, :], k.ps[2 + u][:, FF:2 * FF], ALU.mult).then_inc(hid_done, 1)

            def y_half(i, c):
                j, u = 2 * i + c, c % 2
                dve.wait_ge(down_done, j + 1)
                wait(dve, y_out[u], 16 * (i + c // 2))
                nc.vector.tensor_copy(Y[u][:, 0:HB], k.ps[5][:, :]).then_inc(y_v, 1)

            def hidden_out(i, c):
                j, u = 2 * i + c, c % 2
                dve.wait_ge(h_turned, j + 1)
                nc.vector.tensor_copy(HT[u][:, :, :], k.ps[4][:, 0:FF].rearrange("p (c n) -> p c n", c=FC)).then_inc(ht_done, 1)

            def step(i, c, last=False):
                if not last:
                    turn_out(i, c + 1)
                times_up(i, c)
                if not (isinstance(i, int) and 2 * i + c == 0):
                    y_half(i, c - 1)
                hidden_out(i, c)

            turn_out(0, 0)
            steps = steps_in_use(dve)
            for c in range(3):
                step(0, c)
            with dve.Fori(1, STEPS) as i:
                with dve.If(i < steps):
                    step(i, 1)
                    step(i, 2)
            step(steps, 1, last=True)
            y_half(steps, 1)

        @block.tensor
        def _(pe):
            def turn_x(i, c):
                j, u = 2 * i + c, c % 2
                pe.wait_ge(x_in[u], 16 * (i + c // 2 + 1))
                wait(pe, xt_a, half * j)
                wait(pe, xt_v, j)
                for n in range(DC):
                    last = nc.tensor.transpose(k.ps[n // half][:, (n % half) * P:(n % half + 1) * P],
                                               X[u][:, n * P:(n + 1) * P], k.ident[:, :])
                last.then_inc(x_turned, 1)

            def gate_up(i, c):
                j, u = 2 * i + c, c % 2
                pe.wait_ge(gu_in[u], 32 * (i + c // 2 + 1))
                pe.wait_ge(xt_a, half * (j + 1))
                pe.wait_ge(xt_v, j + 1)
                wait(pe, hid_done, j - 1)
                for n in range(DC):
                    last = nc.tensor.matmul(k.ps[2 + u][:, :].rearrange("p (w f) -> p w f", w=2), XT[u][:, n, :],
                                            WGU[u][:, :, n, :], start=(n == 0), stop=(n == DC - 1))
                last.then_inc(gu_done, 1)

            def down(i, c):
                j, u = 2 * i + c, c % 2
                pe.wait_ge(d_in[u], 16 * (i + c // 2 + 1))
                pe.wait_ge(ht_done, j + 1)
                wait(pe, y_a, j)
                wait(pe, y_v, j)
                for b in range(2):
                    for n in range(FC):
                        last = nc.tensor.matmul(k.ps[5 + b][:, :], HT[u][:, n, :], WD[u][:, n, b * HB:(b + 1) * HB],
                                                start=(n == 0), stop=(n == FC - 1))
                last.then_inc(down_done, 1)

            def turn_hidden(i, c):
                j, u = 2 * i + c, c % 2
                pe.wait_ge(hid_done, j + 1)
                wait(pe, ht_done, j)
                for n in range(FC):
                    last = nc.tensor.transpose(k.ps[4][:, n * P:(n + 1) * P], SG[u][:, n * P:(n + 1) * P], k.ident[:, :])
                last.then_inc(h_turned, 1)

            def step(i, c, last=False):
                gate_up(i, c)
                if not last:
                    turn_x(i, c + 1)
                if not (isinstance(i, int) and 2 * i + c == 0):
                    down(i, c - 1)
                turn_hidden(i, c)

            turn_x(0, 0)
            steps = steps_in_use(pe)
            for c in range(3):
                step(0, c)
            with pe.Fori(1, STEPS) as i:
                with pe.If(i < steps):
                    step(i, 1)
                    step(i, 2)
            step(steps, 1, last=True)
            down(steps, 1)
            for u in range(2):
                pe.wait_ge(y_out[u], 16 * (steps + 1))


def combine_block(k, tag, ctx, slots_y, slot_i, gates):
    nc = k.nc
    rows_in = [ctx.enter_context(nc.sbuf_tensor(f"{tag}_gathered{i}", [P, D], F32)) for i in range(4)]
    landed = [k.sem(f"{tag}_gathered{i}") for i in range(4)]
    added = k.sem(f"{tag}_added")
    with nc.Block() as block:
        @block.gpsimd
        def _(pool):
            for t in range(NT):
                for j in range(TOPK):
                    n = TOPK * t + j
                    if n >= 4:
                        pool.wait_ge(added, n - 3)
                    pool.indirect_dma_start(rows_in[n % 4][0:rows(t), :], None, slots_y,
                                            bass.IndirectOffsetOnAxis(ap=slot_i[0:rows(t), j, t:t + 1], axis=0))\
                        .then_inc(landed[n % 4], 16)

        @block.vector
        def _(dve):
            for t in range(NT):
                for j in range(TOPK):
                    n = TOPK * t + j
                    dve.wait_ge(landed[n % 4], 16 * (n // 4 + 1))
                    if n:
                        dve.wait_ge(added, n)
                    part = k.h[0:rows(t), t, :]
                    nc.vector.scalar_tensor_tensor(out=part, in0=rows_in[n % 4][0:rows(t), :], scalar=gates[0:rows(t), j, t:t + 1],
                                                   in1=part, op0=ALU.mult, op1=ALU.add).then_inc(added, 1)



def kvq_block(k, a, kv_xT, q_xT, ks, v, kT, qT, o, smp_q):
    nc = k.nc
    done, out_v, out_a = k.sem("kvq_done"), k.sem("kvq_out_dve"), k.sem("kvq_out_act")
    turned, kt_out = k.sem("kT_turned"), k.sem("kT_out")
    qs_copied, qs_turned = k.sem("sample_q_copied"), k.sem("sample_q_turned")
    stored = k.sem("kv_stored")
    order = [("k", i, t) for i in range(2) for t in range(NT)]
    for h in range(HEADS):
        order += ([("qs", h // 4)] if h % 4 == 0 else []) + [("q", h)]
    order += [("v", i, t) for i in range(2) for t in range(NT)]
    count = {u: n + 1 for n, u in enumerate(order)}
    nv, outs = 0, {}
    for u in order:
        if u[0] == "qs":
            outs[u] = (out_a, 10 * u[1] + 4)
        elif u[0] == "q":
            outs[u] = (out_a, 10 * (u[1] // 4) + 2 * (u[1] % 4 + 1) + (2 if u[1] % 4 else 0))
        else:
            nv += 1
            outs[u] = (out_v, nv)
    bank_of, before, last_in, n = {}, {}, {}, 0
    for u in order:
        if u[0] == "q":
            bank_of[u] = 2 + u[1] % 2
        elif u[0] == "qs":
            bank_of[u] = 4
        else:
            bank_of[u] = n % 2
            n += 1
        before[u] = last_in.get(bank_of[u])
        last_in[bank_of[u]] = u
    with nc.Block() as block:
        @block.tensor
        def _(pe):
            def begin(u):
                if before[u] is not None:
                    pe.wait_ge(*outs[before[u]])
                return k.ps[bank_of[u]]

            def by_token(kind):
                for i in range(2):
                    w = k.take_weights(pe)
                    for t in range(NT):
                        project_tokens(nc, begin((kind, i, t)), kv_xT, w, t).then_inc(done, 1)
                    k.w_done.append((done, count[(kind, i, NT - 1)]))

            by_token("k")
            for h in range(HEADS):
                if h % 4 == 0:
                    w = k.take_weights(pe)
                    k.w_done.append((done, count[("q", h + 3)]))
                    project_tokens(nc, begin(("qs", h // 4)), q_xT, w, PT).then_inc(done, 1)
                bank = begin(("q", h))
                for c in range(DC):
                    last = nc.tensor.matmul(bank[:, :], w[:, c, (h % 4) * P:(h % 4 + 1) * P], q_xT[:, c, 0:SEQ],
                                            start=(c == 0), stop=(c == DC - 1))
                last.then_inc(done, 1)
                if h % 4 == 0:
                    pe.wait_ge(qs_copied, h // 4 + 1)
                    nc.tensor.transpose(k.ps[4][:, P:2 * P], smp_q[:, :], k.ident[:, :]).then_inc(qs_turned, 1)
            pe.wait_ge(out_v, 2 * NT)
            for h in range(HEADS):
                if h:
                    pe.wait_ge(kt_out, 2 * h)
                for t in range(PT):
                    nc.tensor.transpose(k.ps[5][:, t * P:(t + 1) * P], ks[:, t, h * P:(h + 1) * P], k.ident[:, :])
                nc.tensor.transpose(k.ps[6][:, 0:SMP], ks[0:SMP, PT, h * P:(h + 1) * P], k.ident[0:SMP, 0:SMP]).then_inc(turned, 1)
            by_token("v")

        @block.sync
        def _(sp):
            for i in range(1, 2):
                k.load_weights(sp, column_halves(a["b_w_q"][0], i * HB))
            k.load_weights(sp, column_halves(a["w_kv"], D))
            k.load_weights(sp, column_halves(a["w_kv"], D + HB))

            def store(src, prompt, sample):
                sp.dma_start(a[prompt][0].rearrange("(t p) h n -> p t (h n)", p=P), src[:, 0:PT, :]).then_inc(stored, 16)
                sp.dma_start(a[sample].rearrange("b t h n -> (b t) (h n)"), src[0:SMP, PT, :]).then_inc(stored, 16)

            sp.wait_ge(out_v, 2 * NT)
            store(ks, "k_prompt", "k_sample")
            for i in range(2):
                k.load_weights(sp, column_halves(a["b_w_o"][0], i * HB))
            sp.wait_ge(out_v, 4 * NT)
            store(v, "v_prompt", "v_sample")
            sp.wait_ge(stored, 64)

        @block.vector
        def _(dve):
            for q in range(1, 4):
                nc.vector.memset(o[32 * q:32 * q + 32, PT, :], 0.0)
            for c in range(2):
                nc.vector.memset(qT[1 - c][c * P // 2:(c + 1) * P // 2, :, :], 0.0)
            for kind, dst in (("k", ks), ("v", v)):
                for i in range(2):
                    for t in range(NT):
                        dve.wait_ge(done, count[(kind, i, t)])
                        for src, part in token_parts(k.ps[bank_of[(kind, i, t)]], dst, i, t):
                            last = nc.vector.tensor_copy(part, src)
                        last.then_inc(out_v, 1)
                if kind == "k":
                    for i in range(2):
                        dve.wait_ge(done, count[("qs", i)])
                        if i:
                            dve.wait_ge(qs_turned, i)
                        nc.vector.tensor_copy(smp_q[:, :], k.ps[4][:, 0:P]).then_inc(qs_copied, 1)

        @block.scalar
        def _(act):
            for h in range(HEADS):
                act.wait_ge(done, count[("q", h)])
                for c in range(2):
                    rows_c = slice(c * P // 2, (c + 1) * P // 2)
                    nc.scalar.activation(qT[c][rows_c, h, 0:SEQ], k.ps[bank_of[("q", h)]][rows_c, :], ACT.Copy, scale=0.125)\
                        .then_inc(out_a, 1)
                if h % 4 == 0:
                    act.wait_ge(qs_turned, h // 4 + 1)
                    for c in range(2):
                        rows_c = slice(c * P // 2, (c + 1) * P // 2)
                        nc.scalar.activation(qT[c][rows_c, h:h + 4, SEQ:TOK],
                                             k.ps[4][rows_c, P:2 * P].rearrange("p (h n) -> p h n", n=SMP), ACT.Copy,
                                             scale=0.125).then_inc(out_a, 1)
            for h in range(HEADS):
                act.wait_ge(turned, h + 1)
                nc.scalar.activation(kT[:, h, 0:SEQ], k.ps[5][:, :], ACT.Copy).then_inc(kt_out, 1)
                nc.scalar.activation(kT[:, h, SEQ:TOK], k.ps[6][:, 0:SMP], ACT.Copy).then_inc(kt_out, 1)



def prompt_attention(k, a, rep, v, kT, qT, qz, kTs, o):
    nc = k.nc
    units = [(h, i) for h in range(HEADS) for i in range(PT)]
    N = len(units)
    half = P // 2
    NS = DC // 2
    with ExitStack() as tmp_ctx:
        def sb(name, shape):
            return tmp_ctx.enter_context(nc.sbuf_tensor(name, shape, F32))
        dist = sb("pa_dist", [P, SEQ])
        bias = [sb(f"pa_bias{i}", [P, SEQ]) for i in range(2)]
        spare = k.xT[:, :, :].rearrange("p c n -> p (c n)")
        S = [spare[:, i * 2 * SEQ:(i + 1) * 2 * SEQ].rearrange("p (c n) -> p c n", c=2) for i in range(NS)]
        aT = [sb(f"pa_at{i}", [P, PT, P]) for i in range(2)]
        st = [sb(f"pa_stat{i}", [P, 10]) for i in range(NS)]
        d_in, bias_ready = k.sem("pa_dist_landed"), k.sem("pa_bias")
        scored, biased, negated, exped = k.sem("pa_scored"), k.sem("pa_biased"), k.sem("pa_negated"), k.sem("pa_exp")
        combined, turned, at_out, o_done, o_out = (k.sem(f"pa_{n}") for n in ("combined", "turned", "at_out", "o_done", "o_out"))
        with nc.Block() as block:
            @block.sync
            def _(sp):
                sp.dma_start(dist[:, :], a["const_dist"]).then_inc(d_in, 16)

            @block.gpsimd
            def _(pool):
                pool.wait_ge(d_in, 16)
                for h in range(HEADS):
                    if h >= 2:
                        pool.wait_ge(biased, 2 * PT * (h - 1))
                    nc.gpsimd.tensor_scalar(bias[h % 2][:, :], dist[:, :], -(2.0 ** -(h + 1)), None, ALU.mult).then_inc(bias_ready, 1)

            @block.tensor
            def _(pe):
                def scores(n):
                    h, i = units[n]
                    w = (i + 1) * P
                    if n >= 2:
                        pe.wait_ge(biased, 2 * (n - 1))
                    for c in range(2):
                        last = nc.tensor.matmul(k.ps[2 * (n % 2) + c][:, 0:w], qT[c][:, h, i * P:(i + 1) * P], kT[:, h, 0:w],
                                                start=True, stop=True)
                        last.then_inc(scored, 1)

                def turn(n):
                    h, i = units[n]
                    pe.wait_ge(combined, n + 1)
                    if n >= 2:
                        pe.wait_ge(at_out, n - 1)
                    for j in range(i + 1):
                        last = nc.tensor.transpose(k.ps[4 + n % 2][:, j * P:(j + 1) * P], S[n % NS][:, 0, j * P:(j + 1) * P], k.ident[:, :])
                    last.then_inc(turned, 1)

                def values(n):
                    h, i = units[n]
                    pe.wait_ge(at_out, n + 1)
                    if n >= 2:
                        pe.wait_ge(o_out, n - 1)
                    for j in range(i + 1):
                        last = nc.tensor.matmul(k.ps[6 + n % 2][:, 0:P], aT[n % 2][:, j, :], v[:, j, h * P:(h + 1) * P],
                                                start=(j == 0), stop=(j == i))
                    last.then_inc(o_done, 1)

                scores(0)
                scores(1)
                for n in range(N):
                    if n + 2 < N:
                        scores(n + 2)
                    turn(n)
                    if n:
                        values(n - 1)
                values(N - 1)

            @block.vector
            def _(dve):
                ch = Chain(dve, k.order["vector"], k.order_n["vector"])
                ch(nc.vector.memset(qz[:, :, :, :], 0.0))
                for c in range(2):
                    part = slice(c * half, (c + 1) * half)
                    ch(nc.vector.tensor_copy(qz[part, :, :, c * DEC_T:(c + 1) * DEC_T],
                                             qT[c][part, :, SEQ:TOK].rearrange("p h (b t) -> p b h t", t=DEC_T)))
                ch(nc.vector.tensor_copy(kTs[:, :, :], kT[:, :, SEQ:TOK]))

                def bias_max(n):
                    h, i = units[n]
                    w = (i + 1) * P
                    dve.wait_ge(bias_ready, h + 1)
                    if n >= NS:
                        dve.wait_ge(turned, n - NS + 1)
                    for c in range(2):
                        dve.wait_ge(scored, 2 * n + c + 1)
                        nc.vector.tensor_tensor_reduce(out=S[n % NS][:, c, 0:w], in0=k.ps[2 * (n % 2) + c][:, 0:w],
                                                       in1=bias[h % 2][:, (PT - 1 - i) * P:SEQ], scale=1.0, scalar=-3e38,
                                                       op0=ALU.add, op1=ALU.max,
                                                       accum_out=st[n % NS][:, c:c + 1]).then_inc(biased, 1)
                    dve.wait_ge(biased, 2 * (n + 1))
                    nc.vector.tensor_scalar(st[n % NS][:, 2:4], st[n % NS][:, 0:2], -1.0, None, ALU.mult).then_inc(negated, 1)

                def combine(n):
                    h, i = units[n]
                    w = (i + 1) * P
                    s = st[n % NS]
                    dve.wait_ge(exped, 2 * (n + 1))
                    ch(nc.vector.reciprocal(s[:, 6:8], s[:, 4:6]))
                    ch(nc.vector.tensor_tensor(s[:, 8:9], s[:, 7:8], rep[:, 2 * P:2 * P + 1], ALU.mult))
                    ch(nc.vector.tensor_scalar(S[n % NS][:, 1, 0:w], S[n % NS][:, 1, 0:w], s[:, 8:9], None, ALU.mult))
                    nc.vector.scalar_tensor_tensor(out=S[n % NS][:, 0, 0:w], in0=S[n % NS][:, 0, 0:w], scalar=s[:, 6:7],
                                                   in1=S[n % NS][:, 1, 0:w], op0=ALU.mult, op1=ALU.add).then_inc(combined, 1)

                bias_max(0)
                for n in range(N):
                    if n + 1 < N:
                        bias_max(n + 1)
                    combine(n)
                k.order_n["vector"] = ch.n

            @block.scalar
            def _(act):
                def exps(n):
                    h, i = units[n]
                    w = (i + 1) * P
                    act.wait_ge(negated, n + 1)
                    for c in range(2):
                        nc.scalar.activation(S[n % NS][:, c, 0:w], S[n % NS][:, c, 0:w], ACT.Exp, bias=st[n % NS][:, 2 + c:3 + c],
                                             accum_out=st[n % NS][:, 4 + c:5 + c]).then_inc(exped, 1)

                def turned_out(n):
                    h, i = units[n]
                    act.wait_ge(turned, n + 1)
                    nc.scalar.activation(aT[n % 2][:, 0:i + 1, :], k.ps[4 + n % 2][:, 0:(i + 1) * P].rearrange("p (j n) -> p j n", n=P),
                                         ACT.Copy).then_inc(at_out, 1)

                def out(n):
                    h, i = units[n]
                    act.wait_ge(o_done, n + 1)
                    nc.scalar.activation(o[:, i, h * P:(h + 1) * P], k.ps[6 + n % 2][:, 0:P], ACT.Copy).then_inc(o_out, 1)

                exps(0)
                for n in range(N):
                    if n + 1 < N:
                        exps(n + 1)
                    turned_out(n)
                    if n:
                        out(n - 1)
                out(N - 1)



def sample_attention(k, a, rep, qz, kTs, o):
    nc = k.nc
    HT = HEADS * DEC_T
    QUAD = 32
    KRING, VRING, GROUP = 4, 8, 4
    GROUPS_ = PAGES // GROUP
    KEYS = PAST + DEC_T
    N5 = GROUPS_ + 1
    half = HEADS // 2
    with ExitStack() as tmp_ctx:
        def sb(name, shape, dt=F32):
            return tmp_ctx.enter_context(nc.sbuf_tensor(name, shape, dt))
        pt = sb("sa_pages", [1, DEC_B * PAGES], I32)
        K = k.wring[k.w_issued % WEIGHT_SLOTS][:, :, :].rearrange("p (r c) n -> p r (c n)", r=KRING)
        V = [sb(f"sa_v{i}", [P, D]) for i in range(VRING)]
        KT = sb("sa_kT", [P, HEADS, GROUP * P])
        S = sb("sa_scores", [P, KEYS])
        W = sb("sa_w", [P, KEYS])
        alibi = sb("sa_alibi", [P, KEYS])
        table = sb("sa_table", [P, 2 + HEADS + DEC_B * SMP])
        red = sb("sa_red", [P, 16])
        AT = sb("sa_at", [P, PAGES + 1, HT])
        Q = sb("sa_q", [P, HEADS, QUAD])
        knew, vnew = sb("sa_knew", [P, HEADS, DEC_T]), sb("sa_vnew", [P, D])
        place = sb("sa_place", [P, SMP])
        own = sb("sa_own", [P, D])
        own_head = table[:, 2:2 + HEADS]
        places = table[:, 2 + HEADS:].rearrange("p (b n) -> p b n", b=DEC_B)
        c_in = k.sem("sa_const_landed")
        k_in, v_in = [k.sem(f"sa_k_landed{i}") for i in range(KRING)], [k.sem(f"sa_v_landed{i}") for i in range(VRING)]
        vn_in = k.sem("sa_vnew_landed")
        names = ("cleared", "turned_a", "turned_b", "kt_out_a", "kt_out_b", "q_ready", "scored", "biased", "max_ready",
                 "exped", "normed", "w_turned", "at_out", "valued", "picked", "place_ready", "summed", "added")
        (cleared, turned_a, turned_b, kt_out_a, kt_out_b, q_ready, scored, biased, max_ready, exped, normed, w_turned,
         at_out, valued, picked, place_ready, summed, added) = (k.sem(f"sa_{n}") for n in names)

        def wait(eng, sem, value):
            if not isinstance(value, int) or value > 0:
                eng.wait_ge(sem, value)

        with nc.Block() as block:
            @block.sync
            def _(sp):
                sp.dma_start(pt[:, :], a["page_table"].rearrange("(x b) n -> x (b n)", x=1)).then_inc(c_in, 16)
                sp.dma_start(alibi[:, :], a["const_rows"][:, 0:KEYS]).then_inc(c_in, 16)
                sp.dma_start(table[:, :], a["const_rows"][:, KEYS:]).then_inc(c_in, 16)
                sp.wait_ge(c_in, 48)
                sp.wait_ge(cleared, 3)

                def load_k(b, p):
                    page = sp.value_load(pt[0:1, bass.ds(b * PAGES + p, 1)], min_val=0, max_val=a["cache_k"].shape[0] - 1)
                    wait(sp, turned_b, PAGES * b + p - KRING + 1)
                    sp.dma_start(K[:, p % KRING, :], a["cache_k"][bass.ds(page, 1), :, :, :].rearrange("a p h n -> (a p) (h n)"))\
                        .then_inc(k_in[p % KRING], 16)

                def load_v(b, g, valued_before):
                    for p in range(GROUP * g, GROUP * (g + 1)):
                        page = sp.value_load(pt[0:1, bass.ds(b * PAGES + p, 1)], min_val=0, max_val=a["cache_k"].shape[0] - 1)
                        wait(sp, valued, valued_before)
                        sp.dma_start(V[p % VRING][:, :], a["cache_v"][bass.ds(page, 1), :, :, :].rearrange("a p h n -> (a p) (h n)"))\
                            .then_inc(v_in[p % VRING], 16)

                def iteration(b, scores, values):
                    for g in range(GROUPS_):
                        if scores:
                            for p in range(GROUP * g, GROUP * (g + 1)):
                                load_k(b, p)
                        if values and g < GROUPS_ - 1:
                            load_v(b - 1, g + 1, N5 * (b - 1) + g)
                        if scores and g == GROUPS_ - 1:
                            load_v(b, 0, N5 * (b - 1) + g)
                        if values and g == 1:
                            wait(sp, valued, N5 * (b - 1))
                            sp.dma_start(vnew[0:DEC_T, :], a["v_sample"][bass.ds(b - 1, 1), :, :, :].rearrange("a t h n -> (a t) (h n)"))\
                                .then_inc(vn_in, 16)

                iteration(0, True, False)
                iteration(1, True, True)
                with sp.Fori(2, DEC_B) as b:
                    iteration(b, True, True)
                iteration(DEC_B, False, True)

            @block.scalar
            def _(act):
                def iteration(b, scores, values):
                    if values:
                        act.wait_ge(max_ready, 2 * b)
                        wait(act, w_turned, N5 * (b - 1))
                        nc.scalar.activation(W[:, :], S[:, :], ACT.Exp, bias=red[:, 6:7], accum_out=red[:, 7:8]).then_inc(exped, 1)
                    for p in range(PAGES if scores else 0):
                        act.wait_ge(turned_a, PAGES * b + p + 1)
                        nc.scalar.activation(KT[:, 0:half, (p % GROUP) * P:(p % GROUP + 1) * P],
                                             k.ps[2 * (p % 2)][:, :].rearrange("p (h n) -> p h n", h=half), ACT.Copy).then_inc(kt_out_a, 1)

                iteration(0, True, False)
                iteration(1, True, True)
                with act.Fori(2, DEC_B) as b:
                    iteration(b, True, True)
                iteration(DEC_B, False, True)

            @block.vector
            def _(dve):
                nc.vector.memset(Q[:, :, :], 0.0)
                nc.vector.memset(vnew[:, :], 0.0).then_inc(cleared, 1)
                nc.vector.memset(AT[:, PAGES, :], 0.0).then_inc(cleared, 1)
                nc.vector.memset(o[0:SMP, PT, :], 0.0).then_inc(cleared, 1)
                dve.wait_ge(cleared, 3)
                dve.wait_ge(c_in, 48)
                nc.vector.tensor_scalar(red[:, 9:10], table[:, 1:2], rep[:, 2 * P:2 * P + 1], table[:, 0:1],
                                        ALU.mult, ALU.add).then_inc(normed, 1)

                def bias_max(b, g):
                    w = GROUP * P if g < GROUPS_ else DEC_T
                    if g == 0:
                        wait(dve, exped, b)
                    dve.wait_ge(scored, N5 * b + g + 1)
                    nc.vector.memset(red[:, 11:12], 0.0)
                    part = slice(g * GROUP * P, g * GROUP * P + w)
                    nc.vector.tensor_tensor_reduce(out=S[:, part], in0=k.ps[4][:, 0:w], in1=alibi[:, part], scale=1.0,
                                                   scalar=-3e38, op0=ALU.add, op1=ALU.max,
                                                   accum_out=red[:, g:g + 1]).then_inc(biased, 1)

                def weights_out(b, g):
                    n = P if g < GROUPS_ else DEC_T
                    w = GROUP if g < GROUPS_ else 1
                    dve.wait_ge(w_turned, N5 * (b - 1) + g + 1)
                    src = k.ps[7][0:n, 0:w * P].rearrange("p (a x) -> p a x", x=QUAD)[:, :, 0:16]
                    src = src.rearrange("p a (h c t) -> p a h t c", h=2, c=2)
                    dst = AT[0:n, GROUP * g:GROUP * g + w, :].rearrange("p w (j h t) -> p (w j) h t", h=2, t=DEC_T)
                    nc.vector.tensor_reduce(out=dst, in_=src, op=ALU.add, axis=AX.X).then_inc(at_out, 1)

                def iteration(b, scores, values):
                    if scores:
                        wait(dve, scored, N5 * b)
                        for n in range(2):
                            nc.vector.tensor_copy(Q[:, n:HEADS:2, 8 * n:8 * n + 8],
                                                  qz[:, bass.ds(b, 1), n:HEADS:2, :].rearrange("p a h n -> p (a h) n"))
                        nc.vector.tensor_copy(knew[:, :, :], kTs[:, :, bass.ds(b * DEC_T, DEC_T)]).then_inc(q_ready, 1)
                    if values:
                        wait(dve, summed, 2 * (b - 1))
                        nc.vector.tensor_copy(place[:, :], places[:, bass.ds(b - 1, 1), :].rearrange("p a n -> p (a n)"))\
                            .then_inc(place_ready, 1)
                    for g in range(GROUPS_):
                        for p in range(GROUP * g, GROUP * (g + 1)):
                            if values and p % GROUP == GROUP - 1:
                                if g == 0:
                                    dve.wait_ge(exped, b)
                                    nc.vector.reciprocal(red[:, 8:9], red[:, 7:8]).then_inc(normed, 1)
                                    dve.wait_ge(normed, 3 * b - 1)
                                    nc.vector.tensor_tensor(red[:, 10:11], red[:, 8:9], red[:, 9:10], ALU.mult).then_inc(normed, 1)
                                    dve.wait_ge(normed, 3 * b)
                                    nc.vector.tensor_scalar(W[:, :], W[:, :], red[:, 10:11], None, ALU.mult).then_inc(normed, 1)
                                weights_out(b, g)
                            if scores:
                                dve.wait_ge(turned_b, PAGES * b + p + 1)
                                nc.vector.tensor_copy(KT[:, half:HEADS, (p % GROUP) * P:(p % GROUP + 1) * P],
                                                      k.ps[2 * (p % 2) + 1][:, :].rearrange("p (h n) -> p h n", h=half))\
                                    .then_inc(kt_out_b, 1)
                        if scores:
                            bias_max(b, g)
                    if values:
                        weights_out(b, GROUPS_)
                    if scores:
                        bias_max(b, GROUPS_)
                        dve.wait_ge(biased, N5 * (b + 1))
                        nc.vector.tensor_reduce(out=red[:, 5:6], in_=red[:, 0:5], op=ALU.max, axis=AX.X).then_inc(max_ready, 1)
                        dve.wait_ge(max_ready, 2 * b + 1)
                        nc.vector.tensor_scalar(red[:, 6:7], red[:, 5:6], -1.0, None, ALU.mult).then_inc(max_ready, 1)
                    if values:
                        dve.wait_ge(valued, N5 * b)
                        wait(dve, summed, 2 * (b - 1))
                        for n in range(2):
                            nc.vector.tensor_tensor(own[:, n * HB:(n + 1) * HB].rearrange("p (h n) -> p h n", n=P),
                                                    k.ps[5 + n][:, :].rearrange("p (h n) -> p h n", n=P),
                                                    bcast(own_head[:, half * n:half * (n + 1)], 2, [P, half, P]), ALU.mult)\
                                .then_inc(picked, 1)
                        for n, bank in enumerate((7, 4)):
                            dve.wait_ge(summed, 2 * (b - 1) + n + 1)
                            part = o[0:SMP, PT, n * HB:(n + 1) * HB]
                            nc.vector.tensor_tensor(part, part, k.ps[bank][0:SMP, :], ALU.add).then_inc(added, 1)

                iteration(0, True, False)
                iteration(1, True, True)
                with dve.Fori(2, DEC_B) as b:
                    iteration(b, True, True)
                iteration(DEC_B, False, True)

            @block.tensor
            def _(pe):
                def turn(b, p):
                    pe.wait_ge(k_in[p % KRING], 16 * (4 * b + p // KRING + 1))
                    for n, (free, signal) in enumerate(((kt_out_a, turned_a), (kt_out_b, turned_b))):
                        wait(pe, free, PAGES * b + p - 1)
                        for h in range(half):
                            hh = n * half + h
                            last = nc.tensor.transpose(k.ps[2 * (p % 2) + n][:, h * P:(h + 1) * P],
                                                       K[:, p % KRING, hh * P:(hh + 1) * P], k.ident[:, :])
                        last.then_inc(signal, 1)

                def score(b, g):
                    wait(pe, biased, N5 * b + g)
                    if g == 0:
                        pe.wait_ge(q_ready, b + 1)
                        wait(pe, added, 2 * (b - 1))
                    if g < GROUPS_:
                        pe.wait_ge(kt_out_a, PAGES * b + GROUP * (g + 1))
                        pe.wait_ge(kt_out_b, PAGES * b + GROUP * (g + 1))
                    for n in range(2):
                        for j in range(4):
                            h = 2 * j + n
                            rhs = KT[:, h, :] if g < GROUPS_ else knew[:, h, :]
                            w = GROUP * P if g < GROUPS_ else DEC_T
                            last = nc.tensor.matmul(k.ps[4][QUAD * j:QUAD * (j + 1), 0:w], Q[:, h, :], rhs, start=(n == 0), stop=(n == 1))
                    last.then_inc(scored, 1)

                def turn_weights(b, g):
                    if g == 0:
                        pe.wait_ge(normed, 3 * b + 1)
                        wait(pe, added, 2 * (b - 1))
                    wait(pe, at_out, N5 * (b - 1) + g)
                    if g < GROUPS_:
                        for n in range(GROUP):
                            p = GROUP * g + n
                            last = nc.tensor.transpose(k.ps[7][:, n * P:(n + 1) * P], W[:, p * P:(p + 1) * P], k.ident[:, :])
                    else:
                        last = nc.tensor.transpose(k.ps[7][0:DEC_T, 0:P], W[:, PAST:KEYS], k.ident[:, :])
                    last.then_inc(w_turned, 1)

                def value(b, g):
                    if g == 0:
                        wait(pe, picked, 2 * (b - 1))
                    pe.wait_ge(at_out, N5 * (b - 1) + g + 1)
                    if g < GROUPS_:
                        for p in range(GROUP * g, GROUP * (g + 1)):
                            pe.wait_ge(v_in[p % VRING], 16 * (2 * (b - 1) + p // VRING + 1))
                    else:
                        pe.wait_ge(vn_in, 16 * b)
                    pages = range(GROUP * g, GROUP * (g + 1)) if g < GROUPS_ else (PAGES,)
                    for n in range(2):
                        for p in pages:
                            q = p % 4
                            rhs = (V[p % VRING] if p < PAGES else vnew)[:, n * HB:(n + 1) * HB]
                            last = nc.tensor.matmul(k.ps[5 + n][QUAD * q:QUAD * (q + 1), :], AT[:, p, :], rhs, start=(p < 4),
                                                    stop=(p == PAGES or (p >= PAGES - 3)))
                    last.then_inc(valued, 1)

                def iteration(b, scores, values):
                    for g in range(GROUPS_):
                        for p in range(GROUP * g, GROUP * (g + 1)):
                            if values and p % GROUP == GROUP - 1:
                                turn_weights(b, g)
                            if scores:
                                turn(b, p)
                        if values:
                            value(b, g)
                        if scores:
                            score(b, g)
                    if values:
                        turn_weights(b, GROUPS_)
                    if scores:
                        score(b, GROUPS_)
                    if values:
                        value(b, GROUPS_)
                        pe.wait_ge(place_ready, b)
                        pe.wait_ge(at_out, N5 * b)
                        pe.wait_ge(biased, N5 * (b + 1) if scores else N5 * b)
                        for n, bank in enumerate((7, 4)):
                            pe.wait_ge(picked, 2 * (b - 1) + n + 1)
                            nc.tensor.matmul(k.ps[bank][0:SMP, :], place[:, :], own[:, n * HB:(n + 1) * HB], start=True, stop=True)\
                                .then_inc(summed, 1)

                iteration(0, True, False)
                iteration(1, True, True)
                with pe.Fori(2, DEC_B) as b:
                    iteration(b, True, True)
                iteration(DEC_B, False, True)



def final_block(k, a):
    nc = k.nc
    with ExitStack() as tmp_ctx:
        wrow = tmp_ctx.enter_context(nc.sbuf_tensor("final_row", [1, D], F32))
        y = tmp_ctx.enter_context(nc.sbuf_tensor("final_y", [P, NT, D], F32))
        w_in, squares, mean, seed = k.sem("final_w_landed"), k.sem("final_squares"), k.sem("final_mean"), k.sem("final_seed")
        spread, ready, stored = k.sem("final_spread"), k.sem("final_ready"), k.sem("final_stored")
        with nc.Block() as block:
            @block.sync
            def _(sp):
                sp.dma_start(wrow[:, :], a["final_norm_w"].rearrange("(a n) -> a n", a=1)).then_inc(w_in, 16)
                for t in range(NT):
                    sp.wait_ge(ready, 2 * (t + 1))
                    dst = a["y_prompt"][0, t * P:(t + 1) * P, :] if t < PT else a["y_sample"].rearrange("b t d -> (b t) d")
                    sp.dma_start(dst, y[0:rows(t), t, :]).then_inc(stored, 16)
                sp.wait_ge(stored, 16 * NT)

            @block.tensor
            def _(pe):
                pe.wait_ge(w_in, 16)
                for i in range(2):
                    last = nc.tensor.matmul(k.ps[i][:, :], k.ones[0:1, :], wrow[0:1, i * HB:(i + 1) * HB], start=True, stop=True)
                last.then_inc(spread, 1)

            @block.scalar
            def _(act):
                for t in range(NT):
                    nc.scalar.activation(y[:, t, :], k.h[:, t, :], ACT.Square, accum_out=k.ss[:, t:t + 1]).then_inc(squares, 1)
                act.wait_ge(mean, 1)
                nc.scalar.activation(k.tmp, k.ms, ACT.Ln).then_inc(seed, 1)
                act.wait_ge(seed, 1)
                nc.scalar.activation(k.r0, k.tmp, ACT.Exp, scale=-0.5).then_inc(seed, 1)

            @block.vector
            def _(dve):
                ch = Chain(dve, k.order["vector"], k.order_n["vector"])
                dve.wait_ge(squares, NT)
                nc.vector.tensor_scalar(k.ms, k.ss, 1.0 / D, EPS, ALU.mult, ALU.add).then_inc(mean, 1)
                dve.wait_ge(mean, 1)
                inverse_root(dve, None, (seed, 2), ch, nc, k.ms, k.r0, k.tmp, k.r)
                dve.wait_ge(spread, 1)
                for t in range(NT):
                    for i in range(2):
                        part = slice(i * HB, (i + 1) * HB)
                        nc.vector.scalar_tensor_tensor(out=y[:, t, part], in0=k.h[:, t, part], scalar=k.r[:, t:t + 1],
                                                       in1=k.ps[i][:, :], op0=ALU.mult, op1=ALU.mult).then_inc(ready, 1)
                k.order_n["vector"] = ch.n



def trunk(nc, a):
    with ExitStack() as ctx:
        k = Core(nc, ctx)
        rep = k.sb("row_gains", [P, 2 * P + 2])
        slots_x = nc.dram_tensor("slots_x", [SLOTS, D], F32, kind="Internal").ap()
        slots_y = nc.dram_tensor("slots_y", [SLOTS, D], F32, kind="Internal").ap()
        zeroed = k.sem("slots_zeroed")
        setup(k, a, rep)
        with k.stage(), ExitStack() as layer:
            sb = lambda name, shape: layer.enter_context(nc.sbuf_tensor(name, shape, F32))
            v, g = sb("hgrn_v", [P, NT, D]), sb("hgrn_g", [P, NT, D])
            norm_block(k, "mix0", [(k.cw[:, 0, :], k.xT)], v)
            hgrn_block(k, a, v, g, v, rep[:, 0:P], (slots_x, slots_y), zeroed)
            by_head = lambda ap: ap.rearrange("p (h n) -> p h n", n=P)
            mix_out_block(k, "out0", v, lambda t: by_head(g[:, t, :]), EPS)
        kv = a["w_kv"]
        with k.stage():
            moe_blocks(k, a, 0, slots_x, slots_y,
                       [column_halves(kv, 0), column_halves(kv, HB), column_halves(a["b_w_q"][0], 0)])
        with k.stage(), ExitStack() as layer:
            sb = lambda name, shape: layer.enter_context(nc.sbuf_tensor(name, shape, F32))
            o = sb("attn_o", [P, NT, D])
            qz, kTs = sb("attn_qz", [P, DEC_B, HEADS, 2 * DEC_T]), sb("attn_kTs", [P, HEADS, SMP])
            with ExitStack() as prompt:
                sb = lambda name, shape: prompt.enter_context(nc.sbuf_tensor(name, shape, F32))
                kT, qT = sb("attn_kT", [P, HEADS, TOK]), [sb(f"attn_qT{c}", [P, HEADS, TOK]) for c in range(2)]
                v = sb("attn_v", [P, NT, D])
                with ExitStack() as proj:
                    sb = lambda name, shape: proj.enter_context(nc.sbuf_tensor(name, shape, F32))
                    q_xT = sb("attn_q_xT", [P, DC, TOK])
                    norm_block(k, "mix1", [(k.cw[:, 2, :], k.xT), (k.cw[:, 1, :], q_xT)], o)
                    kvq_block(k, a, k.xT, q_xT, o, v, kT, qT, o, sb("attn_smp_q", [P, P]))
                prompt_attention(k, a, rep, v, kT, qT, qz, kTs, o)
            sample_attention(k, a, rep, qz, kTs, o)
            subln = bcast(rep[:, P:2 * P], 1, [P, HEADS, P])
            mix_out_block(k, "out1", o, lambda t: subln, SUBLN_EPS)
        moe_blocks(k, a, 1, slots_x, slots_y, [])
        final_block(k, a)


INPUTS = ["x_prompt", "x_sample", "state_hgrn", "cache_k", "cache_v", "page_table", "norm_mix_w", "norm_ffn_w", "a_w_in",
          "a_lb_logits", "a_gnorm_w", "a_w_o", "kv_norm_w", "w_kv", "b_w_q", "b_lambda_q1", "b_lambda_k1", "b_lambda_q2",
          "b_lambda_k2", "b_subln_w", "b_w_o", "moe_w_group", "moe_w_sub", "moe_w_gate", "moe_w_up", "moe_w_down",
          "final_norm_w"]
OUTPUTS = [("y_prompt", (1, SEQ, D)), ("y_sample", (DEC_B, DEC_T, D)), ("state_prompt", (1, 1, HEADS, P, P)),
           ("state_sample", (1, DEC_B, HEADS, P, P)), ("k_prompt", (1, SEQ, HEADS, P)), ("v_prompt", (1, SEQ, HEADS, P)),
           ("k_sample", (DEC_B, DEC_T, HEADS, P)), ("v_sample", (DEC_B, DEC_T, HEADS, P))]


def constants():
    import numpy as np

    f32 = np.float32
    q, key = np.arange(P)[:, None], np.arange(SEQ)[None, :]
    dist = (SEQ - P + q - key).astype(f32)
    dist[dist < 0] = MASKED
    row = np.arange(P)
    j, x = row // 32, row % 32
    used, head, half, t = x < 16, 2 * j + x // 8, x // 4 % 2, x % 4
    pos = np.arange(PAST + DEC_T)[None, :]
    slope = (2.0 ** -(head + 1.0))[:, None].astype(f32)
    alibi = -slope * (PAST + t[:, None] - pos).astype(f32)
    alibi[pos > PAST + t[:, None]] = -MASKED
    alibi[~used] = 0
    halves = np.stack([used & (half == 0), used & (half == 1)], 1)
    own_head = (x // DEC_T)[:, None] == np.arange(HEADS)[None, :]
    place = np.arange(SMP)[None, None, :] == np.arange(DEC_B)[None, :, None] * DEC_T + (x % DEC_T)[:, None, None]
    return {"const_dist": dist, "const_rows": np.concatenate([alibi, halves, own_head, place.reshape(P, -1)], 1).astype(f32)}


def kernel(**inputs):
    import numpy as np
    import concourse.bacc as bacc
    from concourse.bass_utils import run_bass_kernel_spmd

    nc = bacc.Bacc("TRN2", target_bir_lowering=False, num_devices=1)
    arrays, a = {}, {}
    given = {n: np.ascontiguousarray(inputs[n]) for n in INPUTS}
    for name, x in {**given, **constants()}.items():
        arrays[name] = x
        a[name] = nc.dram_tensor(name, x.shape, mybir.dt.from_np(x.dtype), kind="ExternalInput").ap()
    for name, shape in OUTPUTS:
        a[name] = nc.dram_tensor(name, shape, F32, kind="ExternalOutput").ap()
    trunk(nc, a)
    r = run_bass_kernel_spmd(nc, [arrays], core_ids=[0])
    return tuple(r.results[0][name] for name, _ in OUTPUTS)
```

```python
import math
from contextlib import ExitStack, contextmanager

import concourse.bass as bass
from concourse import mybir

F32 = mybir.dt.float32
I32 = mybir.dt.int32
ALU = mybir.AluOpType
ACT = mybir.ActivationFunctionType
AX = mybir.AxisListType

P = 128
D = 1024
DC = D // P
SEQ = 512
DEC_B, DEC_T = 8, 4
SMP = DEC_B * DEC_T
TOK = SEQ + SMP
PT = SEQ // P
NT = PT + 1
HEADS = 8
HB = 512
EPG, GROUPS, EXPERTS, TOPK = 4, 4, 16, 2
FF = 256
BLOCKS = (TOK * TOPK - EXPERTS) // P + EXPERTS
SLOTS = BLOCKS * P
PAGE, PAGES = 128, 16
PAST = PAGE * PAGES
LEVELS = (8, 16, 32, 64, 128)
LAM_INIT = 0.8 - 0.6 * math.exp(-0.3)
FG_MIN = 2.0 ** -63
MASKED = 1e30
EPS, SUBLN_EPS = 1e-6, 1e-5
WEIGHT_SLOTS = 3


def rows(t):
    return P if t < PT else SMP


def cols(t):
    return slice(t * P, t * P + rows(t))


class Chain:

    def __init__(self, eng, sem, start=0):
        self.eng, self.sem, self.n = eng, sem, start

    def __call__(self, ins):
        self.n = self.n + 1
        ins.then_inc(self.sem, 1)
        self.eng.wait_ge(self.sem, self.n)


class Core:

    def __init__(self, nc, ctx):
        self.nc, self.ctx, self.stage_sems = nc, ctx, None
        self.ps = [self.psum(f"bank{i}", [P, HB]) for i in range(8)]
        self.ident = self.sb("ident", [P, P])
        self.ones = self.sb("ones", [1, P])
        self.h = self.sb("h", [P, NT, D])
        self.xT = self.sb("xT", [P, DC, TOK])
        self.stat = self.sb("stat", [P, 64])
        self.head_squares = self.sb("head_squares", [P, NT, HEADS])
        self.ss, self.ms, self.r0 = self.stat[:, 0:5], self.stat[:, 8:13], self.stat[:, 16:21]
        self.tmp, self.r = self.stat[:, 24:29], self.stat[:, 32:37]
        self.wring = [self.sb(f"wring{i}", [P, DC, HB]) for i in range(WEIGHT_SLOTS)]
        self.cw = self.sb("column_weights", [P, 5, DC])
        self.rowbuf = self.sb("row_weights", [1, 2 * P + 4 * 64])
        self.lamwork = self.sb("lambda_products", [1, 2, 64])
        self.levelmask = self.sb("level_masks", [P, 1 + len(LEVELS), P])
        self.restart = self.sb("scan_restart", [P, TOK])
        self.batchmask = self.sb("batch_mask", [SMP, DEC_B])
        self.lb = self.sb("lower_bound", [P, 4, HEADS])
        self.w_in = [self.sem(f"weights_landed{i}") for i in range(WEIGHT_SLOTS)]
        self.w_done = []
        self.w_issued = 0
        self.w_taken = 0
        self.order = {n: self.sem(f"{n}_order") for n in ("vector", "scalar", "gpsimd")}
        self.order_n = dict.fromkeys(self.order, 0)

    def sb(self, name, shape, dt=F32):
        return self.ctx.enter_context(self.nc.sbuf_tensor(name, shape, dt))

    def psum(self, name, shape, dt=F32):
        return self.ctx.enter_context(self.nc.psum_tensor(name, shape, dt))

    def sem(self, name):
        if self.stage_sems is None:
            return self.ctx.enter_context(self.nc.semaphore(name))
        self.stage_sems.append(self.nc.alloc_semaphore(name))
        return self.stage_sems[-1]

    @contextmanager
    def stage(self):
        self.stage_sems = []
        yield
        self.w_done = [None] * len(self.w_done)
        self.nc.clear_and_free_semaphores(self.stage_sems)
        self.nc.all_engine_barrier()
        self.stage_sems = None

    def load_weights(self, sp, halves):
        n = self.w_issued
        if n >= WEIGHT_SLOTS and self.w_done[n - WEIGHT_SLOTS]:
            sp.wait_ge(*self.w_done[n - WEIGHT_SLOTS])
        slot = n % WEIGHT_SLOTS
        for dst, src in halves(self.wring[slot]):
            sp.dma_start(dst, src).then_inc(self.w_in[slot], 16)
        self.w_issued += 1

    def take_weights(self, pe):
        n = self.w_taken
        pe.wait_ge(self.w_in[n % WEIGHT_SLOTS], 32 * (n // WEIGHT_SLOTS + 1))
        self.w_taken += 1
        return self.wring[n % WEIGHT_SLOTS]


def column_halves(w, n0):
    view = w.rearrange("(c p) n -> p c n", p=P)
    half = DC // 2
    return lambda tile: [(tile[:, 0:half, :], view[:, 0:half, n0:n0 + HB]),
                         (tile[:, half:DC, :], view[:, half:DC, n0:n0 + HB])]


def bcast(ap, axis, shape):
    return ap.unsqueeze(axis).to_broadcast(shape)



def setup(k, a, rep):
    nc = k.nc
    tokens_in, rows_in, columns_in = k.sem("tokens_landed"), k.sem("row_weights_landed"), k.sem("column_weights_landed")
    ident_made, turned, out = k.sem("ident_made"), k.sem("columns_turned"), k.sem("columns_out")
    summed, spread = k.sem("lambda_summed"), k.sem("rows_spread")
    lam = k.rowbuf[:, 2 * P:].rearrange("a (i n) -> a i n", i=4)
    s = k.stat[0:1, 40:48]
    by_feature = (a["norm_mix_w"][0], a["norm_mix_w"][1], a["kv_norm_w"], a["norm_ffn_w"][0], a["norm_ffn_w"][1],
                  a["a_lb_logits"][0])
    n_cols = len(by_feature) * DC
    with nc.sbuf_tensor("column_weights_by_row", [n_cols, P], F32) as weight_rows, nc.Block() as block:
        @block.sync
        def _(sp):
            for t in range(PT):
                sp.dma_start(k.h[:, t, :], a["x_prompt"][0, t * P:(t + 1) * P, :]).then_inc(tokens_in, 16)
            sp.dma_start(k.h[0:SMP, PT, :], a["x_sample"].rearrange("b t d -> (b t) d")).then_inc(tokens_in, 16)
            sp.wait_ge(columns_in, 16 * len(by_feature))
            sp.wait_ge(rows_in, 16 * 6)
            for i in range(2):
                k.load_weights(sp, column_halves(a["a_w_in"][0], 2 * D + i * HB))
            k.load_weights(sp, head_pair_halves(a, 0))
            sp.wait_ge(tokens_in, 16 * NT)

        @block.scalar
        def _(act):
            for i, w in enumerate((a["b_lambda_q1"], a["b_lambda_k1"], a["b_lambda_q2"], a["b_lambda_k2"])):
                act.dma_start(lam[:, i, :], w).then_inc(rows_in, 16)
            act.dma_start(k.rowbuf[:, 0:P], a["a_gnorm_w"]).then_inc(rows_in, 16)
            act.dma_start(k.rowbuf[:, P:2 * P], a["b_subln_w"]).then_inc(rows_in, 16)
            for i, w in enumerate(by_feature):
                act.dma_start(weight_rows[i * DC:(i + 1) * DC, :], w.rearrange("(c p) -> c p", p=P)).then_inc(columns_in, 16)
            act.wait_ge(summed, 2)
            nc.scalar.activation(s[:, 2:4], s[:, 0:2], ACT.Exp).then_inc(summed, 1)

        @block.gpsimd
        def _(pool):
            ch = Chain(pool, k.order["gpsimd"], k.order_n["gpsimd"])
            ch(pool.memset(k.ident[:, :], 0.0))
            ch(pool.affine_select(out=k.ident[:, :], in_=k.ident[:, :], compare_op=ALU.not_equal, fill=1.0,
                                  base=0, pattern=[[-1, P]], channel_multiplier=1))
            nc.gpsimd.memset(k.ones[:, :], 1.0).then_inc(ident_made, 1)
            ch(pool.memset(k.levelmask[:, :, :], 0.0))
            m = k.levelmask[:, 0, :].rearrange("p (n r) -> p n r", r=4)
            ch(pool.memset(m, 1.0))
            ch(pool.affine_select(out=m, in_=m, compare_op=ALU.is_ge, fill=0.0, base=0,
                                  pattern=[[-4, P // 4], [0, 4]], channel_multiplier=1))
            ch(pool.affine_select(out=m, in_=m, compare_op=ALU.is_ge, fill=0.0, base=0,
                                  pattern=[[4, P // 4], [1, 4]], channel_multiplier=-1))
            for i, size in enumerate(LEVELS):
                half = size // 2
                m = k.levelmask[:, i + 1, :].rearrange("p (n r) -> p n r", r=size)[:, :, half:size]
                ch(pool.memset(m, 1.0))
                ch(pool.affine_select(out=m, in_=m, compare_op=ALU.is_ge, fill=0.0, base=0,
                                      pattern=[[-size, P // size], [0, half]], channel_multiplier=1))
                ch(pool.affine_select(out=m, in_=m, compare_op=ALU.is_ge, fill=0.0, base=half - 1,
                                      pattern=[[size, P // size], [0, half]], channel_multiplier=-1))
            ch(pool.memset(k.restart[:, :], 1.0))
            ch(pool.memset(k.restart[:, 0:SEQ].rearrange("p (c n) -> p c n", n=P)[:, :, 0:1], 0.0))
            ch(pool.memset(k.restart[:, SEQ:TOK].rearrange("p (c n) -> p c n", n=DEC_T)[:, :, 0:1], 0.0))
            ch(pool.memset(k.batchmask[:, :], 1.0))
            ch(pool.affine_select(out=k.batchmask[:, :], in_=k.batchmask[:, :], compare_op=ALU.is_ge, fill=0.0,
                                  base=0, pattern=[[-DEC_T, DEC_B]], channel_multiplier=1))
            ch(pool.affine_select(out=k.batchmask[:, :], in_=k.batchmask[:, :], compare_op=ALU.is_ge, fill=0.0,
                                  base=DEC_T - 1, pattern=[[DEC_T, DEC_B]], channel_multiplier=-1))
            k.order_n["gpsimd"] = ch.n

        @block.vector
        def _(dve):
            for q in range(1, 4):
                nc.vector.memset(k.h[32 * q:32 * q + 32, PT, :], 0.0)
            dve.wait_ge(rows_in, 16 * 6)
            for i in range(2):
                nc.vector.tensor_tensor_reduce(out=k.lamwork[:, i, :],
                                               in0=lam[:, 2 * i, :], in1=lam[:, 2 * i + 1, :], scale=1.0, scalar=0.0,
                                               op0=ALU.mult, op1=ALU.add, accum_out=s[:, i:i + 1]).then_inc(summed, 1)
            dve.wait_ge(summed, 3)
            nc.vector.scalar_tensor_tensor(out=s[:, 4:5], in0=s[:, 3:4], scalar=-LAM_INIT, in1=s[:, 2:3], op0=ALU.add,
                                           op1=ALU.subtract).then_inc(summed, 1)
            dve.wait_ge(turned, 1)
            nc.vector.tensor_copy(k.cw[:, :, :].rearrange("p i c -> p (i c)"), k.ps[6][:, 0:n_cols - DC]).then_inc(out, 1)
            nc.vector.tensor_copy(k.lb[:, 0, :], k.ps[6][:, n_cols - DC:n_cols]).then_inc(out, 1)
            dve.wait_ge(spread, 1)
            nc.vector.tensor_copy(rep[:, 0:P], k.ps[7][:, 0:P]).then_inc(out, 1)
            nc.vector.tensor_scalar(rep[:, P:2 * P], k.ps[7][:, P:2 * P], 1.0 - LAM_INIT, None, ALU.mult).then_inc(out, 1)
            nc.vector.tensor_copy(rep[:, 2 * P:2 * P + 1], k.ps[7][:, 2 * P:2 * P + 1]).then_inc(out, 1)

        @block.tensor
        def _(pe):
            pe.wait_ge(ident_made, 1)
            pe.wait_ge(columns_in, 16 * len(by_feature))
            nc.tensor.transpose(k.ps[6][:, 0:n_cols], weight_rows[0:n_cols, :], k.ident[0:n_cols, 0:n_cols]).then_inc(turned, 1)
            pe.wait_ge(rows_in, 16 * 6)
            nc.tensor.matmul(k.ps[7][:, 0:2 * P], k.ones[0:1, :], k.rowbuf[:, 0:2 * P], start=True, stop=True)
            pe.wait_ge(summed, 4)
            nc.tensor.matmul(k.ps[7][:, 2 * P:2 * P + 1], k.ones[0:1, :], s[:, 4:5], start=True, stop=True).then_inc(spread, 1)


def head_pair_halves(a, pair):
    view = a["a_w_in"][0].rearrange("(c p) n -> p c n", p=P)
    n = 2 * P
    return lambda tile: [(tile[:, :, 0:n], view[:, :, pair * n:(pair + 1) * n]),
                         (tile[:, :, n:2 * n], view[:, :, D + pair * n:D + (pair + 1) * n])]



def inverse_root(dve, ch, nc, ms, root, r0, r):
    ch(nc.vector.reciprocal(r0, root))
    ch(nc.vector.tensor_tensor(r, r0, r0, ALU.mult))
    ch(nc.vector.tensor_tensor(r, r, ms, ALU.mult))
    ch(nc.vector.tensor_scalar(r, r, -0.5, 1.5, ALU.mult, ALU.add))
    ch(nc.vector.tensor_tensor(r, r0, r, ALU.mult))


class TileNorm:

    def __init__(self, k, tag, weights, xs, ready=None, banks=((0, 1), (2, 3))):
        self.k, self.weights, self.xs, self.ready, self.banks = k, weights, xs, ready, banks
        self.squared, self.mean, self.rooted = k.sem(f"{tag}_squared"), k.sem(f"{tag}_mean"), k.sem(f"{tag}_rooted")
        self.xs_ready, self.turned = k.sem(f"{tag}_xs"), k.sem(f"{tag}_turned")
        self.out_v, self.out_a = k.sem(f"{tag}_out_dve"), k.sem(f"{tag}_out_act")

    def bank(self, t, n):
        return self.k.ps[self.banks[t % len(self.banks)][n]]

    def root(self, act, t):
        k, nc = self.k, self.k.nc
        if self.ready is not None:
            act.wait_ge(*self.ready(t))
        nc.scalar.activation(self.xs[:, t, :], k.h[:, t, :], ACT.Square, accum_out=k.ss[:, t:t + 1]).then_inc(self.squared, 1)
        act.wait_ge(self.mean, t + 1)
        nc.scalar.activation(k.tmp[:, t:t + 1], k.ms[:, t:t + 1], ACT.Sqrt).then_inc(self.rooted, 1)

    def inverse(self, dve, ch, t):
        k, nc = self.k, self.k.nc
        col = slice(t, t + 1)
        dve.wait_ge(self.squared, t + 1)
        nc.vector.tensor_scalar(k.ms[:, col], k.ss[:, col], 1.0 / D, EPS, ALU.mult, ALU.add).then_inc(self.mean, 1)
        dve.wait_ge(self.rooted, t + 1)
        inverse_root(dve, ch, nc, k.ms[:, col], k.tmp[:, col], k.r0[:, col], k.r[:, col])

    def scale(self, dve, ch, t):
        self.inverse(dve, ch, t)
        self.k.nc.vector.tensor_scalar(self.xs[:, t, :], self.k.h[:, t, :], self.k.r[:, t:t + 1], None, ALU.mult)\
            .then_inc(self.xs_ready, 1)

    def turn(self, pe, t):
        nc, half = self.k.nc, DC // 2
        pe.wait_ge(self.xs_ready, t + 1)
        if t >= len(self.banks):
            pe.wait_ge(self.out_v, t - len(self.banks) + 1)
            pe.wait_ge(self.out_a, t - len(self.banks) + 1)
        for c in range(DC):
            last = nc.tensor.transpose(self.bank(t, c // half)[:, (c % half) * P:(c % half) * P + rows(t)],
                                       self.xs[0:rows(t), t, c * P:(c + 1) * P], self.k.ident[0:rows(t), 0:rows(t)])
        last.then_inc(self.turned, 1)

    def out_first(self, dve, t):
        half = DC // 2
        dve.wait_ge(self.turned, t + 1)
        for w, out in self.weights:
            src = self.bank(t, 0)[:, :].rearrange("p (c n) -> p c n", c=half)[:, :, 0:rows(t)]
            last = self.k.nc.vector.tensor_tensor(out[:, 0:half, cols(t)], src, bcast(w[:, 0:half], 2, [P, half, rows(t)]), ALU.mult)
        last.then_inc(self.out_v, 1)

    def out_second(self, act, t):
        half = DC // 2
        act.wait_ge(self.turned, t + 1)
        for w, out in self.weights:
            for c in range(half, DC):
                src = self.bank(t, 1)[:, (c - half) * P:(c - half) * P + rows(t)]
                last = self.k.nc.scalar.activation(out[:, c, cols(t)], src, ACT.Copy, scale=w[:, c:c + 1])
        last.then_inc(self.out_a, 1)


def norm_block(k, tag, weights, xs):
    nc = k.nc
    norm = TileNorm(k, tag, weights, xs)
    squared_v = k.sem(f"{tag}_squared_dve")
    ACT_TILES = (0, 2, 4)
    with nc.Block() as block:
        @block.scalar
        def _(act):
            for t in ACT_TILES:
                nc.scalar.activation(xs[:, t, :], k.h[:, t, :], ACT.Square, accum_out=k.ss[:, t:t + 1]).then_inc(norm.squared, 1)
            act.wait_ge(norm.mean, 1)
            nc.scalar.activation(k.tmp, k.ms, ACT.Sqrt).then_inc(norm.rooted, 1)
            for t in range(NT):
                norm.out_second(act, t)

        @block.vector
        def _(dve):
            ch = Chain(dve, k.order["vector"], k.order_n["vector"])
            for t in range(NT):
                if t not in ACT_TILES:
                    nc.vector.tensor_tensor_reduce(out=xs[:, t, :], in0=k.h[:, t, :], in1=k.h[:, t, :], scale=1.0,
                                                   scalar=0.0, op0=ALU.mult, op1=ALU.add,
                                                   accum_out=k.ss[:, t:t + 1]).then_inc(squared_v, 1)
            dve.wait_ge(norm.squared, len(ACT_TILES))
            dve.wait_ge(squared_v, NT - len(ACT_TILES))
            nc.vector.tensor_scalar(k.ms, k.ss, 1.0 / D, EPS, ALU.mult, ALU.add).then_inc(norm.mean, 1)
            dve.wait_ge(norm.mean, 1)
            dve.wait_ge(norm.rooted, 1)
            inverse_root(dve, ch, nc, k.ms, k.tmp, k.r0, k.r)
            for t in range(NT):
                nc.vector.tensor_scalar(xs[:, t, :], k.h[:, t, :], k.r[:, t:t + 1], None, ALU.mult).then_inc(norm.xs_ready, 1)
                if t >= 2:
                    norm.out_first(dve, t - 2)
            for t in (PT - 1, PT):
                norm.out_first(dve, t)
            k.order_n["vector"] = ch.n

        @block.tensor
        def _(pe):
            for t in range(NT):
                norm.turn(pe, t)



def project_tokens(nc, bank, xT, w, t):
    for c in range(DC):
        if t < PT:
            last = nc.tensor.matmul(bank[:, :], xT[:, c, cols(t)], w[:, c, :], start=(c == 0), stop=(c == DC - 1))
        else:
            for j in range(HB // P):
                last = nc.tensor.matmul(bank[SMP * j:SMP * (j + 1), 0:P], xT[:, c, cols(t)], w[:, c, j * P:(j + 1) * P],
                                        start=(c == 0), stop=(c == DC - 1))
    return last


def token_parts(bank, out, i, t):
    if t < PT:
        return [(bank[:, :], out[:, t, i * HB:(i + 1) * HB])]
    return [(bank[SMP * j:SMP * (j + 1), 0:P], out[0:SMP, t, i * HB + j * P:i * HB + (j + 1) * P]) for j in range(HB // P)]



GATE_UNITS = [[("g", n // NT, n % NT) for n in range(*span)] for span in ((0, 2), (2, 3), (3, 4), (4, 5), (5, 6), (6, 7),
                                                                          (7, 8), (8, 8), (8, 10))]
GATE_TILE_AT = [0, 4]



def hgrn_block(k, a, v, g, o, gnorm, slots, zeroed):
    nc = k.nc
    NLEV = 1 + len(LEVELS)
    with ExitStack() as tmp_ctx:
        def sb(name, shape):
            return tmp_ctx.enter_context(nc.sbuf_tensor(name, shape, F32))

        f_in, q = [sb(f"gla_fin{i}", [P, TOK]) for i in range(2)], [sb(f"gla_q{i}", [P, TOK]) for i in range(2)]
        kk, b = sb("gla_k", [P, TOK]), sb("gla_b", [P, TOK])
        mid4 = sb("gla_mid4", [P, TOK // 4])
        diff = [sb(f"gla_diff{i}", [P, TOK]) for i in range(2)]
        inv4 = sb("gla_inv4", [P, TOK])
        eb, kd = sb("gla_eb", [P, TOK]), inv4
        QE = [sb(f"gla_qe{i}", [P, TOK if i == 0 else SEQ]) for i in range(NLEV)]
        KE = [sb(f"gla_ke{i}", [P, TOK if i == 0 else SEQ]) for i in range(NLEV)]
        smp_qf = sb("gla_sample_qf", [P, P])
        QS = sb("gla_qs", [P, TOK])
        QB = sb("gla_qb", [P, DEC_B * (SMP + DEC_T)])
        A = sb("gla_att", [P, PT, P])
        AS = sb("gla_att_s", [SMP, SMP])
        kdT, kdTs = sb("gla_kdT", [P, PT, P]), sb("gla_kdTs", [SMP, P])
        below = sb("gla_vm", [P, DEC_B, P])
        vm = below[0:SMP, :, :]
        zero = below[SMP:P, :, :].rearrange("p b n -> p (b n)")
        ZERO = P - SMP
        assert SLOTS % ZERO == 0
        S = sb("gla_s", [P, PT, P])
        s0 = [sb(f"gla_s0_{i}", [P, DEC_B, P]) for i in range(2)]
        sn = sb("gla_sn", [P, DEC_B, P])

        units = {}
        order = [("v", i, t) for i in range(2) for t in range(NT)]
        for h in range(HEADS):
            if h % 2 == 0:
                order += [("s", h // 2)]
            order += [("f", h), ("q", h)] + GATE_UNITS[h]
        order += GATE_UNITS[HEADS]
        n = 0
        for i, u in enumerate(order):
            if u[0] == "s":
                units[u] = (i + 1, 2)
            else:
                units[u] = (i + 1, n % 2)
                n += 1
        proj_done, s_copied, s_turned = k.sem("proj_done"), k.sem("sample_qf_copied"), k.sem("sample_qf_turned")
        v_out, qf_out, g_out = k.sem("v_evacuated"), k.sem("qf_evacuated"), k.sem("g_evacuated")
        evacuated = {}
        for u in order:
            if u[0] == "v":
                evacuated[u] = (v_out, NT * u[1] + u[2] + 1)
            elif u[0] == "g":
                evacuated[u] = (g_out, NT * u[1] + u[2] + 1)
            else:
                evacuated[u] = (qf_out, 4 * u[1] + {"f": 1, "q": 3}[u[0]] if u[0] != "s" else 8 * u[1] + 8)
        before = {}
        last_in = {}
        for u in order:
            before[u] = last_in.get(units[u][1])
            last_in[units[u][1]] = u

        fgc_ready, logf_ready, b_ready = k.sem("fg_ready"), k.sem("logf_ready"), k.sem("b_ready")
        diff_ready, exp_ready = k.sem("diff_ready"), k.sem("exp_ready")
        q_lev, k_lev = k.sem("q_level_ready"), k.sem("k_level_ready")
        kk_ready = k.sem("k_ready")
        turned, turned_out = k.sem("kd_turned"), k.sem("kd_turned_out")
        att_done, att_taken = k.sem("att_done"), k.sem("att_taken")
        ds_done, s_ready = k.sem("state_step_done"), k.sem("state_ready")
        sds_done, sn_ready, sn_scaled = k.sem("sample_step_done"), k.sem("sample_state_ready"), k.sem("sample_state_scaled")
        vm_ready, o_done, o_out = k.sem("vm_ready"), k.sem("o_done"), k.sem("o_evacuated")
        zero_made, squared = k.sem("zero_made"), k.sem("gla_squared")
        s0_in = [k.sem(f"s0_landed{i}") for i in range(2)]
        s_store, sn_store = k.sem("s_stored"), k.sem("sn_stored")
        head = lambda h: slice(h * P, (h + 1) * P)
        blocks = lambda ap, n: ap.rearrange("p (c n) -> p c n", n=n)
        QBd = QB[:, :].rearrange("p (b x) -> p b x", x=SMP + DEC_T)[:, :, 0:DEC_T]

        with nc.Block() as block:
            @block.scalar
            def _(act):
                def evacuate_qf(h):
                    x = SMP * (h % 2)
                    if h % 2 == 0:
                        act.wait_ge(proj_done, units[("s", h // 2)][0])
                        nc.scalar.activation(smp_qf[:, :], k.ps[2][:, 0:P], ACT.Copy).then_inc(s_copied, 1)
                    done, bank = units[("f", h)]
                    act.wait_ge(proj_done, done)
                    if h >= 2:
                        act.wait_ge(q_lev, (NLEV + 2) * (h - 1))
                    nc.scalar.activation(f_in[h % 2][:, 0:SEQ], k.ps[bank][:, :], ACT.Sigmoid).then_inc(qf_out, 1)
                    act.wait_ge(s_turned, h // 2 + 1)
                    nc.scalar.activation(f_in[h % 2][:, SEQ:TOK], k.ps[2][:, P + 2 * SMP + x:P + 3 * SMP + x], ACT.Sigmoid)\
                        .then_inc(qf_out, 1)
                    done, bank = units[("q", h)]
                    act.wait_ge(proj_done, done)
                    nc.scalar.activation(q[h % 2][:, 0:SEQ], k.ps[bank][:, :], ACT.Silu).then_inc(qf_out, 1)
                    nc.scalar.activation(q[h % 2][:, SEQ:TOK], k.ps[2][:, P + x:P + SMP + x], ACT.Silu).then_inc(qf_out, 1)

                def gate(u):
                    done, bank = units[u]
                    _, i, t = u
                    act.wait_ge(proj_done, done)
                    for src, dst in token_parts(k.ps[bank], g, i, t):
                        last = nc.scalar.activation(dst, src, ACT.Silu)
                    last.then_inc(g_out, 1)

                def exponentials(h):
                    act.wait_ge(fgc_ready, 2 * h + 2)
                    nc.scalar.activation(f_in[h % 2][:, :], f_in[h % 2][:, :], ACT.Ln).then_inc(logf_ready, 1)
                    if h:
                        squares(h - 1)
                    base = (NLEV + 1) * h
                    act.wait_ge(diff_ready, base + 1)
                    if h:
                        act.wait_ge(sn_scaled, h)
                    nc.scalar.activation(inv4[:, :], diff[0][:, :], ACT.Exp, scale=-1.0).then_inc(exp_ready, 1)
                    nc.scalar.activation(diff[0][:, :], diff[0][:, :], ACT.Exp).then_inc(exp_ready, 1)
                    nc.scalar.activation(eb[:, :], b[:, :], ACT.Exp).then_inc(exp_ready, 1)
                    for i in range(1, NLEV + 1):
                        act.wait_ge(diff_ready, base + i + 1)
                        w = TOK if i == NLEV else SEQ
                        nc.scalar.activation(diff[i % 2][:, 0:w], diff[i % 2][:, 0:w], ACT.Exp).then_inc(exp_ready, 1)

                def results(h):
                    act.wait_ge(turned, h + 1)
                    if h:
                        act.wait_ge(squared, h)
                    nc.scalar.activation(kdT[:, :, :], k.ps[5][:, :], ACT.Copy).then_inc(turned_out, 1)
                    nc.scalar.activation(kdTs[:, :], k.ps[6][0:SMP, P:2 * P], ACT.Copy).then_inc(turned_out, 1)
                    act.wait_ge(o_done, h + 1)
                    nc.scalar.activation(o[:, 0:PT, head(h)], k.ps[7][:, :].rearrange("p (c n) -> p c n", c=PT), ACT.Copy)\
                        .then_inc(o_out, 1)
                    nc.scalar.activation(o[0:SMP, PT, head(h)], k.ps[6][0:SMP, 2 * P:3 * P], ACT.Copy).then_inc(o_out, 1)

                def squares(h):
                    for c in range(PT):
                        last = nc.scalar.activation(kdT[:, c, :], k.ps[7][:, c * P:(c + 1) * P], ACT.Square,
                                                    accum_out=k.head_squares[:, c, h:h + 1])
                    last.then_inc(squared, 1)

                for h in range(HEADS):
                    evacuate_qf(h)
                    for u in GATE_UNITS[h]:
                        gate(u)
                    if h:
                        results(h - 1)
                    exponentials(h)
                for u in GATE_UNITS[HEADS]:
                    gate(u)
                results(HEADS - 1)
                squares(HEADS - 1)

            @block.vector
            def _(dve):
                ch = Chain(dve, k.order["vector"], k.order_n["vector"])
                lb = k.lb
                nc.vector.memset(below[:, :, :], 0.0).then_inc(zero_made, 1)
                ch(nc.vector.tensor_tensor(lb[:, 1, :], lb[:, 0, :], lb[:, 0, :], ALU.subtract))
                ch(nc.vector.tensor_scalar(lb[:, 1, :], lb[:, 1, :], 1.0, None, ALU.add))
                ch(nc.vector.tensor_tensor(lb[:, 2, :], lb[:, 1, :], lb[:, 1, :], ALU.subtract))
                ch(nc.vector.tensor_scalar(lb[:, 3, :], lb[:, 2, :], -1.0, 1.0, ALU.mult, ALU.add))
                for i, lev in enumerate(LEVELS):
                    nc.vector.memset(QE[i + 1][:, :], 0.0)
                    ch(nc.vector.memset(KE[i + 1][:, :], 0.0))
                nc.vector.memset(QB[:, :], 0.0)
                nc.vector.memset(A[:, :, :], 0.0)
                ch(nc.vector.memset(AS[:, :], 0.0))
                for x in range(1, 4):
                    nc.vector.memset(g[32 * x:32 * x + 32, PT, :], 0.0)
                    nc.vector.memset(v[32 * x:32 * x + 32, PT, :], 0.0)
                for i in range(2):
                    for t in range(NT):
                        done, bank = units[("v", i, t)]
                        dve.wait_ge(proj_done, done)
                        for src, dst in token_parts(k.ps[bank], v, i, t):
                            last = nc.vector.tensor_copy(dst, src)
                        last.then_inc(v_out, 1)

                def elementwise(h):
                    dve.wait_ge(qf_out, 4 * h + 2)
                    if h:
                        dve.wait_ge(k_lev, (NLEV + 1) * h)
                    nc.vector.tensor_scalar(f_in[h % 2][:, :], f_in[h % 2][:, :], lb[:, 3, h:h + 1], lb[:, 2, h:h + 1],
                                            ALU.mult, ALU.add).then_inc(fgc_ready, 1)
                    dve.wait_ge(fgc_ready, 2 * h + 1)
                    nc.vector.tensor_scalar(kk[:, :], f_in[h % 2][:, :], -1.0, 1.0, ALU.mult, ALU.add).then_inc(kk_ready, 1)
                    dve.wait_ge(kk_ready, h + 1)
                    nc.vector.tensor_scalar(f_in[h % 2][:, :], f_in[h % 2][:, :], FG_MIN, None, ALU.max).then_inc(fgc_ready, 1)
                    dve.wait_ge(logf_ready, h + 1)
                    ch(nc.vector.tensor_tensor_scan(b[:, :], k.restart[:, :], f_in[h % 2][:, :], 0.0, ALU.mult, ALU.add))
                    b4 = blocks(b[:, :], 4)
                    ch(nc.vector.tensor_tensor(mid4[:, :], b4[:, :, 1], b4[:, :, 2], ALU.add))
                    nc.vector.scalar_tensor_tensor(out=blocks(diff[0][:, :], 4), in0=bcast(mid4[:, :], 2, [P, TOK // 4, 4]),
                                                   scalar=0.5, in1=b4, op0=ALU.mult, op1=ALU.subtract).then_inc(diff_ready, 1)
                    ebase = (NLEV + 3) * h
                    for i in range(1, NLEV + 1):
                        d = diff[i % 2]
                        if i >= 2:
                            dve.wait_ge(k_lev, (NLEV + 1) * h + i - 1)
                            dve.wait_ge(q_lev, (NLEV + 2) * h + i)
                        if i < NLEV:
                            size = LEVELS[i - 1]
                            half = size // 2
                            bv, dv = blocks(b[:, 0:SEQ], size), blocks(d[:, 0:SEQ], size)
                            mid = bcast(bv[:, :, half - 1], 2, [P, SEQ // size, half])
                            nc.vector.tensor_tensor(dv[:, :, 0:half], mid, bv[:, :, 0:half], ALU.subtract)
                            nc.vector.tensor_tensor(dv[:, :, half:size], bv[:, :, half:size], mid, ALU.subtract)\
                                .then_inc(diff_ready, 1)
                        else:
                            for lo, hi, n in ((0, SEQ, P), (SEQ, TOK, DEC_T)):
                                bv, dv = blocks(b[:, lo:hi], n), blocks(d[:, lo:hi], n)
                                last = nc.vector.tensor_tensor(dv, bcast(bv[:, :, n - 1], 2, [P, (hi - lo) // n, n]), bv,
                                                               ALU.subtract)
                            last.then_inc(diff_ready, 1)
                        j = i - 1
                        if h and j == 0:
                            dve.wait_ge(att_done, (NLEV + 1) * h)
                            dve.wait_ge(o_done, h)
                        if j == 0:
                            dve.wait_ge(qf_out, 4 * h + 4)
                            dve.wait_ge(exp_ready, ebase + 3)
                            nc.vector.tensor_tensor(QE[0][:, :], q[h % 2][:, :], inv4[:, :], ALU.mult).then_inc(q_lev, 1)
                            nc.vector.tensor_tensor(QS[:, :], q[h % 2][:, :], eb[:, :], ALU.mult).then_inc(q_lev, 1)
                        else:
                            size = LEVELS[j - 1]
                            dve.wait_ge(exp_ready, ebase + 3 + j)
                            up = slice(size // 2, size)
                            nc.vector.tensor_tensor(blocks(QE[j][:, :], size)[:, :, up], blocks(q[h % 2][:, 0:SEQ], size)[:, :, up],
                                                    blocks(diff[j % 2][:, 0:SEQ], size)[:, :, up], ALU.mult).then_inc(q_lev, 1)
                    dve.wait_ge(q_lev, (NLEV + 2) * h + 2)
                    nc.vector.tensor_copy(QBd, blocks(QS[:, SEQ:TOK], DEC_T)).then_inc(q_lev, 1)

                def matrices(h):
                    if h:
                        dve.wait_ge(o_done, h)
                    for i in range(NLEV):
                        dve.wait_ge(att_done, (NLEV + 1) * h + i + 1)
                        nc.vector.copy_predicated(A[:, :, :], bcast(k.levelmask[:, i, :].bitcast(I32), 1, [P, PT, P]),
                                                  k.ps[3 + i % 2][:, :].rearrange("p (c n) -> p c n", c=PT)).then_inc(att_taken, 1)
                        dve.wait_ge(att_taken, (NLEV + 1) * h + i + 1)
                    dve.wait_ge(att_done, (NLEV + 1) * (h + 1))
                    nc.vector.copy_predicated(AS[:, :], k.levelmask[0:SMP, 0, 0:SMP].bitcast(I32), k.ps[7][0:SMP, 0:SMP])\
                        .then_inc(att_taken, 1)
                    dve.wait_ge(ds_done, h + 1)
                    if h:
                        dve.wait_ge(s_store, 16 * h)
                    for c in range(PT):
                        new, step = S[:, c, :], k.ps[5][:, c * P:(c + 1) * P]
                        if c == 0:
                            nc.vector.tensor_copy(new, step).then_inc(s_ready, 1)
                        else:
                            dve.wait_ge(s_ready, PT * h + c)
                            nc.vector.scalar_tensor_tensor(out=new, in0=S[:, c - 1, :],
                                                           scalar=eb[:, c * P + P - 1:c * P + P], in1=step,
                                                           op0=ALU.mult, op1=ALU.add).then_inc(s_ready, 1)
                    dve.wait_ge(sds_done, h + 1)
                    dve.wait_ge(sn_scaled, h + 1)
                    for i in range(2):
                        part = sn[:, 4 * i:4 * i + 4, :]
                        nc.vector.tensor_tensor(part, part, k.ps[3 + i][:, :].rearrange("p (c n) -> p c n", c=4), ALU.add)\
                            .then_inc(sn_ready, 1)

                elementwise(0)
                for h in range(1, HEADS):
                    matrices(h - 1)
                    elementwise(h)
                for i in range(2):
                    for t in range(NT):
                        dve.wait_ge(g_out, NT * i + t + 1)
                        gv = g[0:rows(t), t, i * HB:(i + 1) * HB].rearrange("p (h n) -> p h n", n=P)
                        nc.vector.tensor_tensor(gv, gv, bcast(gnorm[0:rows(t), :], 1, [rows(t), 4, P]), ALU.mult)
                matrices(HEADS - 1)
                k.order_n["vector"] = ch.n

            @block.gpsimd
            def _(pool):
                for h in range(HEADS):
                    ebase = (NLEV + 3) * h
                    if h:
                        pool.wait_ge(att_done, (NLEV + 1) * h)
                    for j in range(NLEV):
                        pool.wait_ge(exp_ready, ebase + (2 if j == 0 else 3 + j))
                        if j == 0:
                            pool.wait_ge(kk_ready, h + 1)
                            nc.gpsimd.tensor_tensor(KE[0][:, :], kk[:, :], diff[0][:, :], ALU.mult).then_inc(k_lev, 1)
                        else:
                            size = LEVELS[j - 1]
                            lo = slice(0, size // 2)
                            nc.gpsimd.tensor_tensor(blocks(KE[j][:, :], size)[:, :, lo], blocks(kk[:, 0:SEQ], size)[:, :, lo],
                                                    blocks(diff[j % 2][:, 0:SEQ], size)[:, :, lo], ALU.mult).then_inc(k_lev, 1)
                    pool.wait_ge(q_lev, (NLEV + 2) * h + 1)
                    pool.wait_ge(exp_ready, ebase + 3 + NLEV)
                    nc.gpsimd.tensor_tensor(kd[:, :], kk[:, :], diff[NLEV % 2][:, :], ALU.mult).then_inc(k_lev, 1)
                    pool.wait_ge(v_out, 2 * NT)
                    if h == 0:
                        pool.wait_ge(zero_made, 1)
                    if h:
                        pool.wait_ge(sds_done, h)
                    nc.gpsimd.tensor_tensor(vm[:, :, :], bcast(v[0:SMP, PT, head(h)], 1, [SMP, DEC_B, P]),
                                            bcast(k.batchmask[:, :], 2, [SMP, DEC_B, P]), ALU.mult).then_inc(vm_ready, 1)
                    pool.wait_ge(s0_in[h % 2], 16 * (h // 2 + 1))
                    if h:
                        pool.wait_ge(sn_store, 16 * h)
                    ends = blocks(eb[:, SEQ:TOK], DEC_T)[:, :, DEC_T - 1]
                    nc.gpsimd.tensor_tensor(sn[:, :, :], s0[h % 2][:, :, :], bcast(ends, 2, [P, DEC_B, P]), ALU.mult)\
                        .then_inc(sn_scaled, 1)

            @block.tensor
            def _(pe):
                def begin(u):
                    if before[u] is not None:
                        pe.wait_ge(*evacuated[before[u]])
                    return k.ps[units[u][1]]

                def by_token(u, w):
                    project_tokens(nc, begin(u), k.xT, w, u[2]).then_inc(proj_done, 1)

                def by_feature(h, w):
                    if h % 2 == 0:
                        project_tokens(nc, begin(("s", h // 2)), k.xT, w, PT).then_inc(proj_done, 1)
                    for kind, off in (("f", 2 * P), ("q", 0)):
                        bank = begin((kind, h))
                        for c in range(DC):
                            lhsT = w[:, c, off + (h % 2) * P:off + (h % 2) * P + P]
                            last = nc.tensor.matmul(bank[:, :], lhsT, k.xT[:, c, 0:SEQ], start=(c == 0), stop=(c == DC - 1))
                        last.then_inc(proj_done, 1)

                def gla(h):
                    pe.wait_ge(v_out, 2 * NT)
                    pe.wait_ge(k_lev, (NLEV + 1) * (h + 1))
                    pe.wait_ge(q_lev, (NLEV + 2) * (h + 1))
                    if h:
                        pe.wait_ge(s_ready, PT * h)
                        pe.wait_ge(squared, h)
                        pe.wait_ge(sn_ready, 2 * h)
                    for c in range(PT):
                        nc.tensor.transpose(k.ps[5][:, c * P:(c + 1) * P], kd[:, c * P:(c + 1) * P], k.ident[:, :])
                    nc.tensor.transpose(k.ps[6][0:SMP, P:2 * P], kd[:, SEQ:TOK], k.ident[:, :]).then_inc(turned, 1)
                    for i in range(NLEV):
                        if i >= 2:
                            pe.wait_ge(att_taken, (NLEV + 1) * h + i - 1)
                        for c in range(PT):
                            part = slice(c * P, (c + 1) * P)
                            last = nc.tensor.matmul(k.ps[3 + i % 2][:, part], KE[i][:, part], QE[i][:, part], start=True, stop=True)
                        last.then_inc(att_done, 1)
                    nc.tensor.matmul(k.ps[7][0:SMP, 0:SMP], KE[0][:, SEQ:TOK], QE[0][:, SEQ:TOK], start=True, stop=True)\
                        .then_inc(att_done, 1)
                    pe.wait_ge(turned_out, 2 * (h + 1))
                    for c in range(PT):
                        last = nc.tensor.matmul(k.ps[5][:, c * P:(c + 1) * P], kdT[:, c, :], v[:, c, head(h)], start=True, stop=True)
                    last.then_inc(ds_done, 1)
                    pe.wait_ge(att_taken, (NLEV + 1) * (h + 1))
                    pe.wait_ge(vm_ready, h + 1)
                    for i in range(2):
                        last = nc.tensor.matmul(k.ps[3 + i][:, :], kdTs[:, :], vm[:, 4 * i:4 * i + 4, :], start=True, stop=True)
                    last.then_inc(sds_done, 1)
                    pe.wait_ge(s_ready, PT * (h + 1))
                    for c in range(PT):
                        out = k.ps[7][:, c * P:(c + 1) * P]
                        nc.tensor.matmul(out, A[:, c, :], v[:, c, head(h)], start=True, stop=(c == 0))
                        if c:
                            nc.tensor.matmul(out, QS[:, c * P:(c + 1) * P], S[:, c - 1, :], start=False, stop=True)
                    out = k.ps[6][0:SMP, 2 * P:3 * P]
                    nc.tensor.matmul(out, AS[:, :], v[0:SMP, PT, head(h)], start=True, stop=False)
                    pe.wait_ge(s0_in[h % 2], 16 * (h // 2 + 1))
                    for bb in range(DEC_B):
                        last = nc.tensor.matmul(out, QB[:, bb * SMP:(bb + 1) * SMP], s0[h % 2][:, bb, :], start=False,
                                                stop=(bb == DEC_B - 1))
                    last.then_inc(o_done, 1)

                for i in range(2):
                    w = k.take_weights(pe)
                    for t in range(NT):
                        by_token(("v", i, t), w)
                    k.w_done.append((proj_done, units[("v", i, NT - 1)][0]))
                for h in range(HEADS):
                    if h % 2 == 0:
                        w = k.take_weights(pe)
                        k.w_done.append((proj_done, units[("q", h + 1)][0]))
                    by_feature(h, w)
                    if h % 2 == 0:
                        pe.wait_ge(s_copied, h // 2 + 1)
                        nc.tensor.transpose(k.ps[2][:, P:2 * P], smp_qf[:, :], k.ident[:, :]).then_inc(s_turned, 1)
                    if h in GATE_TILE_AT:
                        w_gate = k.take_weights(pe)
                        i = GATE_TILE_AT.index(h)
                        k.w_done.append((proj_done, units[("g", i, NT - 1)][0]))
                    for u in GATE_UNITS[h]:
                        by_token(u, w_gate)
                    if h:
                        gla(h - 1)
                for u in GATE_UNITS[HEADS]:
                    by_token(u, w_gate)
                gla(HEADS - 1)

            def store(sp, h):
                sp.wait_ge(s_ready, PT * (h + 1))
                sp.dma_start(a["state_prompt"][0, 0, h, :, :], S[:, PT - 1, :]).then_inc(s_store, 16)
                sp.wait_ge(sn_ready, 2 * (h + 1))
                sp.dma_start(a["state_sample"][0, :, h, :, :].rearrange("b k v -> k b v"), sn[:, :, :])\
                    .then_inc(sn_store, 16)

            @block.sync
            def _(sp):
                gate_tile = lambda i: column_halves(a["a_w_in"][0], 3 * D + i * HB)
                tiles = {0: [gate_tile(0), head_pair_halves(a, 1)], 2: [head_pair_halves(a, 2)],
                         4: [gate_tile(1), head_pair_halves(a, 3)]}
                for h in range(HEADS):
                    for tile in tiles.get(h, ()):
                        k.load_weights(sp, tile)
                    if h >= 2:
                        sp.wait_ge(sn_scaled, h - 1)
                        sp.wait_ge(o_done, h - 1)
                    sp.dma_start(s0[h % 2][:, :, :], a["state_hgrn"][0, :, h, :, :].rearrange("b k v -> k b v"))\
                        .then_inc(s0_in[h % 2], 16)
                    if h == 0:
                        sp.wait_ge(zero_made, 1)
                    for j in range(h * SLOTS // ZERO // HEADS, (h + 1) * SLOTS // ZERO // HEADS):
                        for x in slots:
                            sp.dma_start(x[j * ZERO:(j + 1) * ZERO, :], zero).then_inc(zeroed, 16)
                    if h >= 1:
                        store(sp, h - 1)
                for i in range(2):
                    k.load_weights(sp, column_halves(a["a_w_o"][0], i * HB))
                store(sp, HEADS - 1)
                sp.wait_ge(s_store, 16 * HEADS)
                sp.wait_ge(sn_store, 16 * HEADS)
                sp.wait_ge(zeroed, 16 * len(slots) * SLOTS // ZERO)



def mix_out_block(k, tag, o, gate, eps, norm_weights):
    nc = k.nc
    squared, summed, mean = k.sem(f"{tag}_squared"), k.sem(f"{tag}_summed"), k.sem(f"{tag}_mean")
    seed, gated = k.sem(f"{tag}_seed"), k.sem(f"{tag}_gated")
    turned, out_a, out_v = k.sem(f"{tag}_turned"), k.sem(f"{tag}_out_act"), k.sem(f"{tag}_out_dve")
    projected, added = k.sem(f"{tag}_projected"), k.sem(f"{tag}_added")
    norm = TileNorm(k, f"{tag}n", norm_weights, o, ready=lambda t: (added, 2 * (t + 1)), banks=((2, 3),))
    half = DC // 2
    by_head = lambda ap: ap.rearrange("p (h n) -> p h n", n=P)
    with ExitStack() as tmp_ctx:
        def sb(name, shape):
            return tmp_ctx.enter_context(nc.sbuf_tensor(f"{tag}_{name}", shape, F32))
        sq = sb("sq", [P, D])
        stats = sb("stats", [P, 4, NT, HEADS])
        flat = [x.rearrange("p t h -> p (t h)") for x in (k.head_squares[:, :, :], *(stats[:, i, :, :] for i in range(4)))]
        with nc.Block() as block:
            @block.scalar
            def _(act):
                nc.scalar.activation(sq[:, :], o[:, PT, :], ACT.Square).then_inc(squared, 1)
                act.wait_ge(mean, 1)
                nc.scalar.activation(flat[2], flat[1], ACT.Sqrt).then_inc(seed, 1)

                def turned_out(t):
                    act.wait_ge(turned, t + 1)
                    src = k.ps[1][:, :].rearrange("p (c n) -> p c n", c=half)[:, :, 0:rows(t)]
                    nc.scalar.activation(k.xT[:, half:DC, cols(t)], src, ACT.Copy).then_inc(out_a, 1)

                turned_out(0)
                for t in range(NT):
                    if t + 1 < NT:
                        turned_out(t + 1)
                    norm.root(act, t)
                    if t:
                        norm.out_second(act, t - 1)
                norm.out_second(act, PT)

            @block.vector
            def _(dve):
                ch = Chain(dve, k.order["vector"], k.order_n["vector"])
                dve.wait_ge(squared, 1)
                nc.vector.tensor_reduce(out=k.head_squares[:, PT, :], in_=by_head(sq[:, :]), op=ALU.add, axis=AX.X).then_inc(summed, 1)
                dve.wait_ge(summed, 1)
                nc.vector.tensor_scalar(flat[1], flat[0], 1.0 / P, eps, ALU.mult, ALU.add).then_inc(mean, 1)
                dve.wait_ge(seed, 1)
                inverse_root(dve, ch, nc, flat[1], flat[2], flat[3], flat[4])

                def scale(t):
                    for h in range(HEADS):
                        part = o[:, t, h * P:(h + 1) * P]
                        last = nc.vector.scalar_tensor_tensor(out=part, in0=part, scalar=stats[:, 3, t, h:h + 1],
                                                              in1=gate(t)[:, h, :], op0=ALU.mult, op1=ALU.mult)
                    last.then_inc(gated, 1)

                def turned_out(t):
                    dve.wait_ge(turned, t + 1)
                    src = k.ps[0][:, :].rearrange("p (c n) -> p c n", c=half)[:, :, 0:rows(t)]
                    nc.vector.tensor_copy(k.xT[:, 0:half, cols(t)], src).then_inc(out_v, 1)

                scale(0)
                scale(1)
                turned_out(0)
                for t in range(2, NT):
                    scale(t)
                for t in range(NT):
                    if t + 1 < NT:
                        turned_out(t + 1)
                    for i in range(2):
                        n = 2 * t + i
                        dve.wait_ge(projected, n + 1)
                        for src, part in token_parts(k.ps[4 + n % 4], k.h, i, t):
                            last = nc.vector.tensor_tensor(part, part, src, ALU.add)
                        last.then_inc(added, 1)
                    norm.scale(dve, ch, t)
                    if t:
                        norm.out_first(dve, t - 1)
                norm.out_first(dve, PT)
                k.order_n["vector"] = ch.n

            @block.tensor
            def _(pe):
                def turn(t):
                    pe.wait_ge(gated, t + 1)
                    if t:
                        pe.wait_ge(out_v, t)
                        pe.wait_ge(out_a, t)
                    for c in range(DC):
                        last = nc.tensor.transpose(k.ps[c // half][:, (c % half) * P:(c % half) * P + rows(t)],
                                                   o[0:rows(t), t, c * P:(c + 1) * P], k.ident[0:rows(t), 0:rows(t)])
                    last.then_inc(turned, 1)

                turn(0)
                w = [k.take_weights(pe) for _ in range(2)]
                k.w_done += [(projected, 2 * NT)] * 2
                for t in range(NT):
                    if t + 1 < NT:
                        turn(t + 1)
                    pe.wait_ge(out_v, t + 1)
                    pe.wait_ge(out_a, t + 1)
                    for i in range(2):
                        n = 2 * t + i
                        if n >= 4:
                            pe.wait_ge(added, n - 3)
                        project_tokens(nc, k.ps[4 + n % 4], k.xT, w[i], t).then_inc(projected, 1)
                    if t:
                        norm.turn(pe, t - 1)
                norm.turn(pe, PT)



def moe_blocks(k, a, layer, xs, slots_x, slots_y, prefetch, final):
    nc = k.nc
    tag = f"moe{layer}"
    with ExitStack() as tmp_ctx:
        def sb(name, shape, dt=F32):
            return tmp_ctx.enter_context(nc.sbuf_tensor(f"{tag}_{name}", shape, dt))

        expert = sb("expert", [P, 2 * BLOCKS])
        expert_i = sb("expert_i", [1, BLOCKS + 1], I32)
        slot_i = sb("slot_i", [P, TOPK, NT], I32)
        gates = sb("gates", [P, TOPK, NT])
        column = k.cw[:, 3 + layer, :]
        buffers = ExpertBuffers(k, a, tag, layer, tmp_ctx, expert_i)
        with ExitStack() as route_ctx:
            route_block(k, a, tag, layer, route_ctx, xs, slots_x, expert, expert_i, slot_i, gates, buffers)
        expert_block(k, a, tag, layer, buffers, slots_x, slots_y, expert_i, column, prefetch)
        combine_block(k, a, tag, buffers.rows, slots_y, slot_i, gates, xs if final else None)


def route_block(k, a, tag, layer, ctx, xs, slots_x, expert, expert_i, slot_i, gates, buffers):
    nc = k.nc

    def sb(name, shape, dt=F32):
        return ctx.enter_context(nc.sbuf_tensor(f"{tag}_{name}", shape, dt))

    E, G = EXPERTS, GROUPS
    COL = 32
    wr = sb("router", [P, DC, COL])
    logT = sb("logits_T", [P, TOK])
    sum4 = sb("sum4", [P, COL])
    tri, onesq = sb("tri", [P, P]), sb("onesq", [P, P])
    L = sb("logits", [P, NT, G + E])
    one = sb("one", [P, 3, NT, 4])
    work = sb("work", [P, 6, NT, E])
    hot = sb("hot", [P, TOPK, NT, E])
    both = sb("both", [P, NT, E])
    sc = sb("scalars", [P, 12, NT])
    counts = sb("counts", [P, 6, E])
    step_i, step = sb("step_i", [P, BLOCKS], I32), sb("step", [P, BLOCKS])
    big = sb("big", [P, BLOCKS, E])
    slot = sb("slot", [P, TOPK, NT])
    fall = sb("fall", [P, 4])
    w_in, made, logit, copied = k.sem(f"{tag}_router_landed"), k.sem(f"{tag}_made"), k.sem(f"{tag}_logit"), k.sem(f"{tag}_copied")
    to_exp, exped, picked = k.sem(f"{tag}_to_exp"), k.sem(f"{tag}_exped"), k.sem(f"{tag}_picked")
    cleared, blocks_ready = k.sem(f"{tag}_router_cleared"), k.sem(f"{tag}_blocks_ready")
    rows_started = k.sem(f"{tag}_rows_started")
    placed, slots_ready, sent = k.sem(f"{tag}_placed"), k.sem(f"{tag}_slots_ready"), k.sem(f"{tag}_sent")
    flat = lambda ap: ap.rearrange("p t e -> p (t e)")
    with nc.Block() as block:
        @block.sync
        def _(sp):
            wv = lambda x: x.rearrange("(c p) n -> p c n", p=P)
            sp.wait_ge(cleared, 1)
            sp.dma_start(wr[:, :, 0:G], wv(a["moe_w_group"][layer])).then_inc(w_in, 16)
            for gg in range(G):
                sp.dma_start(wr[:, :, G + EPG * gg:G + EPG * (gg + 1)], wv(a["moe_w_sub"][layer, gg])).then_inc(w_in, 16)
            sp.wait_ge(blocks_ready, 1)
            sp.wait_ge(rows_started, 1)
            e = buffers.expert(sp, 0)
            buffers.load_gate_up(sp, 0, e)
            buffers.load_down(sp, 0, e)

        @block.gpsimd
        def _(pool):
            ch = Chain(pool, k.order["gpsimd"], k.order_n["gpsimd"])
            nc.gpsimd.memset(onesq[:, :], 1.0)
            ch(nc.gpsimd.memset(tri[:, :], 1.0))
            ch(nc.gpsimd.affine_select(out=tri[:, :], in_=tri[:, :], compare_op=ALU.is_gt, fill=0.0, base=0,
                                       pattern=[[1, P]], channel_multiplier=-1))
            nc.gpsimd.iota(step_i[:, :], pattern=[[1, BLOCKS]], base=0, channel_multiplier=0).then_inc(made, 1)
            pool.wait_ge(made, 1)
            nc.gpsimd.tensor_copy(step[:, :], step_i[:, :]).then_inc(made, 1)
            ch(nc.gpsimd.memset(sum4[:, :], 0.0))
            for j in range(P // COL):
                ins = nc.gpsimd.affine_select(out=sum4[:, :], in_=sum4[:, :], compare_op=ALU.not_equal, fill=1.0,
                                              base=-COL * j, pattern=[[-1, COL]], channel_multiplier=1)
                ch(ins) if j < P // COL - 1 else ins.then_inc(made, 1)
            k.order_n["gpsimd"] = ch.n
            pool.wait_ge(slots_ready, 1)
            for j in range(TOPK):
                for t in range(NT):
                    pool.indirect_dma_start(slots_x, bass.IndirectOffsetOnAxis(ap=slot_i[0:rows(t), j, t:t + 1], axis=0),
                                            xs[0:rows(t), t, :], None).then_inc(sent, 16)
            pool.sem_inc(rows_started, 1)
            pool.wait_ge(sent, 16 * TOPK * NT)

        @block.tensor
        def _(pe):
            pe.wait_ge(w_in, 16 * (1 + G))
            for lo, hi, bank in ((0, SEQ, k.ps[0]), (SEQ, TOK, k.ps[2])):
                for c in range(DC):
                    j = c % 4
                    last = nc.tensor.matmul(bank[COL * j:COL * (j + 1), 0:hi - lo], wr[:, c, :], k.xT[:, c, lo:hi],
                                            start=(c < 4), stop=(c >= 4))
                last.then_inc(logit, 1)
            pe.wait_ge(copied, 2)
            pe.wait_ge(made, 3)
            for t in range(NT):
                last = nc.tensor.matmul(k.ps[3][0:rows(t), t * COL:(t + 1) * COL], logT[:, cols(t)], sum4[:, :],
                                        start=True, stop=True)
            last.then_inc(logit, 1)
            pe.wait_ge(picked, 1)
            every = both[:, :, :].rearrange("p t e -> p (t e)")
            nc.tensor.matmul(k.ps[1][:, 0:NT * E], tri[:, :], every, start=True, stop=True)
            nc.tensor.matmul(k.ps[1][:, NT * E:2 * NT * E], onesq[:, :], every, start=True, stop=True).then_inc(placed, 1)

        @block.scalar
        def _(act):
            act.wait_ge(to_exp, 1)
            nc.scalar.activation(work[:, 0, :, 0:G], work[:, 0, :, 0:G], ACT.Exp).then_inc(exped, 1)
            act.wait_ge(to_exp, 2)
            nc.scalar.activation(sc[:, 4, :], sc[:, 4, :], ACT.Exp).then_inc(exped, 1)

        @block.vector
        def _(dve):
            ch = Chain(dve, k.order["vector"], k.order_n["vector"])
            TT, TS = nc.vector.tensor_tensor, nc.vector.tensor_scalar
            full = lambda ap: bcast(ap, 2, [P, NT, 4])
            nc.vector.memset(wr[:, :, :], 0.0).then_inc(cleared, 1)
            ch(nc.vector.memset(L[:, :, :], 0.0))
            dve.wait_ge(made, 2)
            ch(TS(fall[:, :], step[:, 0:4], -1.0, 4.0, ALU.mult, ALU.add))
            dve.wait_ge(logit, 1)
            nc.vector.tensor_copy(logT[:, 0:SEQ], k.ps[0][:, :]).then_inc(copied, 1)
            dve.wait_ge(logit, 2)
            nc.vector.tensor_copy(logT[:, SEQ:TOK], k.ps[2][:, 0:SMP]).then_inc(copied, 1)
            dve.wait_ge(logit, 3)
            by_tile = k.ps[3][:, 0:NT * COL].rearrange("p (t e) -> p t e", e=COL)
            ch(nc.vector.tensor_copy(L[:, 0:PT, :], by_tile[:, 0:PT, 0:G + E]))
            ch(nc.vector.tensor_copy(L[0:SMP, PT, :], by_tile[0:SMP, PT, 0:G + E]))

            def first_largest(values, top, out):
                ch(nc.vector.tensor_reduce(out=top, in_=values, op=ALU.max, axis=AX.X))
                ch(TT(out, values, full(top), ALU.is_equal))
                ch(TT(out, out, bcast(fall[:, :], 1, [P, NT, 4]), ALU.mult))
                ch(nc.vector.tensor_reduce(out=sc[:, 10, :], in_=out, op=ALU.max, axis=AX.X))
                ch(TT(out, out, full(sc[:, 10, :]), ALU.is_equal))

            first_largest(L[:, :, 0:G], sc[:, 0, :], one[:, 0, :, :])
            TT(work[:, 0, :, 0:G], L[:, :, 0:G], full(sc[:, 0, :]), ALU.subtract).then_inc(to_exp, 1)
            ch(TT(work[:, 1, :, :].rearrange("p t (g e) -> p t g e", g=G), L[:, :, G:G + E].rearrange("p t (g e) -> p t g e", g=G),
                  bcast(one[:, 0, :, :], 3, [P, NT, G, EPG]), ALU.mult))
            ch(nc.vector.tensor_reduce(out=work[:, 2, :, 0:EPG], in_=work[:, 1, :, :].rearrange("p t (g e) -> p t e g", g=G),
                                       op=ALU.add, axis=AX.X))
            first_largest(work[:, 2, :, 0:EPG], sc[:, 1, :], one[:, 1, :, :])
            ch(nc.vector.scalar_tensor_tensor(out=work[:, 3, :, 0:EPG], in0=one[:, 1, :, :], scalar=-3e38,
                                              in1=work[:, 2, :, 0:EPG], op0=ALU.mult, op1=ALU.add))
            first_largest(work[:, 3, :, 0:EPG], sc[:, 2, :], one[:, 2, :, :])
            TT(sc[:, 4, :], sc[:, 2, :], sc[:, 1, :], ALU.subtract).then_inc(to_exp, 1)
            for j in range(TOPK):
                ch(TT(hot[:, j, :, :].rearrange("p t (g e) -> p t g e", g=G), bcast(one[:, 0, :, :], 3, [P, NT, G, EPG]),
                      bcast(one[:, 1 + j, :, :], 2, [P, NT, G, EPG]), ALU.mult))
            ch(TT(both[:, :, :], hot[:, 0, :, :], hot[:, 1, :, :], ALU.add))
            for q in range(1, 4):
                ch(nc.vector.memset(both[32 * q:32 * q + 32, PT, :], 0.0))
            dve.sem_inc(picked, 1)
            dve.wait_ge(exped, 2)
            ch(nc.vector.tensor_reduce(out=sc[:, 3, :], in_=work[:, 0, :, 0:G], op=ALU.add, axis=AX.X))
            ch(TS(sc[:, 5, :], sc[:, 4, :], 1.0, None, ALU.add))
            ch(TT(sc[:, 5, :], sc[:, 5, :], sc[:, 3, :], ALU.mult))
            ch(nc.vector.reciprocal(gates[:, 0, :], sc[:, 5, :]))
            ch(TT(gates[:, 1, :], gates[:, 0, :], sc[:, 4, :], ALU.mult))
            dve.wait_ge(placed, 1)
            totals = k.ps[1][:, NT * E:2 * NT * E].rearrange("p (t e) -> p t e", e=E)
            before = work[:, 0, :, :]
            ch(nc.vector.memset(before[:, 0, :], 0.0))
            for t in range(1, NT):
                ch(TT(before[:, t, :], before[:, t - 1, :], totals[:, t - 1, :], ALU.add))
            cnt = counts[:, 5, :]
            ch(TT(cnt, before[:, PT, :], totals[:, PT, :], ALU.add))
            ch(TT(before, before, k.ps[1][:, 0:NT * E].rearrange("p (t e) -> p t e", e=E), ALU.add))
            ch(TS(counts[:, 0, :], cnt, 0.0, None, ALU.is_gt))
            for i in range(1, NT):
                ch(nc.vector.scalar_tensor_tensor(out=counts[:, 0, :], in0=cnt, scalar=float(i * P), in1=counts[:, 0, :],
                                                  op0=ALU.is_gt, op1=ALU.add))
            ch(TS(counts[:, 1, :], counts[:, 0, :], 0.0, 1.0, ALU.mult, ALU.add))
            ch(nc.vector.tensor_tensor_scan(counts[:, 2, :], counts[:, 1, :], counts[:, 0, :], 0.0, ALU.mult, ALU.add))
            ch(TT(counts[:, 3, :], counts[:, 2, :], counts[:, 0, :], ALU.subtract))
            ch(nc.vector.scalar_tensor_tensor(out=work[:, 4, :, :], in0=bcast(counts[:, 3, :], 1, [P, NT, E]), scalar=float(P),
                                              in1=before,
                                              op0=ALU.mult, op1=ALU.add))
            for j in range(TOPK):
                ch(TT(work[:, 5, :, :], work[:, 4, :, :], hot[:, j, :, :], ALU.mult))
                ch(nc.vector.tensor_reduce(out=slot[:, j, :], in_=work[:, 5, :, :], op=ALU.add, axis=AX.X))
            ch(nc.vector.tensor_copy(slot_i[:, :, :], slot[:, :, :]))
            dve.sem_inc(slots_ready, 1)
            ch(TT(big[:, :, :], bcast(counts[:, 2, :], 1, [P, BLOCKS, E]), bcast(step[:, :], 2, [P, BLOCKS, E]), ALU.is_le))
            ch(nc.vector.tensor_reduce(out=expert[:, 0:BLOCKS], in_=big[:, :, :], op=ALU.add, axis=AX.X))
            ch(TS(expert[:, 0:BLOCKS], expert[:, 0:BLOCKS], float(E - 1), None, ALU.min))
            ch(TS(counts[:, 4, 0:BLOCKS // 2 - 2], step[:, 4:BLOCKS:2], counts[:, 2, E - 1:E], None, ALU.is_lt))
            ch(nc.vector.tensor_reduce(out=counts[:, 4, E - 1:E], in_=counts[:, 4, 0:BLOCKS // 2 - 2], op=ALU.add, axis=AX.X))
            ch(TS(expert[:, BLOCKS:BLOCKS + 1], counts[:, 4, E - 1:E], 1.0, None, ALU.add))
            nc.vector.tensor_copy(expert_i[:, :], expert[0:1, 0:BLOCKS + 1]).then_inc(blocks_ready, 1)
            k.order_n["vector"] = ch.n


class ExpertBuffers:

    def __init__(self, k, a, tag, layer, ctx, expert_i):
        sb = lambda name, shape: ctx.enter_context(k.nc.sbuf_tensor(f"{tag}_{name}", shape, F32))
        self.a, self.layer, self.expert_i, self.sb = a, layer, expert_i, sb
        self.WGU = [sb(f"wgu{i}", [P, 2, DC, FF]) for i in range(2)]
        self.WD = [sb(f"wd{i}", [P, FF // P, D]) for i in range(2)]
        self.gu_in = [k.sem(f"{tag}_gu_landed{i}") for i in range(2)]
        self.d_in = [k.sem(f"{tag}_down_landed{i}") for i in range(2)]

    def expert(self, sp, j):
        return sp.value_load(self.expert_i[0:1, bass.ds(j, 1)], min_val=0, max_val=EXPERTS - 1)

    def load_gate_up(self, sp, u, e):
        for n, w in enumerate((self.a["moe_w_gate"], self.a["moe_w_up"])):
            sp.dma_start(self.WGU[u][:, n, :, :], w[self.layer, bass.ds(e, 1), :, :].rearrange("a (c p) f -> p (a c) f", p=P))\
                .then_inc(self.gu_in[u], 16)

    def load_down(self, sp, u, e):
        sp.dma_start(self.WD[u][:, :, :], self.a["moe_w_down"][self.layer, bass.ds(e, 1), :, :].rearrange("a (c p) n -> p (a c) n", p=P))\
            .then_inc(self.d_in[u], 16)


def expert_block(k, a, tag, layer, buffers, slots_x, slots_y, expert_i, column, prefetch):
    nc, sb = k.nc, buffers.sb
    NB = 2
    FC = FF // P
    half = DC // 2
    X = [sb(f"x{i}", [P, D]) for i in range(NB)]
    WGU, WD, gu_in, d_in = buffers.WGU, buffers.WD, buffers.gu_in, buffers.d_in
    XT = [sb(f"xt{i}", [P, DC, P]) for i in range(NB)]
    SG = [sb(f"sg{i}", [P, FF]) for i in range(NB)]
    HT = [sb(f"ht{i}", [P, FC, P]) for i in range(NB)]
    Y = [sb(f"y{i}", [P, D]) for i in range(NB)]
    buffers.rows = [*X, *Y, WD[0][:, 0, :]]
    x_in = [k.sem(f"{tag}_x_landed{i}") for i in range(NB)]
    y_out = [k.sem(f"{tag}_y_stored{i}") for i in range(NB)]
    x_turned, xt_a, xt_v = k.sem(f"{tag}_x_turned"), k.sem(f"{tag}_xt_act"), k.sem(f"{tag}_xt_dve")
    gu_done, silu_done, hid_done = k.sem(f"{tag}_gu_done"), k.sem(f"{tag}_silu_done"), k.sem(f"{tag}_hid_done")
    h_turned, ht_done = k.sem(f"{tag}_h_turned"), k.sem(f"{tag}_ht_done")
    down_done, y_a, y_v = k.sem(f"{tag}_down_done"), k.sem(f"{tag}_y_act"), k.sem(f"{tag}_y_dve")
    STEPS = (BLOCKS - 2) // 2
    assert BLOCKS % 2 == 0 and BLOCKS >= 6

    def steps_in_use(eng):
        return eng.value_load(expert_i[0:1, BLOCKS:BLOCKS + 1], min_val=1, max_val=STEPS)

    def wait(eng, sem, value):
        if not isinstance(value, int) or value > 0:
            eng.wait_ge(sem, value)

    with nc.Block() as block:
        @block.sync
        def _(sp):
            def load(i, c):
                j, u = 2 * i + c, c % 2
                e = buffers.expert(sp, j)
                wait(sp, x_turned, j - 1)
                sp.dma_start(X[u][:, :], slots_x[bass.ds(j * P, P), :]).then_inc(x_in[u], 16)
                wait(sp, gu_done, j - 1)
                buffers.load_gate_up(sp, u, e)
                wait(sp, down_done, j - 1)
                buffers.load_down(sp, u, e)

            for u in range(NB):
                sp.dma_start(X[u][:, :], slots_x[u * P:(u + 1) * P, :]).then_inc(x_in[u], 16)
            e = buffers.expert(sp, 1)
            buffers.load_gate_up(sp, 1, e)
            buffers.load_down(sp, 1, e)
            steps = steps_in_use(sp)
            with sp.Fori(1, STEPS + 1) as i:
                with sp.If(i <= steps):
                    load(i, 0)
                    load(i, 1)
            for halves in prefetch:
                k.load_weights(sp, halves)

        @block.scalar
        def _(act):
            def turn_out(i, c):
                j, u = 2 * i + c, c % 2
                act.wait_ge(x_turned, j + 1)
                for n in range(half, DC):
                    nc.scalar.activation(XT[u][:, n, :], k.ps[1][:, (n - half) * P:(n - half + 1) * P], ACT.Copy,
                                         scale=column[:, n:n + 1]).then_inc(xt_a, 1)

            def silu(i, c):
                j, u = 2 * i + c, c % 2
                act.wait_ge(gu_done, j + 1)
                wait(act, h_turned, j - 1)
                nc.scalar.activation(SG[u][:, :], k.ps[2 + u][:, 0:FF], ACT.Silu).then_inc(silu_done, 1)

            def y_store(i, c):
                j, u = 2 * i + c, c % 2
                act.wait_ge(down_done, j + 1)
                wait(act, y_out[u], 16 * (i + c // 2))
                nc.scalar.activation(Y[u][:, HB:D], k.ps[6][:, :], ACT.Copy).then_inc(y_a, 1)
                act.wait_ge(y_v, j + 1)
                act.wait_ge(y_a, j + 1)
                act.dma_start(slots_y[bass.ds(j * P, P), :], Y[u][:, :]).then_inc(y_out[u], 16)

            def step(i, c, last=False):
                silu(i, c)
                if not last:
                    turn_out(i, c + 1)
                if not (isinstance(i, int) and 2 * i + c == 0):
                    y_store(i, c - 1)

            turn_out(0, 0)
            steps = steps_in_use(act)
            for c in range(3):
                step(0, c)
            with act.Fori(1, STEPS) as i:
                with act.If(i < steps):
                    step(i, 1)
                    step(i, 2)
            step(steps, 1, last=True)
            y_store(steps, 1)

        @block.vector
        def _(dve):
            def turn_out(i, c):
                j, u = 2 * i + c, c % 2
                dve.wait_ge(x_turned, j + 1)
                nc.vector.tensor_tensor(XT[u][:, 0:half, :], k.ps[0][:, :].rearrange("p (c n) -> p c n", c=half),
                                        bcast(column[:, 0:half], 2, [P, half, P]), ALU.mult).then_inc(xt_v, 1)

            def times_up(i, c):
                j, u = 2 * i + c, c % 2
                dve.wait_ge(silu_done, j + 1)
                nc.vector.tensor_tensor(SG[u][:, :], SG[u][:, :], k.ps[2 + u][:, FF:2 * FF], ALU.mult).then_inc(hid_done, 1)

            def y_half(i, c):
                j, u = 2 * i + c, c % 2
                dve.wait_ge(down_done, j + 1)
                wait(dve, y_out[u], 16 * (i + c // 2))
                nc.vector.tensor_copy(Y[u][:, 0:HB], k.ps[5][:, :]).then_inc(y_v, 1)

            def hidden_out(i, c):
                j, u = 2 * i + c, c % 2
                dve.wait_ge(h_turned, j + 1)
                nc.vector.tensor_copy(HT[u][:, :, :], k.ps[4][:, 0:FF].rearrange("p (c n) -> p c n", c=FC)).then_inc(ht_done, 1)

            def step(i, c, last=False):
                if not last:
                    turn_out(i, c + 1)
                times_up(i, c)
                if not (isinstance(i, int) and 2 * i + c == 0):
                    y_half(i, c - 1)
                hidden_out(i, c)

            turn_out(0, 0)
            steps = steps_in_use(dve)
            for c in range(3):
                step(0, c)
            with dve.Fori(1, STEPS) as i:
                with dve.If(i < steps):
                    step(i, 1)
                    step(i, 2)
            step(steps, 1, last=True)
            y_half(steps, 1)

        @block.tensor
        def _(pe):
            def turn_x(i, c):
                j, u = 2 * i + c, c % 2
                pe.wait_ge(x_in[u], 16 * (i + c // 2 + 1))
                wait(pe, xt_a, half * j)
                wait(pe, xt_v, j)
                for n in range(DC):
                    last = nc.tensor.transpose(k.ps[n // half][:, (n % half) * P:(n % half + 1) * P],
                                               X[u][:, n * P:(n + 1) * P], k.ident[:, :])
                last.then_inc(x_turned, 1)

            def gate_up(i, c):
                j, u = 2 * i + c, c % 2
                pe.wait_ge(gu_in[u], 32 * (i + c // 2 + 1))
                pe.wait_ge(xt_a, half * (j + 1))
                pe.wait_ge(xt_v, j + 1)
                wait(pe, hid_done, j - 1)
                for n in range(DC):
                    last = nc.tensor.matmul(k.ps[2 + u][:, :].rearrange("p (w f) -> p w f", w=2), XT[u][:, n, :],
                                            WGU[u][:, :, n, :], start=(n == 0), stop=(n == DC - 1))
                last.then_inc(gu_done, 1)

            def down(i, c):
                j, u = 2 * i + c, c % 2
                pe.wait_ge(d_in[u], 16 * (i + c // 2 + 1))
                pe.wait_ge(ht_done, j + 1)
                wait(pe, y_a, j)
                wait(pe, y_v, j)
                for b in range(2):
                    for n in range(FC):
                        last = nc.tensor.matmul(k.ps[5 + b][:, :], HT[u][:, n, :], WD[u][:, n, b * HB:(b + 1) * HB],
                                                start=(n == 0), stop=(n == FC - 1))
                last.then_inc(down_done, 1)

            def turn_hidden(i, c):
                j, u = 2 * i + c, c % 2
                pe.wait_ge(hid_done, j + 1)
                wait(pe, ht_done, j)
                for n in range(FC):
                    last = nc.tensor.transpose(k.ps[4][:, n * P:(n + 1) * P], SG[u][:, n * P:(n + 1) * P], k.ident[:, :])
                last.then_inc(h_turned, 1)

            def step(i, c, last=False):
                gate_up(i, c)
                if not last:
                    turn_x(i, c + 1)
                if not (isinstance(i, int) and 2 * i + c == 0):
                    down(i, c - 1)
                turn_hidden(i, c)

            turn_x(0, 0)
            steps = steps_in_use(pe)
            for c in range(3):
                step(0, c)
            with pe.Fori(1, STEPS) as i:
                with pe.If(i < steps):
                    step(i, 1)
                    step(i, 2)
            step(steps, 1, last=True)
            down(steps, 1)
            for u in range(2):
                pe.wait_ge(y_out[u], 16 * (steps + 1))


def combine_block(k, a, tag, rows_in, slots_y, slot_i, gates, y):
    nc = k.nc
    landed = [k.sem(f"{tag}_gathered{i}") for i in range(4)]
    added = k.sem(f"{tag}_added")
    if y is not None:
        w_in, spread, ready, stored = k.sem("final_w_landed"), k.sem("final_w_spread"), k.sem("final_ready"), k.sem("final_stored")
        wrow = rows_in[4][0:1, :]
        norm = TileNorm(k, "final", [], y, ready=lambda t: (added, TOPK * (t + 1)))
    with nc.Block() as block:
        @block.gpsimd
        def _(pool):
            for t in range(NT):
                for j in range(TOPK):
                    n = TOPK * t + j
                    if n >= 4:
                        pool.wait_ge(added, n - 3)
                    pool.indirect_dma_start(rows_in[n % 4][0:rows(t), :], None, slots_y,
                                            bass.IndirectOffsetOnAxis(ap=slot_i[0:rows(t), j, t:t + 1], axis=0))\
                        .then_inc(landed[n % 4], 16)

        @block.vector
        def _(dve):
            ch = Chain(dve, k.order["vector"], k.order_n["vector"])

            def final(t):
                norm.inverse(dve, ch, t)
                dve.wait_ge(spread, 1)
                for i in range(2):
                    part = slice(i * HB, (i + 1) * HB)
                    nc.vector.scalar_tensor_tensor(out=y[:, t, part], in0=k.h[:, t, part], scalar=k.r[:, t:t + 1],
                                                   in1=k.ps[i][:, :], op0=ALU.mult, op1=ALU.mult).then_inc(ready, 1)

            for t in range(NT):
                for j in range(TOPK):
                    n = TOPK * t + j
                    dve.wait_ge(landed[n % 4], 16 * (n // 4 + 1))
                    if n:
                        dve.wait_ge(added, n)
                    part = k.h[0:rows(t), t, :]
                    nc.vector.scalar_tensor_tensor(out=part, in0=rows_in[n % 4][0:rows(t), :], scalar=gates[0:rows(t), j, t:t + 1],
                                                   in1=part, op0=ALU.mult, op1=ALU.add).then_inc(added, 1)
                if y is not None and t:
                    final(t - 1)
            if y is not None:
                final(PT)
            k.order_n["vector"] = ch.n

        if y is not None:
            @block.sync
            def _(sp):
                sp.dma_start(wrow[:, :], a["final_norm_w"].rearrange("(a n) -> a n", a=1)).then_inc(w_in, 16)
                for t in range(NT):
                    sp.wait_ge(ready, 2 * (t + 1))
                    dst = a["y_prompt"][0, t * P:(t + 1) * P, :] if t < PT else a["y_sample"].rearrange("b t d -> (b t) d")
                    sp.dma_start(dst, y[0:rows(t), t, :]).then_inc(stored, 16)
                sp.wait_ge(stored, 16 * NT)

            @block.tensor
            def _(pe):
                pe.wait_ge(w_in, 16)
                for i in range(2):
                    last = nc.tensor.matmul(k.ps[i][:, :], k.ones[0:1, :], wrow[0:1, i * HB:(i + 1) * HB], start=True, stop=True)
                last.then_inc(spread, 1)

            @block.scalar
            def _(act):
                for t in range(NT):
                    norm.root(act, t)



def kvq_block(k, a, kv_xT, q_xT, ks, v, kT, qT, o, smp_q):
    nc = k.nc
    done, out_v, out_a = k.sem("kvq_done"), k.sem("kvq_out_dve"), k.sem("kvq_out_act")
    turned, kt_out = k.sem("kT_turned"), k.sem("kT_out")
    qs_copied, qs_turned = k.sem("sample_q_copied"), k.sem("sample_q_turned")
    stored = k.sem("kv_stored")
    order = [("k", i, t) for i in range(2) for t in range(NT)]
    for h in range(HEADS):
        order += ([("qs", h // 4)] if h % 4 == 0 else []) + [("q", h)]
    order += [("v", i, t) for i in range(2) for t in range(NT)]
    count = {u: n + 1 for n, u in enumerate(order)}
    nv, outs = 0, {}
    for u in order:
        if u[0] == "qs":
            outs[u] = (out_a, 10 * u[1] + 4)
        elif u[0] == "q":
            outs[u] = (out_a, 10 * (u[1] // 4) + 2 * (u[1] % 4 + 1) + (2 if u[1] % 4 else 0))
        else:
            nv += 1
            outs[u] = (out_v, nv)
    bank_of, before, last_in, n = {}, {}, {}, 0
    for u in order:
        if u[0] == "q":
            bank_of[u] = 2 + u[1] % 2
        elif u[0] == "qs":
            bank_of[u] = 4
        else:
            bank_of[u] = n % 2
            n += 1
        before[u] = last_in.get(bank_of[u])
        last_in[bank_of[u]] = u
    with nc.Block() as block:
        @block.tensor
        def _(pe):
            def begin(u):
                if before[u] is not None:
                    pe.wait_ge(*outs[before[u]])
                return k.ps[bank_of[u]]

            def by_token(kind):
                for i in range(2):
                    w = k.take_weights(pe)
                    for t in range(NT):
                        project_tokens(nc, begin((kind, i, t)), kv_xT, w, t).then_inc(done, 1)
                    k.w_done.append((done, count[(kind, i, NT - 1)]))

            by_token("k")
            for h in range(HEADS):
                if h % 4 == 0:
                    w = k.take_weights(pe)
                    k.w_done.append((done, count[("q", h + 3)]))
                    project_tokens(nc, begin(("qs", h // 4)), q_xT, w, PT).then_inc(done, 1)
                bank = begin(("q", h))
                for c in range(DC):
                    last = nc.tensor.matmul(bank[:, :], w[:, c, (h % 4) * P:(h % 4 + 1) * P], q_xT[:, c, 0:SEQ],
                                            start=(c == 0), stop=(c == DC - 1))
                last.then_inc(done, 1)
                if h % 4 == 0:
                    pe.wait_ge(qs_copied, h // 4 + 1)
                    nc.tensor.transpose(k.ps[4][:, P:2 * P], smp_q[:, :], k.ident[:, :]).then_inc(qs_turned, 1)
            pe.wait_ge(out_v, 2 * NT)
            for h in range(HEADS):
                if h:
                    pe.wait_ge(kt_out, 2 * h)
                for t in range(PT):
                    nc.tensor.transpose(k.ps[5][:, t * P:(t + 1) * P], ks[:, t, h * P:(h + 1) * P], k.ident[:, :])
                nc.tensor.transpose(k.ps[6][:, 0:SMP], ks[0:SMP, PT, h * P:(h + 1) * P], k.ident[0:SMP, 0:SMP]).then_inc(turned, 1)
            by_token("v")

        @block.sync
        def _(sp):
            for i in range(1, 2):
                k.load_weights(sp, column_halves(a["b_w_q"][0], i * HB))
            k.load_weights(sp, column_halves(a["w_kv"], D))
            k.load_weights(sp, column_halves(a["w_kv"], D + HB))

            def store(src, prompt, sample):
                sp.dma_start(a[prompt][0].rearrange("(t p) h n -> p t (h n)", p=P), src[:, 0:PT, :]).then_inc(stored, 16)
                sp.dma_start(a[sample].rearrange("b t h n -> (b t) (h n)"), src[0:SMP, PT, :]).then_inc(stored, 16)

            sp.wait_ge(out_v, 2 * NT)
            store(ks, "k_prompt", "k_sample")
            for i in range(2):
                k.load_weights(sp, column_halves(a["b_w_o"][0], i * HB))
            sp.wait_ge(out_v, 4 * NT)
            store(v, "v_prompt", "v_sample")
            sp.wait_ge(stored, 64)

        @block.vector
        def _(dve):
            for q in range(1, 4):
                nc.vector.memset(o[32 * q:32 * q + 32, PT, :], 0.0)
            for c in range(2):
                nc.vector.memset(qT[1 - c][c * P // 2:(c + 1) * P // 2, :, :], 0.0)
            for kind, dst in (("k", ks), ("v", v)):
                for i in range(2):
                    for t in range(NT):
                        dve.wait_ge(done, count[(kind, i, t)])
                        for src, part in token_parts(k.ps[bank_of[(kind, i, t)]], dst, i, t):
                            last = nc.vector.tensor_copy(part, src)
                        last.then_inc(out_v, 1)
                if kind == "k":
                    for i in range(2):
                        dve.wait_ge(done, count[("qs", i)])
                        if i:
                            dve.wait_ge(qs_turned, i)
                        nc.vector.tensor_copy(smp_q[:, :], k.ps[4][:, 0:P]).then_inc(qs_copied, 1)

        @block.scalar
        def _(act):
            for h in range(HEADS):
                act.wait_ge(done, count[("q", h)])
                for c in range(2):
                    rows_c = slice(c * P // 2, (c + 1) * P // 2)
                    nc.scalar.activation(qT[c][rows_c, h, 0:SEQ], k.ps[bank_of[("q", h)]][rows_c, :], ACT.Copy, scale=0.125)\
                        .then_inc(out_a, 1)
                if h % 4 == 0:
                    act.wait_ge(qs_turned, h // 4 + 1)
                    for c in range(2):
                        rows_c = slice(c * P // 2, (c + 1) * P // 2)
                        nc.scalar.activation(qT[c][rows_c, h:h + 4, SEQ:TOK],
                                             k.ps[4][rows_c, P:2 * P].rearrange("p (h n) -> p h n", n=SMP), ACT.Copy,
                                             scale=0.125).then_inc(out_a, 1)
            for h in range(HEADS):
                act.wait_ge(turned, h + 1)
                nc.scalar.activation(kT[:, h, 0:SEQ], k.ps[5][:, :], ACT.Copy).then_inc(kt_out, 1)
                nc.scalar.activation(kT[:, h, SEQ:TOK], k.ps[6][:, 0:SMP], ACT.Copy).then_inc(kt_out, 1)



class KeyPages:
    SLOTS = 4

    def __init__(self, k, a, ctx):
        self.k, self.cache = k, a["cache_k"]
        self.table_view = a["page_table"].rearrange("(x b) n -> x (b n)", x=1)
        self.table = ctx.enter_context(k.nc.sbuf_tensor("sa_pages", [1, DEC_B * PAGES], I32))
        self.table_in = k.sem("sa_page_table_landed")
        self.landed = [k.sem(f"sa_k_landed{i}") for i in range(self.SLOTS)]

    def ring(self):
        return self.k.wring[self.k.w_issued % WEIGHT_SLOTS][:, :, :].rearrange("p (r c) n -> p r (c n)", r=self.SLOTS)

    def page(self, sp, b, p):
        return sp.value_load(self.table[0:1, bass.ds(b * PAGES + p, 1)], min_val=0, max_val=self.cache.shape[0] - 1)

    def load(self, sp, page, p):
        src = self.cache[bass.ds(page, 1), :, :, :].rearrange("a p h n -> (a p) (h n)")
        sp.dma_start(self.ring()[:, p % self.SLOTS, :], src).then_inc(self.landed[p % self.SLOTS], 16)



def prompt_attention(k, a, rep, v, kT, qT, qz, kTs, o, keys):
    nc = k.nc
    units = [(h, i) for h in range(HEADS) for i in range(PT)]
    N = len(units)
    half = P // 2
    NS = DC // 2
    with ExitStack() as tmp_ctx:
        def sb(name, shape):
            return tmp_ctx.enter_context(nc.sbuf_tensor(name, shape, F32))
        dist = sb("pa_dist", [P, SEQ])
        bias = [sb(f"pa_bias{i}", [P, SEQ]) for i in range(2)]
        spare = k.xT[:, :, :].rearrange("p c n -> p (c n)")
        S = [spare[:, i * 2 * SEQ:(i + 1) * 2 * SEQ].rearrange("p (c n) -> p c n", c=2) for i in range(NS)]
        aT = [sb(f"pa_at{i}", [P, PT, P]) for i in range(2)]
        st = [sb(f"pa_stat{i}", [P, 10]) for i in range(NS)]
        d_in, bias_ready = k.sem("pa_dist_landed"), k.sem("pa_bias")
        scored, biased, negated, exped = k.sem("pa_scored"), k.sem("pa_biased"), k.sem("pa_negated"), k.sem("pa_exp")
        combined, turned, at_out, o_done, o_out = (k.sem(f"pa_{n}") for n in ("combined", "turned", "at_out", "o_done", "o_out"))
        with nc.Block() as block:
            @block.sync
            def _(sp):
                sp.dma_start(dist[:, :], a["const_dist"]).then_inc(d_in, 16)
                sp.dma_start(keys.table[:, :], keys.table_view).then_inc(keys.table_in, 16)
                sp.wait_ge(keys.table_in, 16)
                for p in range(keys.SLOTS):
                    keys.load(sp, keys.page(sp, 0, p), p)

            @block.gpsimd
            def _(pool):
                pool.wait_ge(d_in, 16)
                for h in range(HEADS):
                    if h >= 2:
                        pool.wait_ge(biased, 2 * PT * (h - 1))
                    nc.gpsimd.tensor_scalar(bias[h % 2][:, :], dist[:, :], -(2.0 ** -(h + 1)), None, ALU.mult).then_inc(bias_ready, 1)

            @block.tensor
            def _(pe):
                def scores(n):
                    h, i = units[n]
                    w = (i + 1) * P
                    if n >= 2:
                        pe.wait_ge(biased, 2 * (n - 1))
                    for c in range(2):
                        last = nc.tensor.matmul(k.ps[2 * (n % 2) + c][:, 0:w], qT[c][:, h, i * P:(i + 1) * P], kT[:, h, 0:w],
                                                start=True, stop=True)
                        last.then_inc(scored, 1)

                def turn(n):
                    h, i = units[n]
                    pe.wait_ge(combined, n + 1)
                    if n >= 2:
                        pe.wait_ge(at_out, n - 1)
                    for j in range(i + 1):
                        last = nc.tensor.transpose(k.ps[4 + n % 2][:, j * P:(j + 1) * P], S[n % NS][:, 0, j * P:(j + 1) * P], k.ident[:, :])
                    last.then_inc(turned, 1)

                def values(n):
                    h, i = units[n]
                    pe.wait_ge(at_out, n + 1)
                    if n >= 2:
                        pe.wait_ge(o_out, n - 1)
                    for j in range(i + 1):
                        last = nc.tensor.matmul(k.ps[6 + n % 2][:, 0:P], aT[n % 2][:, j, :], v[:, j, h * P:(h + 1) * P],
                                                start=(j == 0), stop=(j == i))
                    last.then_inc(o_done, 1)

                scores(0)
                scores(1)
                for n in range(N):
                    if n + 2 < N:
                        scores(n + 2)
                    turn(n)
                    if n:
                        values(n - 1)
                values(N - 1)

            @block.vector
            def _(dve):
                ch = Chain(dve, k.order["vector"], k.order_n["vector"])
                ch(nc.vector.memset(qz[:, :, :, :], 0.0))
                for c in range(2):
                    part = slice(c * half, (c + 1) * half)
                    ch(nc.vector.tensor_copy(qz[part, :, :, c * DEC_T:(c + 1) * DEC_T],
                                             qT[c][part, :, SEQ:TOK].rearrange("p h (b t) -> p b h t", t=DEC_T)))
                ch(nc.vector.tensor_copy(kTs[:, :, :], kT[:, :, SEQ:TOK]))

                def bias_max(n):
                    h, i = units[n]
                    w = (i + 1) * P
                    dve.wait_ge(bias_ready, h + 1)
                    if n >= NS:
                        dve.wait_ge(turned, n - NS + 1)
                    for c in range(2):
                        dve.wait_ge(scored, 2 * n + c + 1)
                        nc.vector.tensor_tensor_reduce(out=S[n % NS][:, c, 0:w], in0=k.ps[2 * (n % 2) + c][:, 0:w],
                                                       in1=bias[h % 2][:, (PT - 1 - i) * P:SEQ], scale=1.0, scalar=-3e38,
                                                       op0=ALU.add, op1=ALU.max,
                                                       accum_out=st[n % NS][:, c:c + 1]).then_inc(biased, 1)
                    dve.wait_ge(biased, 2 * (n + 1))
                    nc.vector.tensor_scalar(st[n % NS][:, 2:4], st[n % NS][:, 0:2], -1.0, None, ALU.mult).then_inc(negated, 1)

                def combine(n):
                    h, i = units[n]
                    w = (i + 1) * P
                    s = st[n % NS]
                    dve.wait_ge(exped, 2 * (n + 1))
                    ch(nc.vector.reciprocal(s[:, 6:8], s[:, 4:6]))
                    ch(nc.vector.tensor_tensor(s[:, 8:9], s[:, 7:8], rep[:, 2 * P:2 * P + 1], ALU.mult))
                    ch(nc.vector.tensor_scalar(S[n % NS][:, 1, 0:w], S[n % NS][:, 1, 0:w], s[:, 8:9], None, ALU.mult))
                    nc.vector.scalar_tensor_tensor(out=S[n % NS][:, 0, 0:w], in0=S[n % NS][:, 0, 0:w], scalar=s[:, 6:7],
                                                   in1=S[n % NS][:, 1, 0:w], op0=ALU.mult, op1=ALU.add).then_inc(combined, 1)

                bias_max(0)
                for n in range(N):
                    if n + 1 < N:
                        bias_max(n + 1)
                    combine(n)
                k.order_n["vector"] = ch.n

            @block.scalar
            def _(act):
                def exps(n):
                    h, i = units[n]
                    w = (i + 1) * P
                    act.wait_ge(negated, n + 1)
                    for c in range(2):
                        nc.scalar.activation(S[n % NS][:, c, 0:w], S[n % NS][:, c, 0:w], ACT.Exp, bias=st[n % NS][:, 2 + c:3 + c],
                                             accum_out=st[n % NS][:, 4 + c:5 + c]).then_inc(exped, 1)

                def turned_out(n):
                    h, i = units[n]
                    act.wait_ge(turned, n + 1)
                    if n >= 2:
                        act.wait_ge(o_out, n - 1)
                    nc.scalar.activation(aT[n % 2][:, 0:i + 1, :], k.ps[4 + n % 2][:, 0:(i + 1) * P].rearrange("p (j n) -> p j n", n=P),
                                         ACT.Copy).then_inc(at_out, 1)

                def out(n):
                    h, i = units[n]
                    act.wait_ge(o_done, n + 1)
                    nc.scalar.activation(o[:, i, h * P:(h + 1) * P], k.ps[6 + n % 2][:, 0:P], ACT.Copy)
                    nc.scalar.activation(aT[n % 2][:, 0, :], k.ps[6 + n % 2][:, 0:P], ACT.Square,
                                         accum_out=k.head_squares[:, i, h:h + 1]).then_inc(o_out, 1)

                exps(0)
                for n in range(N):
                    if n + 1 < N:
                        exps(n + 1)
                    turned_out(n)
                    if n:
                        out(n - 1)
                out(N - 1)



def sample_attention(k, a, rep, qz, kTs, o, keys):
    nc = k.nc
    HT = HEADS * DEC_T
    QUAD = 32
    KRING, VRING, GROUP = keys.SLOTS, 8, 4
    GROUPS_ = PAGES // GROUP
    KEYS = PAST + DEC_T
    N5 = GROUPS_ + 1
    half = HEADS // 2
    with ExitStack() as tmp_ctx:
        def sb(name, shape, dt=F32):
            return tmp_ctx.enter_context(nc.sbuf_tensor(name, shape, dt))
        K = keys.ring()
        V = [sb(f"sa_v{i}", [P, D]) for i in range(VRING)]
        KT = sb("sa_kT", [P, HEADS, GROUP * P])
        S = sb("sa_scores", [P, KEYS])
        W = sb("sa_w", [P, KEYS])
        alibi = sb("sa_alibi", [P, KEYS])
        table = sb("sa_table", [P, 2 + HEADS + DEC_B * SMP])
        red = sb("sa_red", [P, 16])
        AT = sb("sa_at", [P, PAGES + 1, HT])
        Q = sb("sa_q", [P, HEADS, QUAD])
        knew, vnew = sb("sa_knew", [P, HEADS, DEC_T]), sb("sa_vnew", [P, D])
        place = sb("sa_place", [P, SMP])
        own = sb("sa_own", [P, D])
        own_head = table[:, 2:2 + HEADS]
        places = table[:, 2 + HEADS:].rearrange("p (b n) -> p b n", b=DEC_B)
        c_in = k.sem("sa_const_landed")
        k_in, v_in = keys.landed, [k.sem(f"sa_v_landed{i}") for i in range(VRING)]
        vn_in = k.sem("sa_vnew_landed")
        names = ("cleared", "turned_a", "turned_b", "kt_out_a", "kt_out_b", "q_ready", "scored", "biased", "max_ready",
                 "exped", "normed", "w_turned", "at_out", "valued", "picked", "place_ready", "summed", "added")
        (cleared, turned_a, turned_b, kt_out_a, kt_out_b, q_ready, scored, biased, max_ready, exped, normed, w_turned,
         at_out, valued, picked, place_ready, summed, added) = (k.sem(f"sa_{n}") for n in names)

        def wait(eng, sem, value):
            if not isinstance(value, int) or value > 0:
                eng.wait_ge(sem, value)

        with nc.Block() as block:
            @block.sync
            def _(sp):
                sp.dma_start(alibi[:, :], a["const_rows"][:, 0:KEYS]).then_inc(c_in, 16)
                sp.dma_start(table[:, :], a["const_rows"][:, KEYS:]).then_inc(c_in, 16)
                sp.wait_ge(cleared, 3)

                def load_k(b, p):
                    if isinstance(b, int) and b * PAGES + p < KRING:
                        return
                    page = keys.page(sp, b, p)
                    wait(sp, turned_b, PAGES * b + p - KRING + 1)
                    keys.load(sp, page, p)

                def load_v(b, g, valued_before):
                    for p in range(GROUP * g, GROUP * (g + 1)):
                        page = keys.page(sp, b, p)
                        wait(sp, valued, valued_before)
                        sp.dma_start(V[p % VRING][:, :], a["cache_v"][bass.ds(page, 1), :, :, :].rearrange("a p h n -> (a p) (h n)"))\
                            .then_inc(v_in[p % VRING], 16)

                def iteration(b, scores, values):
                    for g in range(GROUPS_):
                        if scores:
                            for p in range(GROUP * g, GROUP * (g + 1)):
                                load_k(b, p)
                        if values and g < GROUPS_ - 1:
                            load_v(b - 1, g + 1, N5 * (b - 1) + g)
                        if scores and g == GROUPS_ - 1:
                            load_v(b, 0, N5 * (b - 1) + g)
                        if values and g == 1:
                            wait(sp, valued, N5 * (b - 1))
                            sp.dma_start(vnew[0:DEC_T, :], a["v_sample"][bass.ds(b - 1, 1), :, :, :].rearrange("a t h n -> (a t) (h n)"))\
                                .then_inc(vn_in, 16)

                iteration(0, True, False)
                iteration(1, True, True)
                with sp.Fori(2, DEC_B) as b:
                    iteration(b, True, True)
                iteration(DEC_B, False, True)

            @block.scalar
            def _(act):
                def iteration(b, scores, values):
                    if values:
                        act.wait_ge(max_ready, 2 * b)
                        wait(act, w_turned, N5 * (b - 1))
                        nc.scalar.activation(W[:, :], S[:, :], ACT.Exp, bias=red[:, 6:7], accum_out=red[:, 7:8]).then_inc(exped, 1)
                    for p in range(PAGES if scores else 0):
                        act.wait_ge(turned_a, PAGES * b + p + 1)
                        nc.scalar.activation(KT[:, 0:half, (p % GROUP) * P:(p % GROUP + 1) * P],
                                             k.ps[2 * (p % 2)][:, :].rearrange("p (h n) -> p h n", h=half), ACT.Copy).then_inc(kt_out_a, 1)

                iteration(0, True, False)
                iteration(1, True, True)
                with act.Fori(2, DEC_B) as b:
                    iteration(b, True, True)
                iteration(DEC_B, False, True)

            @block.vector
            def _(dve):
                nc.vector.memset(Q[:, :, :], 0.0)
                nc.vector.memset(vnew[:, :], 0.0).then_inc(cleared, 1)
                nc.vector.memset(AT[:, PAGES, :], 0.0).then_inc(cleared, 1)
                nc.vector.memset(o[0:SMP, PT, :], 0.0).then_inc(cleared, 1)
                dve.wait_ge(cleared, 3)
                dve.wait_ge(c_in, 32)
                nc.vector.tensor_scalar(red[:, 9:10], table[:, 1:2], rep[:, 2 * P:2 * P + 1], table[:, 0:1],
                                        ALU.mult, ALU.add).then_inc(normed, 1)

                def bias_max(b, g):
                    w = GROUP * P if g < GROUPS_ else DEC_T
                    if g == 0:
                        wait(dve, exped, b)
                    dve.wait_ge(scored, N5 * b + g + 1)
                    nc.vector.memset(red[:, 11:12], 0.0)
                    part = slice(g * GROUP * P, g * GROUP * P + w)
                    nc.vector.tensor_tensor_reduce(out=S[:, part], in0=k.ps[4][:, 0:w], in1=alibi[:, part], scale=1.0,
                                                   scalar=-3e38, op0=ALU.add, op1=ALU.max,
                                                   accum_out=red[:, g:g + 1]).then_inc(biased, 1)

                def weights_out(b, g):
                    n = P if g < GROUPS_ else DEC_T
                    w = GROUP if g < GROUPS_ else 1
                    dve.wait_ge(w_turned, N5 * (b - 1) + g + 1)
                    src = k.ps[7][0:n, 0:w * P].rearrange("p (a x) -> p a x", x=QUAD)[:, :, 0:16]
                    src = src.rearrange("p a (h c t) -> p a h t c", h=2, c=2)
                    dst = AT[0:n, GROUP * g:GROUP * g + w, :].rearrange("p w (j h t) -> p (w j) h t", h=2, t=DEC_T)
                    nc.vector.tensor_reduce(out=dst, in_=src, op=ALU.add, axis=AX.X).then_inc(at_out, 1)

                def iteration(b, scores, values):
                    if scores:
                        wait(dve, scored, N5 * b)
                        for n in range(2):
                            nc.vector.tensor_copy(Q[:, n:HEADS:2, 8 * n:8 * n + 8],
                                                  qz[:, bass.ds(b, 1), n:HEADS:2, :].rearrange("p a h n -> p (a h) n"))
                        nc.vector.tensor_copy(knew[:, :, :], kTs[:, :, bass.ds(b * DEC_T, DEC_T)]).then_inc(q_ready, 1)
                    if values:
                        wait(dve, summed, 2 * (b - 1))
                        nc.vector.tensor_copy(place[:, :], places[:, bass.ds(b - 1, 1), :].rearrange("p a n -> p (a n)"))\
                            .then_inc(place_ready, 1)
                    for g in range(GROUPS_):
                        for p in range(GROUP * g, GROUP * (g + 1)):
                            if values and p % GROUP == GROUP - 1:
                                if g == 0:
                                    dve.wait_ge(exped, b)
                                    nc.vector.reciprocal(red[:, 8:9], red[:, 7:8]).then_inc(normed, 1)
                                    dve.wait_ge(normed, 3 * b - 1)
                                    nc.vector.tensor_tensor(red[:, 10:11], red[:, 8:9], red[:, 9:10], ALU.mult).then_inc(normed, 1)
                                    dve.wait_ge(normed, 3 * b)
                                    nc.vector.tensor_scalar(W[:, :], W[:, :], red[:, 10:11], None, ALU.mult).then_inc(normed, 1)
                                weights_out(b, g)
                            if scores:
                                dve.wait_ge(turned_b, PAGES * b + p + 1)
                                nc.vector.tensor_copy(KT[:, half:HEADS, (p % GROUP) * P:(p % GROUP + 1) * P],
                                                      k.ps[2 * (p % 2) + 1][:, :].rearrange("p (h n) -> p h n", h=half))\
                                    .then_inc(kt_out_b, 1)
                        if scores:
                            bias_max(b, g)
                    if values:
                        weights_out(b, GROUPS_)
                    if scores:
                        bias_max(b, GROUPS_)
                        dve.wait_ge(biased, N5 * (b + 1))
                        nc.vector.tensor_reduce(out=red[:, 5:6], in_=red[:, 0:5], op=ALU.max, axis=AX.X).then_inc(max_ready, 1)
                        dve.wait_ge(max_ready, 2 * b + 1)
                        nc.vector.tensor_scalar(red[:, 6:7], red[:, 5:6], -1.0, None, ALU.mult).then_inc(max_ready, 1)
                    if values:
                        dve.wait_ge(valued, N5 * b)
                        wait(dve, summed, 2 * (b - 1))
                        for n in range(2):
                            nc.vector.tensor_tensor(own[:, n * HB:(n + 1) * HB].rearrange("p (h n) -> p h n", n=P),
                                                    k.ps[5 + n][:, :].rearrange("p (h n) -> p h n", n=P),
                                                    bcast(own_head[:, half * n:half * (n + 1)], 2, [P, half, P]), ALU.mult)\
                                .then_inc(picked, 1)
                        for n, bank in enumerate((7, 4)):
                            dve.wait_ge(summed, 2 * (b - 1) + n + 1)
                            part = o[0:SMP, PT, n * HB:(n + 1) * HB]
                            nc.vector.tensor_tensor(part, part, k.ps[bank][0:SMP, :], ALU.add).then_inc(added, 1)

                iteration(0, True, False)
                iteration(1, True, True)
                with dve.Fori(2, DEC_B) as b:
                    iteration(b, True, True)
                iteration(DEC_B, False, True)

            @block.tensor
            def _(pe):
                def turn(b, p):
                    pe.wait_ge(k_in[p % KRING], 16 * (4 * b + p // KRING + 1))
                    for n, (free, signal) in enumerate(((kt_out_a, turned_a), (kt_out_b, turned_b))):
                        wait(pe, free, PAGES * b + p - 1)
                        for h in range(half):
                            hh = n * half + h
                            last = nc.tensor.transpose(k.ps[2 * (p % 2) + n][:, h * P:(h + 1) * P],
                                                       K[:, p % KRING, hh * P:(hh + 1) * P], k.ident[:, :])
                        last.then_inc(signal, 1)

                def score(b, g):
                    wait(pe, biased, N5 * b + g)
                    if g == 0:
                        pe.wait_ge(q_ready, b + 1)
                        wait(pe, added, 2 * (b - 1))
                    if g < GROUPS_:
                        pe.wait_ge(kt_out_a, PAGES * b + GROUP * (g + 1))
                        pe.wait_ge(kt_out_b, PAGES * b + GROUP * (g + 1))
                    for n in range(2):
                        for j in range(4):
                            h = 2 * j + n
                            rhs = KT[:, h, :] if g < GROUPS_ else knew[:, h, :]
                            w = GROUP * P if g < GROUPS_ else DEC_T
                            last = nc.tensor.matmul(k.ps[4][QUAD * j:QUAD * (j + 1), 0:w], Q[:, h, :], rhs, start=(n == 0), stop=(n == 1))
                    last.then_inc(scored, 1)

                def turn_weights(b, g):
                    if g == 0:
                        pe.wait_ge(normed, 3 * b + 1)
                        wait(pe, added, 2 * (b - 1))
                    wait(pe, at_out, N5 * (b - 1) + g)
                    if g < GROUPS_:
                        for n in range(GROUP):
                            p = GROUP * g + n
                            last = nc.tensor.transpose(k.ps[7][:, n * P:(n + 1) * P], W[:, p * P:(p + 1) * P], k.ident[:, :])
                    else:
                        last = nc.tensor.transpose(k.ps[7][0:DEC_T, 0:P], W[:, PAST:KEYS], k.ident[:, :])
                    last.then_inc(w_turned, 1)

                def value(b, g):
                    if g == 0:
                        wait(pe, picked, 2 * (b - 1))
                    pe.wait_ge(at_out, N5 * (b - 1) + g + 1)
                    if g < GROUPS_:
                        for p in range(GROUP * g, GROUP * (g + 1)):
                            pe.wait_ge(v_in[p % VRING], 16 * (2 * (b - 1) + p // VRING + 1))
                    else:
                        pe.wait_ge(vn_in, 16 * b)
                    pages = range(GROUP * g, GROUP * (g + 1)) if g < GROUPS_ else (PAGES,)
                    for n in range(2):
                        for p in pages:
                            q = p % 4
                            rhs = (V[p % VRING] if p < PAGES else vnew)[:, n * HB:(n + 1) * HB]
                            last = nc.tensor.matmul(k.ps[5 + n][QUAD * q:QUAD * (q + 1), :], AT[:, p, :], rhs, start=(p < 4),
                                                    stop=(p == PAGES or (p >= PAGES - 3)))
                    last.then_inc(valued, 1)

                def iteration(b, scores, values):
                    for g in range(GROUPS_):
                        for p in range(GROUP * g, GROUP * (g + 1)):
                            if values and p % GROUP == GROUP - 1:
                                turn_weights(b, g)
                            if scores:
                                turn(b, p)
                        if values:
                            value(b, g)
                        if scores:
                            score(b, g)
                    if values:
                        turn_weights(b, GROUPS_)
                    if scores:
                        score(b, GROUPS_)
                    if values:
                        value(b, GROUPS_)
                        pe.wait_ge(place_ready, b)
                        pe.wait_ge(at_out, N5 * b)
                        pe.wait_ge(biased, N5 * (b + 1) if scores else N5 * b)
                        for n, bank in enumerate((7, 4)):
                            pe.wait_ge(picked, 2 * (b - 1) + n + 1)
                            nc.tensor.matmul(k.ps[bank][0:SMP, :], place[:, :], own[:, n * HB:(n + 1) * HB], start=True, stop=True)\
                                .then_inc(summed, 1)

                iteration(0, True, False)
                iteration(1, True, True)
                with pe.Fori(2, DEC_B) as b:
                    iteration(b, True, True)
                iteration(DEC_B, False, True)



def trunk(nc, a):
    with ExitStack() as ctx:
        k = Core(nc, ctx)
        rep = k.sb("row_gains", [P, 2 * P + 2])
        slots_x = nc.dram_tensor("slots_x", [SLOTS, D], F32, kind="Internal").ap()
        slots_y = nc.dram_tensor("slots_y", [SLOTS, D], F32, kind="Internal").ap()
        zeroed = k.sem("slots_zeroed")
        setup(k, a, rep)
        with ExitStack() as layer:
            v = layer.enter_context(nc.sbuf_tensor("hgrn_v", [P, NT, D], F32))
            with k.stage(), nc.sbuf_tensor("hgrn_g", [P, NT, D], F32) as g:
                norm_block(k, "mix0", [(k.cw[:, 0, :], k.xT)], v)
                hgrn_block(k, a, v, g, v, rep[:, 0:P], (slots_x, slots_y), zeroed)
                by_head = lambda ap: ap.rearrange("p (h n) -> p h n", n=P)
                mix_out_block(k, "out0", v, lambda t: by_head(g[:, t, :]), EPS, [(k.cw[:, 3, :], k.xT)])
            kv = a["w_kv"]
            with k.stage():
                moe_blocks(k, a, 0, v, slots_x, slots_y,
                           [column_halves(kv, 0), column_halves(kv, HB), column_halves(a["b_w_q"][0], 0)], final=False)
        with ExitStack() as layer:
            sb = lambda name, shape: layer.enter_context(nc.sbuf_tensor(name, shape, F32))
            o = sb("attn_o", [P, NT, D])
            with k.stage(), ExitStack() as attention:
                sb = lambda name, shape: attention.enter_context(nc.sbuf_tensor(name, shape, F32))
                qz, kTs = sb("attn_qz", [P, DEC_B, HEADS, 2 * DEC_T]), sb("attn_kTs", [P, HEADS, SMP])
                keys = KeyPages(k, a, attention)
                with ExitStack() as prompt:
                    sb = lambda name, shape: prompt.enter_context(nc.sbuf_tensor(name, shape, F32))
                    kT, qT = sb("attn_kT", [P, HEADS, TOK]), [sb(f"attn_qT{c}", [P, HEADS, TOK]) for c in range(2)]
                    v = sb("attn_v", [P, NT, D])
                    with ExitStack() as proj:
                        sb = lambda name, shape: proj.enter_context(nc.sbuf_tensor(name, shape, F32))
                        q_xT = sb("attn_q_xT", [P, DC, TOK])
                        norm_block(k, "mix1", [(k.cw[:, 2, :], k.xT), (k.cw[:, 1, :], q_xT)], o)
                        kvq_block(k, a, k.xT, q_xT, o, v, kT, qT, o, sb("attn_smp_q", [P, P]))
                    prompt_attention(k, a, rep, v, kT, qT, qz, kTs, o, keys)
                sample_attention(k, a, rep, qz, kTs, o, keys)
                subln = bcast(rep[:, P:2 * P], 1, [P, HEADS, P])
                mix_out_block(k, "out1", o, lambda t: subln, SUBLN_EPS, [(k.cw[:, 4, :], k.xT)])
            moe_blocks(k, a, 1, o, slots_x, slots_y, [], final=True)


INPUTS = ["x_prompt", "x_sample", "state_hgrn", "cache_k", "cache_v", "page_table", "norm_mix_w", "norm_ffn_w", "a_w_in",
          "a_lb_logits", "a_gnorm_w", "a_w_o", "kv_norm_w", "w_kv", "b_w_q", "b_lambda_q1", "b_lambda_k1", "b_lambda_q2",
          "b_lambda_k2", "b_subln_w", "b_w_o", "moe_w_group", "moe_w_sub", "moe_w_gate", "moe_w_up", "moe_w_down",
          "final_norm_w"]
OUTPUTS = [("y_prompt", (1, SEQ, D)), ("y_sample", (DEC_B, DEC_T, D)), ("state_prompt", (1, 1, HEADS, P, P)),
           ("state_sample", (1, DEC_B, HEADS, P, P)), ("k_prompt", (1, SEQ, HEADS, P)), ("v_prompt", (1, SEQ, HEADS, P)),
           ("k_sample", (DEC_B, DEC_T, HEADS, P)), ("v_sample", (DEC_B, DEC_T, HEADS, P))]


def constants():
    import numpy as np

    f32 = np.float32
    q, key = np.arange(P)[:, None], np.arange(SEQ)[None, :]
    dist = (SEQ - P + q - key).astype(f32)
    dist[dist < 0] = MASKED
    row = np.arange(P)
    j, x = row // 32, row % 32
    used, head, half, t = x < 16, 2 * j + x // 8, x // 4 % 2, x % 4
    pos = np.arange(PAST + DEC_T)[None, :]
    slope = (2.0 ** -(head + 1.0))[:, None].astype(f32)
    alibi = -slope * (PAST + t[:, None] - pos).astype(f32)
    alibi[pos > PAST + t[:, None]] = -MASKED
    alibi[~used] = 0
    halves = np.stack([used & (half == 0), used & (half == 1)], 1)
    own_head = (x // DEC_T)[:, None] == np.arange(HEADS)[None, :]
    place = np.arange(SMP)[None, None, :] == np.arange(DEC_B)[None, :, None] * DEC_T + (x % DEC_T)[:, None, None]
    return {"const_dist": dist, "const_rows": np.concatenate([alibi, halves, own_head, place.reshape(P, -1)], 1).astype(f32)}


def kernel(**inputs):
    import numpy as np
    import concourse.bacc as bacc
    from concourse.bass_utils import run_bass_kernel_spmd

    nc = bacc.Bacc("TRN2", target_bir_lowering=False, num_devices=1)
    arrays, a = {}, {}
    given = {n: np.ascontiguousarray(inputs[n]) for n in INPUTS}
    for name, x in {**given, **constants()}.items():
        arrays[name] = x
        a[name] = nc.dram_tensor(name, x.shape, mybir.dt.from_np(x.dtype), kind="ExternalInput").ap()
    for name, shape in OUTPUTS:
        a[name] = nc.dram_tensor(name, shape, F32, kind="ExternalOutput").ap()
    trunk(nc, a)
    r = run_bass_kernel_spmd(nc, [arrays], core_ids=[0])
    return tuple(r.results[0][name] for name, _ in OUTPUTS)
```
